# Optimizing a Trainium2 kernel written in Bass

```python
import jax
import jax.numpy as jnp
from jax import lax
import numpy as np

D_MODEL = 1024
BATCH = 1
SEQ = 512
DEPTH = 1
DEC_BATCH = 8
DEC_SEQ = 4
PAST_LEN = 2048
PAGE_SIZE = 128

ATTN_HEADS = 8
HEAD_DIM = 64
ATTN_WIDTH = ATTN_HEADS * HEAD_DIM
CONV_CHANNELS = D_MODEL - ATTN_WIDTH
MIX_WIDTH = ATTN_WIDTH + CONV_CHANNELS
IN_WIDTH = 3 * ATTN_WIDTH + 2 * CONV_CHANNELS
CONV_K = 31
MOBA_BLOCK = 256
MOBA_TOPK = 3
Q_CHUNK = 16
PEER_HEADS = 8
N_KEYS = 128
N_EXPERTS = N_KEYS * N_KEYS
PEER_TOPK = 16
D_KEY = 256
HALF_KEY = D_KEY // 2
TOK_CHUNK = 256
EPS = 1e-6

kernel_name = 'hymba_conformer_moba_peer_step'

def rms_norm(x, g):
    xf = x.astype(jnp.float32)
    xf = xf * lax.rsqrt(jnp.mean(xf * xf, axis=-1, keepdims=True) + EPS)
    return xf.astype(x.dtype) * g

def attend(q, k_sel, v_sel, sel_ok, k_loc, v_loc, loc_ok):
    scale = HEAD_DIM ** -0.5
    s_loc = jnp.einsum('bthd,blhd->bthl', q, k_loc, preferred_element_type=jnp.float32) * scale
    s_loc = jnp.where(loc_ok[None, :, None, :], s_loc, -jnp.inf)
    if k_sel is None:
        p = jax.nn.softmax(s_loc, axis=-1).astype(v_loc.dtype)
        return jnp.einsum('bthl,blhd->bthd', p, v_loc)
    s_sel = jnp.einsum('bthd,bthnd->bthn', q, k_sel, preferred_element_type=jnp.float32) * scale
    if sel_ok is not None:
        s_sel = jnp.where(sel_ok[None, :, None, :], s_sel, -jnp.inf)
    n_s = s_sel.shape[-1]
    p = jax.nn.softmax(jnp.concatenate([s_sel, s_loc], axis=-1), axis=-1).astype(v_loc.dtype)
    return (jnp.einsum('bthn,bthnd->bthd', p[..., :n_s], v_sel)
            + jnp.einsum('bthl,blhd->bthd', p[..., n_s:], v_loc))

def moba_prompt(q, k, v):
    b, s, h, dh = q.shape
    nb_full = s // MOBA_BLOCK
    n_sel = min(MOBA_TOPK, (s - 1) // MOBA_BLOCK)
    s_pad = -(-s // MOBA_BLOCK) * MOBA_BLOCK
    pad = ((0, 0), (0, s_pad - s), (0, 0), (0, 0))
    k_pad = jnp.pad(k, pad)
    v_pad = jnp.pad(v, pad)
    q_blk = jnp.arange(s) // MOBA_BLOCK
    if n_sel > 0:
        k_blocks = k_pad[:, :nb_full * MOBA_BLOCK].reshape(b, nb_full, MOBA_BLOCK, h, dh)
        v_blocks = v_pad[:, :nb_full * MOBA_BLOCK].reshape(b, nb_full, MOBA_BLOCK, h, dh)
        k_mean = jnp.mean(k_blocks, axis=2, dtype=jnp.float32)
        gate = jnp.einsum('bshd,bnhd->bshn', q.astype(jnp.float32), k_mean)
        fully_past = jnp.arange(nb_full)[None, :] < q_blk[:, None]
        gate = jnp.where(fully_past[None, :, None, :], gate, -jnp.inf)
        _, sel = lax.top_k(gate, n_sel)
        sel_ok = jnp.arange(n_sel)[None, :] < q_blk[:, None]
        b_idx = jnp.arange(b)[:, None, None, None]
        h_idx = jnp.arange(h)[None, None, :, None]

    def one_chunk(c):
        t0 = c * Q_CHUNK
        blk0 = (t0 // MOBA_BLOCK) * MOBA_BLOCK
        q_c = lax.dynamic_slice_in_dim(q, t0, Q_CHUNK, axis=1)
        k_loc = lax.dynamic_slice_in_dim(k_pad, blk0, MOBA_BLOCK, axis=1)
        v_loc = lax.dynamic_slice_in_dim(v_pad, blk0, MOBA_BLOCK, axis=1)
        loc_ok = (blk0 + jnp.arange(MOBA_BLOCK))[None, :] <= (t0 + jnp.arange(Q_CHUNK))[:, None]
        if n_sel == 0:
            return attend(q_c, None, None, None, k_loc, v_loc, loc_ok)
        sel_c = lax.dynamic_slice_in_dim(sel, t0, Q_CHUNK, axis=1)
        k_sel = k_blocks[b_idx, sel_c, :, h_idx].reshape(b, Q_CHUNK, h, n_sel * MOBA_BLOCK, dh)
        v_sel = v_blocks[b_idx, sel_c, :, h_idx].reshape(b, Q_CHUNK, h, n_sel * MOBA_BLOCK, dh)
        ok_c = jnp.repeat(lax.dynamic_slice_in_dim(sel_ok, t0, Q_CHUNK, axis=0), MOBA_BLOCK, axis=1)
        return attend(q_c, k_sel, v_sel, ok_c, k_loc, v_loc, loc_ok)

    out = lax.map(one_chunk, jnp.arange(s // Q_CHUNK))
    return jnp.moveaxis(out, 0, 1).reshape(b, s, h, dh)

def moba_sample(q, k_new, v_new, k_pool, v_pool, page_table):
    db, t, h, dh = q.shape
    n_pages = page_table.shape[1]
    past = n_pages * PAGE_SIZE
    ppb = MOBA_BLOCK // PAGE_SIZE
    nb_past = past // MOBA_BLOCK
    n_sel = min(MOBA_TOPK, nb_past)
    own_page0 = nb_past * ppb
    r = past - nb_past * MOBA_BLOCK
    own_pages = page_table[:, own_page0:]
    k_loc = jnp.concatenate([k_pool[own_pages].reshape(db, r, h, dh), k_new], axis=1)
    v_loc = jnp.concatenate([v_pool[own_pages].reshape(db, r, h, dh), v_new], axis=1)
    loc_ok = jnp.concatenate([jnp.ones((t, r), dtype=bool), jnp.tril(jnp.ones((t, t), dtype=bool))], axis=1)
    if n_sel == 0:
        return attend(q, None, None, None, k_loc, v_loc, loc_ok)
    page_mean = jnp.mean(k_pool, axis=1, dtype=jnp.float32)
    pm_seq = page_mean[page_table[:, :own_page0]]
    k_mean = pm_seq.reshape(db, nb_past, ppb, h, dh).mean(axis=2)
    gate = jnp.einsum('bthd,bnhd->bthn', q.astype(jnp.float32), k_mean)
    _, sel = lax.top_k(gate, n_sel)
    logical = sel[..., None] * ppb + jnp.arange(ppb)
    phys = page_table[jnp.arange(db)[:, None, None, None, None], logical]
    h_idx = jnp.arange(h)[None, None, :, None, None]
    k_sel = k_pool[phys, :, h_idx].reshape(db, t, h, n_sel * MOBA_BLOCK, dh)
    v_sel = v_pool[phys, :, h_idx].reshape(db, t, h, n_sel * MOBA_BLOCK, dh)
    return attend(q, k_sel, v_sel, None, k_loc, v_loc, loc_ok)

def peer_ffn(x, w_query, keys1, keys2, expert_u, expert_v):
    lead = x.shape[:-1]
    xt = x.reshape(-1, D_MODEL)
    n = xt.shape[0]
    chunk = min(TOK_CHUNK, n)
    n_chunks = -(-n // chunk)
    xt = jnp.pad(xt, ((0, n_chunks * chunk - n), (0, 0)))

    def one(xc):
        qh = (xc @ w_query).astype(jnp.float32).reshape(chunk, PEER_HEADS, D_KEY)
        s1 = jnp.einsum('nhk,hmk->nhm', qh[..., :HALF_KEY], keys1.astype(jnp.float32))
        s2 = jnp.einsum('nhk,hmk->nhm', qh[..., HALF_KEY:], keys2.astype(jnp.float32))
        v1, i1 = lax.top_k(s1, PEER_TOPK)
        v2, i2 = lax.top_k(s2, PEER_TOPK)
        cand = (v1[..., :, None] + v2[..., None, :]).reshape(chunk, PEER_HEADS, PEER_TOPK * PEER_TOPK)
        cidx = (i1[..., :, None] * N_KEYS + i2[..., None, :]).reshape(chunk, PEER_HEADS, PEER_TOPK * PEER_TOPK)
        top, pos = lax.top_k(cand, PEER_TOPK)
        idx = jnp.take_along_axis(cidx, pos, axis=-1)
        g = jax.nn.softmax(top, axis=-1).astype(xc.dtype)
        act = jax.nn.gelu(jnp.einsum('nd,nhkd->nhk', xc, expert_u[idx]), approximate=False)
        return jnp.einsum('nhk,nhkd->nd', g * act, expert_v[idx])

    out = lax.map(one, xt.reshape(n_chunks, chunk, D_MODEL))
    return out.reshape(-1, D_MODEL)[:n].reshape(lead + (D_MODEL,))

def layer_front(x, norm1_g, w_in, q_norm_g, k_norm_g):
    xn = rms_norm(x, norm1_g)
    proj = xn @ w_in
    q, k, v, a, gt = jnp.split(proj, [ATTN_WIDTH, 2 * ATTN_WIDTH, 3 * ATTN_WIDTH, 3 * ATTN_WIDTH + CONV_CHANNELS], axis=-1)
    hs = x.shape[:-1] + (ATTN_HEADS, HEAD_DIM)
    q = rms_norm(q.reshape(hs), q_norm_g)
    k = rms_norm(k.reshape(hs), k_norm_g)
    v = v.reshape(hs)
    u = a * jax.nn.sigmoid(gt)
    return q, k, v, u

def conv_branch(u_ext, conv_w, conv_b, conv_norm_g):
    c = lax.conv_general_dilated(u_ext, conv_w[:, None, :], (1,), 'VALID',
                                 dimension_numbers=('NWC', 'WIO', 'NWC'),
                                 feature_group_count=CONV_CHANNELS) + conv_b
    return jax.nn.silu(rms_norm(c, conv_norm_g))

def layer_back(x, attn, conv, w_out, norm2_g, w_query, keys1, keys2, expert_u, expert_v):
    mix = jnp.concatenate([attn.reshape(x.shape[:-1] + (ATTN_WIDTH,)), conv], axis=-1)
    h = x + mix @ w_out
    return h + peer_ffn(rms_norm(h, norm2_g), w_query, keys1, keys2, expert_u, expert_v)

def setup_inputs(seed: int = 0) -> dict:
    key = jax.random.key(seed)
    ks = jax.random.split(key, 24)
    f32 = jnp.float32
    n_pages = PAST_LEN // PAGE_SIZE
    n_used = DEC_BATCH * n_pages
    n_phys = n_used + max(1, n_used // 4)
    page_table = jax.random.permutation(ks[0], n_phys)[:n_used].reshape(DEC_BATCH, n_pages).astype(jnp.int32)

    def nrm(k, shape, s):
        return jax.random.normal(k, shape, f32) * s

    return {
        'x_prompt': nrm(ks[1], (BATCH, SEQ, D_MODEL), 1.0),
        'x_sample': nrm(ks[2], (DEC_BATCH, DEC_SEQ, D_MODEL), 1.0),
        'cache_k': nrm(ks[3], (DEPTH, n_phys, PAGE_SIZE, ATTN_HEADS, HEAD_DIM), 1.0),
        'cache_v': nrm(ks[4], (DEPTH, n_phys, PAGE_SIZE, ATTN_HEADS, HEAD_DIM), 1.0),
        'state_conv': nrm(ks[5], (DEPTH, DEC_BATCH, CONV_K - 1, CONV_CHANNELS), 0.5),
        'page_table': page_table,
        'norm1_g': 1.0 + nrm(ks[6], (DEPTH, D_MODEL), 0.1),
        'w_in': nrm(ks[7], (DEPTH, D_MODEL, IN_WIDTH), D_MODEL ** -0.5),
        'q_norm_g': 1.0 + nrm(ks[8], (DEPTH, ATTN_HEADS, HEAD_DIM), 0.1),
        'k_norm_g': 1.0 + nrm(ks[9], (DEPTH, ATTN_HEADS, HEAD_DIM), 0.1),
        'conv_w': nrm(ks[10], (DEPTH, CONV_K, CONV_CHANNELS), CONV_K ** -0.5),
        'conv_b': nrm(ks[11], (DEPTH, CONV_CHANNELS), 0.02),
        'conv_norm_g': 1.0 + nrm(ks[12], (DEPTH, CONV_CHANNELS), 0.1),
        'w_out': nrm(ks[13], (DEPTH, MIX_WIDTH, D_MODEL), MIX_WIDTH ** -0.5),
        'norm2_g': 1.0 + nrm(ks[14], (DEPTH, D_MODEL), 0.1),
        'peer_w_query': nrm(ks[15], (DEPTH, D_MODEL, PEER_HEADS * D_KEY), D_MODEL ** -0.5),
        'peer_keys1': nrm(ks[16], (DEPTH, PEER_HEADS, N_KEYS, HALF_KEY), HALF_KEY ** -0.5),
        'peer_keys2': nrm(ks[17], (DEPTH, PEER_HEADS, N_KEYS, HALF_KEY), HALF_KEY ** -0.5),
        'peer_u': nrm(ks[18], (DEPTH, N_EXPERTS, D_MODEL), D_MODEL ** -0.5),
        'peer_v': nrm(ks[19], (DEPTH, N_EXPERTS, D_MODEL), PEER_HEADS ** -0.5),
    }

def reference(x_prompt, x_sample, cache_k, cache_v, state_conv, page_table,
              norm1_g, w_in, q_norm_g, k_norm_g, conv_w, conv_b, conv_norm_g,
              w_out, norm2_g, peer_w_query, peer_keys1, peer_keys2, peer_u, peer_v):
    xp = x_prompt
    xs = x_sample
    kp_rows, vp_rows, cp_rows, ks_rows, vs_rows, cs_rows = [], [], [], [], [], []
    for l in range(DEPTH):
        peer_args = (peer_w_query[l], peer_keys1[l], peer_keys2[l], peer_u[l], peer_v[l])
        q, k, v, u = layer_front(xp, norm1_g[l], w_in[l], q_norm_g[l], k_norm_g[l])
        attn = moba_prompt(q, k, v)
        conv = conv_branch(jnp.pad(u, ((0, 0), (CONV_K - 1, 0), (0, 0))), conv_w[l], conv_b[l], conv_norm_g[l])
        xp = layer_back(xp, attn, conv, w_out[l], norm2_g[l], *peer_args)
        kp_rows.append(k)
        vp_rows.append(v)
        cp_rows.append(u[:, -(CONV_K - 1):])
        q, k, v, u = layer_front(xs, norm1_g[l], w_in[l], q_norm_g[l], k_norm_g[l])
        attn = moba_sample(q, k, v, cache_k[l], cache_v[l], page_table)
        u_ext = jnp.concatenate([state_conv[l], u], axis=1)
        conv = conv_branch(u_ext, conv_w[l], conv_b[l], conv_norm_g[l])
        xs = layer_back(xs, attn, conv, w_out[l], norm2_g[l], *peer_args)
        ks_rows.append(k)
        vs_rows.append(v)
        cs_rows.append(u_ext[:, -(CONV_K - 1):])
    return (xp, xs, jnp.stack(kp_rows), jnp.stack(vp_rows), jnp.stack(cp_rows),
            jnp.stack(ks_rows), jnp.stack(vs_rows), jnp.stack(cs_rows))


_drawn_inputs = setup_inputs


def setup_inputs(seed=0):
    import zlib

    import numpy as np

    out = dict(_drawn_inputs(seed))
    spreads = {}
    factors = {'q_norm_g': 3.136}
    for name, (base, spread) in spreads.items():
        noise = np.random.default_rng([zlib.crc32(name.encode()), seed]).standard_normal(out[name].shape)
        drawn = base * np.exp(spread * noise) if base else spread * noise
        out[name] = jnp.asarray(drawn.astype(out[name].dtype))
    for name, factor in factors.items():
        out[name] = (out[name] * factor).astype(out[name].dtype)
    return out
```

```python
import concourse.bass as bass
from concourse import mybir

F32 = mybir.dt.float32
F32R = mybir.dt.float32r
I32 = mybir.dt.int32
U32 = mybir.dt.uint32
ALU = mybir.AluOpType
ACT = mybir.ActivationFunctionType
AX = mybir.AxisListType

P = 128
D = 1024
KD = D // P
SEQ = 512
DEC_B, DEC_T = 8, 4
NDEC = DEC_B * DEC_T
N = SEQ + NDEC
HALF = N // 2
NT = (N + P - 1) // P
ROWS = [min(P, N - P * t) for t in range(NT)]
HEADS, HD = 8, 64
PAIRS = HEADS // 2
CH = 512
CC = CH // P
TAPS = 31
PAD = TAPS - 1
PAGES, PAGE = 16, 128
POOL_PAGES = 160
BLOCK, TOPB = 256, 3
PAST = PAGES * PAGE
NBLK = PAST // BLOCK
KEYS_ALL = PAST + NDEC
PH = 8
TOPK = 16
SLOTS = PH * TOPK
EPS = 1e-6
NEG = -1.0e30
FLOOR = -3.0e38

WC = 2048
WCOL = WC // KD
N_IN, N_OUT, N_WQ = 10, 4, 8
W_CHUNKS = N_IN + N_OUT + N_WQ
STEPS = 64
GCHUNK = 32
NG = N // GCHUNK
TOK = 4
GROUPS = GCHUNK // TOK


def halves(ap):
    return ap[:, :, 0:HALF]


def two(ap):
    return ap.rearrange("p (b n) -> p b n", b=2)


def wait(engine, semaphore, value):
    if not isinstance(value, int) or value > 0:
        engine.wait_ge(semaphore, value)


def alone(engine, ready):
    engine.sem_inc(ready, 1)


def after_projection(chunk):
    return sum(5 if c < 6 else 2 for c in range(chunk + 1))


def build_layer(nc, io):
    base = nc.sbuf_base + 31 & ~31
    top = nc.sbuf_usable_end
    place = {"at": base}

    def sb(name, shape, dtype=F32, at=None):
        size = 4
        for s in shape[1:]:
            size *= s
        if at is None:
            at = place["at"]
        place["at"] = at + size + 31 & ~31
        assert place["at"] <= top, (name, place["at"], top)
        return nc.alloc_sbuf_tensor_at(name, shape, dtype, offset=at)

    resid = sb("resid", [P, KD, N])
    x_hi = sb("x_hi", [P, KD, N], F32R)
    x_lo = sb("x_lo", [P, KD, N], F32R)
    w_raw = sb("w_raw", [P, 2, WC])
    w_hi = sb("w_hi", [P, 2, WC], F32R)
    w_lo = sb("w_lo", [P, 2, WC], F32R)
    ident = sb("ident", [P, P])
    ones = sb("ones", [P, P])
    iota = sb("iota", [P, P])
    rstd = sb("rstd", [P, N])
    g1 = sb("g1", [P, KD])
    g2 = sb("g2", [P, KD])
    eps = sb("eps", [P, 1])
    stats = sb("stats", [P, 64])
    overlay = place["at"]

    v_nat = sb("v_nat", [P, NT, CH])
    q_t = sb("q_t", [P, PAIRS, N])
    k_t = sb("k_t", [P, PAIRS, N])
    u_p = sb("u_p", [P, CC, PAD + SEQ])
    u_s = sb("u_s", [P, CC, DEC_B, PAD + DEC_T])
    conv = sb("conv", [P, CC, N])
    q_blk = sb("q_blk", [P, DEC_B, PAIRS, HEADS * DEC_T])
    gq = sb("gq", [P, CH])
    gk = sb("gk", [P, CH])
    taps = sb("taps", [P, CC, TAPS])
    conv_b = sb("conv_b", [P, CC])
    conv_g = sb("conv_g", [P, CC])
    causal = sb("causal", [P, P])
    own = sb("own", [P, 2, NDEC])
    page_row = sb("page_row", [1, DEC_B * PAGES], I32)
    page_ring = sb("page_ring", [P, 2, 4, CH])
    sq = sb("sq", [P, 2, N])
    at_keys = place["at"]
    page_kt = sb("page_kt", [P, 2, PAIRS, 4 * PAGE])
    end_keys = place["at"]
    qk_nat = sb("qk_nat", [P, 2, NT, WCOL], at=at_keys)
    s_nat = sb("s_nat", [P, KEYS_ALL], at=end_keys)
    o_nat = sb("o_nat", [P, CH])
    p_nat = sb("p_nat", [P, 2, SEQ], at=end_keys)
    p_tr = sb("p_tr", [P, 2, SEQ])
    at_q = overlay + 4 * NT * CH
    pages_pt = sb("pages_pt", [P, PAGES, P], at=at_q)
    own_pt = sb("own_pt", [NDEC, P])
    sqc = sb("sqc", [P, 2, N], at=at_q + 4 * PAIRS * N)
    sig_c = sb("sig_c", [P, CC, N], at=at_q + 8 * PAIRS * N)

    keys = sb("keys", [P, 2 * PH, P], at=overlay)
    qh_t = sb("qh_t", [P, 2, 2, N])
    best = sb("best", [P, NT, PH, 2, TOPK])
    best_i = sb("best_i", [P, NT, PH, 2, TOPK])
    m16 = sb("m16", [P, NT, 2, TOPK])
    i16 = sb("i16", [P, NT, 2, TOPK], U32)
    rest = sb("rest", [P, 2, P])
    slots = sb("slots", [P, 3, N])
    at_cand = place["at"]
    cand = sb("cand", [P, PH, TOPK, TOPK])
    crest = sb("crest", [P, 2, TOPK * TOPK])
    hot = sb("hot", [P, SLOTS, TOPK])
    top16 = sb("top16", [P, PH, TOPK])
    pos16 = sb("pos16", [P, PH, TOPK], U32)
    digit = sb("digit", [P, 2, SLOTS], U32)
    digit_f = sb("digit_f", [P, 2, SLOTS])
    found = sb("found", [P, 3, SLOTS])
    den = sb("den", [P, PH])
    current = sb("current", [P, 2, 3, GCHUNK], at=at_cand)
    hot1 = sb("hot1", [P, 2, TOK, P])
    hot2 = sb("hot2", [P, 2, TOK, P])
    g_out = sb("g_out", [P, 2, P, GCHUNK])

    v_raw = sb("v_raw", [P, 2, WC], at=overlay)
    v_hi = sb("v_hi", [P, 2, WC], F32R)
    v_lo = sb("v_lo", [P, 2, WC], F32R)
    g_in = sb("g_in", [P, 2, NG, 4 * GCHUNK])
    act = sb("act", [P, 2, N])
    prod = sb("prod", [P, 2, N])
    a_hi = sb("a_hi", [P, 2, 2, N], F32R)
    a_lo = sb("a_lo", [P, 2, 2, N], F32R)

    pair = [nc.alloc_psum_tensor(f"pair{i}", [P, 2, 512], F32) for i in range(4)]

    gates = nc.dram_tensor("gates", [NG, P, P, GCHUNK], F32).ap()

    names = {}

    def sem(name):
        if name not in names:
            names[name] = nc.alloc_semaphore(name)
        return names[name]

    state_loaded = sem("state_loaded")
    v_waited, pool_waited = sem("v_waited"), sem("pool_waited")
    x_loaded, small_loaded, pages_known = sem("x_loaded"), sem("small_loaded"), sem("pages_known")
    w_loaded = [sem("w_loaded0"), sem("w_loaded1")]
    w_split, projected = sem("w_split"), sem("projected")
    const_ready = sem("const_ready")
    sq1_done, sum1_done, root1_done, x_ready = sem("sq1_done"), sem("sum1_done"), sem("root1_done"), sem("x_ready")
    qk_sq, qk_sum, qk_root, qk_scaled, qk_ready = sem("qk_sq"), sem("qk_sum"), sem("qk_root"), sem("qk_scaled"), sem("qk_ready")
    qk_turned, qk_kept, v_kept = sem("qk_turned"), sem("qk_kept"), sem("v_kept")
    gate_sig, u_done = sem("gate_sig"), sem("u_done")
    stored = sem("stored")
    ps_done, pm_done, pe_done, pn_done = sem("ps_done"), sem("pm_done"), sem("pe_done"), sem("pn_done")
    pt_done, ptc_done, pv_done, po_done = sem("pt_done"), sem("ptc_done"), sem("pv_done"), sem("po_done")
    q_blk_ready = sem("q_blk_ready")
    page_loaded = [sem("page_loaded0"), sem("page_loaded1")]
    page_turned, page_kept, page_scored, own_scored = sem("page_turned"), sem("page_kept"), sem("page_scored"), sem("own_scored")
    s_kept, s_max, s_exp, s_normed = sem("s_kept"), sem("s_max"), sem("s_exp"), sem("s_normed")
    s_turned, s_turned_kept, pages_used, o_done = sem("s_turned"), sem("s_turned_kept"), sem("pages_used"), sem("o_done")
    o_kept, o_turned, o_mixed = sem("o_kept"), sem("o_turned"), sem("o_mixed")
    conv_done, sqc_done, sumc_done, rootc_done, z_done, sigc_done = (
        sem("conv_done"), sem("sqc_done"), sem("sumc_done"), sem("rootc_done"), sem("z_done"), sem("sigc_done"))
    mix_ready, h_done = sem("mix_ready"), sem("h_done")
    sq2_done, sum2_done, root2_done, x2_ready = sem("sq2_done"), sem("sum2_done"), sem("root2_done"), sem("x2_ready")
    keys_loaded, qh_kept, scored, ranked = sem("keys_loaded"), sem("qh_kept"), sem("scored"), sem("ranked")
    rt_top, rt_exp, rt_found, rt_turned, rt_kept = sem("rt_top"), sem("rt_exp"), sem("rt_found"), sem("rt_turned"), sem("rt_kept")
    current_ready, hot1_ready, hot2_ready = sem("current_ready"), sem("hot1_ready"), sem("hot2_ready")
    g_made, g_kept = sem("g_made"), sem("g_kept")
    g_stored = [sem("g_stored0"), sem("g_stored1")]
    u_loaded = [sem("u_loaded0"), sem("u_loaded1")]
    v_loaded = [sem("v_loaded0"), sem("v_loaded1")]
    g_loaded = [sem("g_loaded0"), sem("g_loaded1")]
    u_hi_done, u_lo_done, v_hi_done, v_lo_done = sem("u_hi_done"), sem("u_lo_done"), sem("v_hi_done"), sem("v_lo_done")
    up_done, gelu_done, a_done, down_done, added = sem("up_done"), sem("gelu_done"), sem("a_done"), sem("down_done"), sem("added")

    SMALL_LOADS = 7
    STORES = 4 + 2 + 1 + CC
    BATCH = 4
    CHUNKS = DEC_B * PAGES // 4
    UNITS = HEADS * (SEQ // P)

    def unit(u):
        return u // HEADS, u // 2 % PAIRS, u % 2

    ORDER = [0, 1, 2, 3, 4, 5, 8, 6, 9, 7]

    with nc.Block() as block:

        @block.sync
        def _(sp):
            def load_pages(cache, offset):
                def two_chunks(i):
                    for half in range(2):
                        if offset == 0:
                            wait(sp, page_turned, 8 * i + 4 * half - 4)
                        else:
                            wait(sp, pages_used, 2 * i + half - 1)
                        for p in range(4):
                            page = sp.value_load(page_row[0:1, bass.ds(8 * i + 4 * half + p, 1)],
                                                 min_val=0, max_val=POOL_PAGES - 1)
                            sp.dma_start(page_ring[:, half, p, :], cache[page, :, :])\
                                .then_inc(page_loaded[half], 16)

                two_chunks(0)
                with sp.Fori(1, CHUNKS // 2) as i:
                    two_chunks(i)

            def load_weights(chunk):
                wait(sp, w_split, chunk - 1)
                if chunk < N_IN:
                    src = io["w_in"][ORDER[chunk]]
                elif chunk < N_IN + N_OUT:
                    src = io["w_out"][chunk - N_IN]
                else:
                    src = io["w_query"][chunk - N_IN - N_OUT]
                sp.dma_start(w_raw[:, chunk % 2, :], src).then_inc(w_loaded[chunk % 2], 16)

            sp.dma_start(resid[:, :, :], io["x_t"]).then_inc(x_loaded, 16)
            for chunk in range(N_IN + 2):
                load_weights(chunk)
            sp.wait_ge(pages_known, 16)
            load_pages(io["cache_k"], 0)
            sp.wait_ge(page_turned, 4 * CHUNKS)
            load_pages(io["cache_v"], 1)
            for chunk in range(N_IN + 2, N_IN + N_OUT):
                load_weights(chunk)
            sp.wait_ge(mix_ready, 1)
            sp.wait_ge(stored, 16 * STORES)
            sp.dma_start(keys[:, :, :], io["keys_t"]).then_inc(keys_loaded, 16)
            for chunk in range(N_IN + N_OUT, W_CHUNKS):
                load_weights(chunk)

            def store_gates(c, parity):
                sp.wait_ge(g_kept, GROUPS * (c + 1))
                sp.dma_start(gates[c], g_out[:, parity, :, :]).then_inc(g_stored[parity], 16)

            def load_u(s, slot):
                sp.dma_start(w_raw[:, slot, :], io["u_t"][s]).then_inc(u_loaded[slot], 16)

            def load_v(s, slot):
                sp.dma_start(v_raw[:, slot, :], io["v_t"][s]).then_inc(v_loaded[slot], 16)

            for slot in range(2):
                sp.wait_ge(w_split, W_CHUNKS - 1 + slot)
                load_u(slot, slot)
            store_gates(0, 0)
            with sp.Fori(0, NG // 2) as i:
                store_gates(2 * i + 1, 1)
                store_gates(2 * i + 2, 0)
            sp.wait_ge(g_stored[0], 16 * (NG // 2 + 1))
            sp.wait_ge(g_stored[1], 16 * (NG // 2))
            sp.wait_ge(g_made, NG * GROUPS)

            by_tiles = gates.rearrange("c p (g i) t -> g p c (i t)", i=4)

            def load_step(it, k):
                s = 4 * it + k
                slot = k % 2
                if not (isinstance(it, int) and it == 0 and k < 2):
                    wait(sp, u_lo_done, s - 1)
                    load_u(s, slot)
                wait(sp, v_lo_done, s - 1)
                load_v(s, slot)
                if k % 2 == 0:
                    wait(sp, a_done, 2 * s - 4)
                    sp.dma_start(g_in[:, k // 2, :, :], by_tiles[2 * it + k // 2])\
                        .then_inc(g_loaded[k // 2], 16)

            for k in range(4):
                load_step(0, k)
            with sp.Fori(1, STEPS // 4) as it:
                for k in range(4):
                    load_step(it, k)
            sp.wait_ge(added, KD * STEPS)
            sp.dma_start(io["y_t"], resid[:, :, :]).then_inc(stored, 16)
            sp.wait_ge(stored, 16 * (STORES + 1))

        @block.gpsimd
        def _(pool):
            pool.memset(ones[:, :], 1.0)
            pool.memset(ident[:, :], 0.0)
            pool.memset(causal[:, :], 0.0)
            pool.memset(own[:, :, :], 0.0)
            pool.memset(eps[:, :], EPS)
            pool.memset(u_p[:, :, 0:PAD], 0.0)
            pool.memset(q_blk[:, :, :, :], 0.0)
            pool.iota(iota[:, :], [[1, P]], base=0, channel_multiplier=0, allow_small_or_imprecise_dtypes=True)
            pool.iota(stats[:, 32:33].bitcast(I32), [[0, 1]], base=0, channel_multiplier=1)
            pool.iota(s_nat[:, 0:NDEC], [[0, DEC_B], [1, DEC_T]], base=0, channel_multiplier=0,
                      allow_small_or_imprecise_dtypes=True)
            pool.drain()
            pool.affine_select(out=ident[:, :], in_=ident[:, :], compare_op=ALU.not_equal, fill=1.0,
                               base=0, pattern=[[-1, P]], channel_multiplier=1)
            pool.affine_select(out=causal[:, :], in_=causal[:, :], compare_op=ALU.is_ge, fill=NEG,
                               base=0, pattern=[[-1, P]], channel_multiplier=1)
            for b in range(2):
                for sign in (1, -1):
                    pool.affine_select(out=own[:, b, :], in_=own[:, b, :], compare_op=ALU.is_ge, fill=NEG,
                                       base=sign * P * b + (0 if sign == 1 else 31),
                                       pattern=[[-32 * sign, DEC_B], [0, DEC_T]], channel_multiplier=sign)
                    pool.drain()
            pool.memset(stats[:, 48:49], 0.0).then_inc(const_ready, 1)

            for chunk in range(W_CHUNKS):
                pool.wait_ge(w_loaded[chunk % 2], 16 * (chunk // 2 + 1))
                if chunk >= 2:
                    pool.wait_ge(projected, after_projection(chunk - 2))
                pool.tensor_copy(w_hi[:, chunk % 2, :], w_raw[:, chunk % 2, :])
                pool.drain()
                pool.tensor_tensor(w_lo[:, chunk % 2, :], w_raw[:, chunk % 2, :],
                                   w_hi[:, chunk % 2, :].bitcast(F32), ALU.subtract).then_inc(w_split, 1)

            def hot_rows(c, parity):
                pool.wait_ge(current_ready, c + 1)
                for q in range(GROUPS):
                    g = GROUPS * c + q
                    wait(pool, g_made, g - 1)
                    alone(pool, pool_waited)
                    for t in range(TOK):
                        column = current[:, parity, 0, TOK * q + t:TOK * q + t + 1]
                        last = pool.tensor_scalar(hot1[:, q % 2, t, :], iota[:, :], column, None, ALU.is_equal)
                    last.then_inc(hot1_ready, 1)

            hot_rows(0, 0)
            with pool.Fori(0, NG // 2) as i:
                hot_rows(2 * i + 1, 1)
                hot_rows(2 * i + 2, 0)

            def split_u(it, k):
                pool.wait_ge(u_hi_done, 4 * it + k + 1)
                pool.tensor_tensor(w_lo[:, k % 2, :], w_raw[:, k % 2, :], w_hi[:, k % 2, :].bitcast(F32),
                                   ALU.subtract).then_inc(u_lo_done, 1)

            for k in range(4):
                split_u(0, k)
            with pool.Fori(1, STEPS // 4) as it:
                for k in range(4):
                    split_u(it, k)

        @block.scalar
        def _(sc):
            sc.dma_start(g1[:, :], io["norm1_g"]).then_inc(small_loaded, 16)
            sc.dma_start(g2[:, :], io["norm2_g"]).then_inc(small_loaded, 16)
            sc.dma_start(gq[:, :], io["q_norm_g"].partition_broadcast(P)).then_inc(small_loaded, 16)
            sc.dma_start(gk[:, :], io["k_norm_g"].partition_broadcast(P)).then_inc(small_loaded, 16)
            sc.dma_start(taps[:, :, :], io["conv_w"]).then_inc(small_loaded, 16)
            sc.dma_start(conv_b[:, :], io["conv_b"]).then_inc(small_loaded, 16)
            sc.dma_start(conv_g[:, :], io["conv_norm_g"]).then_inc(small_loaded, 16)
            for cc in range(CC):
                sc.dma_start(u_s[:, cc, :, 0:PAD], io["state_t"][:, cc]).then_inc(state_loaded, 16)
            sc.dma_start(page_row[:, :], io["page_table"]).then_inc(pages_known, 16)

            def squares(dst, src, block_count, loaded, summed, done):
                for kd in range(block_count):
                    loaded(kd)
                    wait(sc, summed, kd - 1)
                    sc.activation(dst[:, kd % 2, :], src[:, kd, :], ACT.Square).then_inc(done, 1)

            def root(banks, width, summed, count, done):
                sc.wait_ge(summed, count)
                sc.activation(two(rstd[:, :]), halves(banks), ACT.Sqrt, bias=eps[:, 0:1], scale=1.0 / width)\
                    .then_inc(done, 1)

            sc.wait_ge(x_loaded, 16)
            sc.wait_ge(const_ready, 1)
            squares(sq, resid, KD, lambda kd: None, sum1_done, sq1_done)
            root(pair[0], D, sum1_done, KD, root1_done)

            def keep_turned(chunk):
                dst = q_t if chunk < 2 else k_t
                for nt in range(NT):
                    m = NT * chunk + nt
                    sc.wait_ge(qk_turned, m + 1)
                    first = 2 * (chunk % 2)
                    sc.activation(dst[:, first:first + 2, P * nt:P * nt + ROWS[nt]],
                                  pair[2][:, m % 2, 0:2 * P].rearrange("p (b n) -> p b n", b=2)[:, :, 0:ROWS[nt]],
                                  ACT.Copy, scale=HD ** -0.5 if chunk < 2 else 1.0).then_inc(qk_kept, 1)

            for chunk in range(6):
                for nt in range(NT):
                    m = NT * chunk + nt
                    r = ROWS[nt]
                    src = pair[m % 4 // 2][0:r, m % 2, 0:WCOL]
                    sc.wait_ge(projected, m + 1)
                    if chunk < 4:
                        sc.activation(sq[0:r, m % 2, 0:WCOL], src, ACT.Square).then_inc(qk_sq, 1)
                        sc.wait_ge(qk_sum, m + 1)
                        sc.activation(stats[0:r, 4 * (m % 4):4 * (m % 4) + 4], stats[0:r, 4 * (m % 4):4 * (m % 4) + 4],
                                      ACT.Sqrt, bias=eps[0:r, 0:1], scale=1.0 / HD).then_inc(qk_root, 1)
                    else:
                        sc.activation(v_nat[0:r, nt, WCOL * (chunk - 4):WCOL * (chunk - 3)], src, ACT.Copy)\
                            .then_inc(v_kept, 1)
                if 1 <= chunk <= 4:
                    keep_turned(chunk - 1)
            sc.wait_ge(qk_ready, 4 * NT)
            sc.wait_ge(v_kept, 2 * NT)
            for dst, src in ((io["k_out"], None), (io["v_out"], v_nat)):
                whole = dst[0:SEQ, :].rearrange("(t p) f -> p t f", p=P)
                for c in range(2):
                    cols = slice(WCOL * c, WCOL * c + WCOL)
                    if src is None:
                        sc.dma_start(whole[:, :, cols], qk_nat[:, c, 0:NT - 1, :]).then_inc(stored, 16)
                        sc.dma_start(dst[SEQ:N, cols], qk_nat[0:NDEC, c, NT - 1, :]).then_inc(stored, 16)
                if src is not None:
                    sc.dma_start(whole, v_nat[:, 0:NT - 1, :]).then_inc(stored, 16)
                    sc.dma_start(dst[SEQ:N, :], v_nat[0:NDEC, NT - 1, :]).then_inc(stored, 16)
            for n, chunk in enumerate((6, 8)):
                for cb in range(2):
                    sc.wait_ge(projected, after_projection(chunk - 1) + cb + 1)
                    if n:
                        sc.wait_ge(u_done, cb + 1)
                    sc.activation(two(sq[:, cb, :]), halves(pair[cb]), ACT.Sigmoid).then_inc(gate_sig, 1)
            sc.wait_ge(u_done, 4)
            sc.wait_ge(state_loaded, 16 * CC)
            sc.wait_ge(small_loaded, 16 * SMALL_LOADS)
            sc.dma_start(io["conv_p_out"], u_p[:, :, SEQ:SEQ + PAD]).then_inc(stored, 16)
            for cc in range(CC):
                sc.dma_start(io["conv_s_out"][:, cc], u_s[:, cc, :, DEC_T:DEC_T + PAD])\
                    .then_inc(stored, 16)

            def prompt_exp(u):
                i = unit(u)[0]
                sc.wait_ge(pm_done, u + 1)
                wait(sc, pt_done, u - 1)
                sc.activation(p_nat[:, u % 2, 0:P * (i + 1)], pair[0][:, u % 2, 0:P * (i + 1)], ACT.Exp,
                              bias=stats[:, 16 + u % 2:17 + u % 2],
                              accum_out=stats[:, 20 + u % 2:21 + u % 2]).then_inc(pe_done, 1)

            def prompt_keep(u):
                i = unit(u)[0]
                sc.wait_ge(pt_done, u + 1)
                wait(sc, pv_done, u - 1)
                sc.activation(p_tr[:, u % 2, 0:P * (i + 1)], pair[1][:, u % 2, 0:P * (i + 1)], ACT.Copy)\
                    .then_inc(ptc_done, 1)

            prompt_exp(0)
            for u in range(UNITS):
                if u + 1 < UNITS:
                    prompt_exp(u + 1)
                prompt_keep(u)

            sc.wait_ge(stored, 16 * STORES)

            def keep_pages(b, i):
                for half in range(2):
                    chunk = 16 * b + 2 * i + half
                    wait(sc, page_scored, chunk - 1)
                    for p in range(4):
                        sc.wait_ge(page_turned, 4 * chunk + p + 1)
                        sc.activation(page_kt[:, half, :, PAGE * p:PAGE * (p + 1)],
                                      pair[2][:, p % 2, :].rearrange("p (a k) -> p a k", a=PAIRS), ACT.Copy)\
                            .then_inc(page_kept, 1)

            def exp_rows(b):
                sc.wait_ge(s_max, b + 1)
                sc.activation(s_nat[:, :], s_nat[:, :], ACT.Exp, bias=stats[:, 24:25], accum_out=stats[:, 25:26])\
                    .then_inc(s_exp, 1)

            def keep_probabilities(b):
                for g in range(5):
                    sc.wait_ge(s_turned, 5 * b + g + 1)
                    if g < 4:
                        sc.activation(pages_pt[:, 4 * g:4 * g + 4, :],
                                      pair[2][:, g % 2, :].rearrange("p (a k) -> p a k", a=4), ACT.Copy)\
                            .then_inc(s_turned_kept, 1)
                    else:
                        sc.activation(own_pt[:, :], pair[2][0:NDEC, 0, 0:P], ACT.Copy).then_inc(s_turned_kept, 1)

            def keep_output(b):
                sc.wait_ge(o_done, b + 1)
                wait(sc, o_turned, b)
                sc.activation(o_nat[:, :], pair[3][:, 1, :], ACT.Copy).then_inc(o_kept, 1)

            keep_pages(0, 0)
            with sc.Fori(1, 8) as i:
                keep_pages(0, i)
            exp_rows(0)
            with sc.Fori(0, 8) as i:
                keep_pages(1, i)
            keep_probabilities(0)
            exp_rows(1)
            squares(sqc, conv, CC, lambda kd: sc.wait_ge(conv_done, 1) if kd == 0 else None, sumc_done, sqc_done)
            keep_output(0)
            root(pair[0], CH, sumc_done, CC, rootc_done)
            keep_probabilities(1)
            sc.wait_ge(z_done, 1)
            for cc in range(CC):
                sc.activation(sig_c[:, cc, :], conv[:, cc, :], ACT.Sigmoid).then_inc(sigc_done, 1)
            keep_output(1)

            squares(sq, resid, KD, lambda kd: sc.wait_ge(h_done, kd + 1), sum2_done, sq2_done)
            root(pair[2], D, sum2_done, KD, root2_done)

            def keep_queries(h):
                for half in range(2):
                    sc.wait_ge(projected, 2 * h + half + 1 + after_projection(N_IN + N_OUT - 1))
                    if half == 0:
                        wait(sc, scored, 3 * h)
                    sc.activation(two(qh_t[:, 0, half, :]), halves(pair[half]), ACT.Copy).then_inc(qh_kept, 1)

            keep_queries(0)
            with sc.Fori(1, PH) as h:
                keep_queries(h)

            for nt in range(NT):
                r = ROWS[nt]
                sc.wait_ge(rt_top, nt + 1)
                sc.activation(top16[0:r, :, :], top16[0:r, :, :], ACT.Exp).then_inc(rt_exp, 1)
                sc.wait_ge(rt_turned, nt + 1)
                sc.activation(slots[:, :, P * nt:P * nt + r],
                              pair[3][:, 1, 0:3 * P].rearrange("p (a n) -> p a n", a=3)[:, :, 0:r], ACT.Copy)\
                    .then_inc(rt_kept, 1)

            def keep_gates(c, parity, stores):
                wait(sc, g_stored[parity], stores)
                for q in range(GROUPS):
                    sc.wait_ge(g_made, GROUPS * c + q + 1)
                    sc.activation(g_out[:, parity, :, TOK * q:TOK * q + TOK].rearrange("p i t -> p t i"),
                                  pair[0][:, q % 2, :].rearrange("p (t i) -> p t i", t=TOK), ACT.Copy)\
                        .then_inc(g_kept, 1)

            keep_gates(0, 0, 0)
            keep_gates(1, 1, 0)
            keep_gates(2, 0, 16)
            with sc.Fori(1, NG // 2) as i:
                keep_gates(2 * i + 1, 1, 16 * i)
                keep_gates(2 * i + 2, 0, 16 * i + 16)

            def high_u(s, loads, slot):
                wait(sc, u_loaded[slot], loads)
                wait(sc, up_done, 2 * s - 2)
                sc.activation(w_hi[:, slot, :], w_raw[:, slot, :], ACT.Copy).then_inc(u_hi_done, 1)

            def mixer(it, k, last=False):
                s = 4 * it + k
                slot = k % 2
                if not (last and k == 3):
                    high_u(s + 1, 16 * (2 * it + (k + 1) // 2 + 1), (k + 1) % 2)
                sc.wait_ge(v_loaded[slot], 16 * (2 * it + k // 2 + 1))
                wait(sc, down_done, KD * s - KD)
                sc.activation(v_hi[:, slot, :], v_raw[:, slot, :], ACT.Copy).then_inc(v_hi_done, 1)
                for j in range(2):
                    sc.wait_ge(up_done, 2 * s + j + 1)
                    wait(sc, a_done, 2 * s + j - 1)
                    sc.activation(two(act[:, j, :]), halves(pair[j]), ACT.Gelu).then_inc(gelu_done, 1)

            sc.wait_ge(projected, after_projection(W_CHUNKS - 1))
            high_u(0, 16, 0)
            for k in range(4):
                mixer(0, k)
            with sc.Fori(1, STEPS // 4 - 1) as it:
                for k in range(4):
                    mixer(it, k)
            for k in range(4):
                mixer(STEPS // 4 - 1, k, last=True)

        @block.vector
        def _(v):
            def reciprocal_rms(rooted):
                v.wait_ge(rooted, 1)
                v.reciprocal(rstd[:, :], rstd[:, :])
                v.drain()

            def parts(kd, src):
                v.tensor_copy(x_hi[:, kd, :], src)
                v.drain()
                return v.tensor_tensor(x_lo[:, kd, :], src, x_hi[:, kd, :].bitcast(F32), ALU.subtract)

            def normed(gain, rooted, ready):
                reciprocal_rms(rooted)
                for kd in range(KD):
                    v.scalar_tensor_tensor(sq[:, kd % 2, :], resid[:, kd, :], gain[:, kd:kd + 1], rstd[:, :],
                                           ALU.mult, ALU.mult)
                    v.drain()
                    last = parts(kd, sq[:, kd % 2, :])
                last.then_inc(ready, 1)

            v.wait_ge(const_ready, 1)
            v.tensor_scalar(stats[:, 33:34].bitcast(I32), stats[:, 32:33].bitcast(I32), DEC_T - 1, None, ALU.bitwise_and)
            v.drain()
            v.tensor_copy(stats[:, 34:35], stats[:, 33:34].bitcast(I32))
            v.drain()
            v.tensor_scalar(s_nat[:, 0:NDEC], s_nat[:, 0:NDEC], stats[:, 34:35], NEG, ALU.is_gt, ALU.mult)
            v.drain()
            for b in range(2):
                v.tensor_tensor(own[:, b, :], own[:, b, :], s_nat[:, 0:NDEC], ALU.add)
            v.wait_ge(small_loaded, 16 * SMALL_LOADS)
            v.wait_ge(state_loaded, 16 * CC)

            normed(g1, root1_done, x_ready)

            for chunk in range(4):
                for nt in range(NT):
                    m = NT * chunk + nt
                    r = ROWS[nt]
                    ss = stats[0:r, 4 * (m % 4):4 * (m % 4) + 4]
                    v.wait_ge(qk_sq, m + 1)
                    v.tensor_reduce(ss, sq[0:r, m % 2, 0:WCOL].rearrange("p (h d) -> p h d", d=HD), AX.X, ALU.add)\
                        .then_inc(qk_sum, 1)
                    v.wait_ge(qk_root, m + 1)
                    v.reciprocal(ss, ss)
                    if chunk >= 2:
                        v.wait_ge(qk_turned, NT * (chunk - 2) + nt + 1)
                    v.drain()
                    dst = qk_nat[0:r, chunk % 2, nt, :]
                    v.tensor_tensor(dst.rearrange("p (h d) -> p h d", d=HD),
                                    pair[m % 4 // 2][0:r, m % 2, 0:WCOL].rearrange("p (h d) -> p h d", d=HD),
                                    ss.unsqueeze(2).to_broadcast([r, 4, HD]), ALU.mult).then_inc(qk_scaled, 1)
                    v.drain()
                    gain = (gq if chunk < 2 else gk)[0:r, WCOL * (chunk % 2):WCOL * (chunk % 2 + 1)]
                    v.tensor_tensor(dst, dst, gain, ALU.mult).then_inc(qk_ready, 1)

            for n in range(2):
                for cb in range(2):
                    cc = 2 * n + cb
                    v.wait_ge(projected, after_projection(6 + 2 * n) + cb + 1)
                    v.wait_ge(gate_sig, 2 * n + cb + 1)
                    src = pair[2 + cb]
                    mid = PAD + HALF
                    v.tensor_tensor(u_p[:, cc, PAD:mid], src[:, 0, 0:HALF], sq[:, cb, 0:HALF], ALU.mult)
                    v.tensor_tensor(u_p[:, cc, mid:PAD + SEQ], src[:, 1, 0:SEQ - HALF], sq[:, cb, HALF:SEQ], ALU.mult)
                    v.tensor_tensor(u_s[:, cc, :, PAD:PAD + DEC_T],
                                    src[:, 1, SEQ - HALF:HALF].rearrange("p (s t) -> p s t", t=DEC_T),
                                    sq[:, cb, SEQ:N].rearrange("p (s t) -> p s t", t=DEC_T), ALU.mult).then_inc(u_done, 1)

            v.wait_ge(qk_kept, 4 * NT)
            for pr in range(PAIRS):
                for hh in range(2):
                    rows = slice(HD * hh, HD * hh + HD)
                    h = 2 * pr + hh
                    last = v.tensor_copy(q_blk[rows, :, pr, DEC_T * h:DEC_T * (h + 1)],
                                         q_t[rows, pr, SEQ:N].rearrange("p (s t) -> p s t", t=DEC_T))
            last.then_inc(q_blk_ready, 1)

            def prompt_max(u):
                i = unit(u)[0]
                v.wait_ge(ps_done, u + 1)
                diagonal = pair[0][:, u % 2, P * i:P * (i + 1)]
                v.tensor_tensor(diagonal, diagonal, causal[:, :], ALU.add)
                v.drain()
                v.tensor_reduce(stats[:, 16 + u % 2:17 + u % 2], pair[0][:, u % 2, 0:P * (i + 1)], AX.X, ALU.max,
                                negate=True).then_inc(pm_done, 1)

            def prompt_norm(u):
                i = unit(u)[0]
                v.wait_ge(pe_done, u + 1)
                total = stats[:, 20 + u % 2:21 + u % 2]
                v.reciprocal(total, total)
                v.drain()
                v.tensor_scalar(p_nat[:, u % 2, 0:P * (i + 1)], p_nat[:, u % 2, 0:P * (i + 1)], total, None, ALU.mult)\
                    .then_inc(pn_done, 1)

            def prompt_mix(w):
                i, pr, _ = unit(2 * w)
                v.wait_ge(pv_done, 2 * w + 2)
                src = pair[2][:, w % 2, 0:P]
                cols = slice(P * i, P * (i + 1))
                v.tensor_copy(x_hi[:, pr, cols], src)
                v.drain()
                v.tensor_tensor(x_lo[:, pr, cols], src, x_hi[:, pr, cols].bitcast(F32), ALU.subtract)\
                    .then_inc(po_done, 1)

            v.wait_ge(projected, after_projection(N_IN - 1))
            prompt_max(0)
            for u in range(UNITS):
                if u + 1 < UNITS:
                    prompt_max(u + 1)
                prompt_norm(u)
                if u % 2 == 0 and u:
                    prompt_mix(u // 2 - 1)
            prompt_mix(UNITS // 2 - 1)

            new = conv[:, :, SEQ:N].rearrange("p c (s t) -> p c s t", t=DEC_T)

            def tap(k):
                for cc in range(CC):
                    w = taps[:, cc, bass.ds(k, 1)]
                    v.scalar_tensor_tensor(conv[:, cc, 0:SEQ], u_p[:, cc, bass.ds(k, SEQ)], w, conv[:, cc, 0:SEQ],
                                           ALU.mult, ALU.add)
                    v.scalar_tensor_tensor(new[:, cc], u_s[:, cc, :, bass.ds(k, DEC_T)], w, new[:, cc],
                                           ALU.mult, ALU.add)
                v.drain()

            for cc in range(CC):
                for dst, src in ((conv[:, cc, 0:SEQ], u_p[:, cc, 0:SEQ]), (new[:, cc], u_s[:, cc, :, 0:DEC_T])):
                    v.tensor_scalar(dst, src, taps[:, cc, 0:1], conv_b[:, cc:cc + 1], ALU.mult, ALU.add)
            v.drain()
            with v.Fori(1, TAPS // 2) as k:
                tap(k)

            def rows_max(b):
                v.wait_ge(page_scored, 16 * (b + 1))
                v.wait_ge(own_scored, b + 1)
                gate, seen = stats[:, 0:8], stats[:, 8:16]
                largest, which = stats[:, 40:48], stats[:, 48:56]
                for half in range(2):
                    v.tensor_reduce(gate[:, 4 * half:4 * half + 4],
                                    pair[half][:, :, :].rearrange("p b (n k) -> p (b n) k", k=BLOCK), AX.X, ALU.add)
                v.drain()
                v.max(largest, gate)
                v.drain()
                v.max_index(which.bitcast(U32), largest, gate)
                v.drain()
                v.tensor_copy(largest, which.bitcast(U32))
                v.drain()
                v.tensor_scalar(seen, iota[:, 0:NBLK], largest[:, 0:1], None, ALU.is_equal)
                v.drain()
                for n in range(1, TOPB):
                    v.scalar_tensor_tensor(seen, iota[:, 0:NBLK], largest[:, n:n + 1], seen, ALU.is_equal, ALU.add)
                    v.drain()
                v.tensor_scalar(seen, seen, 1.0, -NEG, ALU.subtract, ALU.mult)
                v.drain()
                wait(v, s_turned, 5 * b)
                for half in range(2):
                    v.tensor_tensor(s_nat[:, PAST // 2 * half:PAST // 2 * (half + 1)].rearrange("p (n k) -> p n k", k=BLOCK),
                                    pair[half][:, :, :].rearrange("p b (n k) -> p (b n) k", k=BLOCK),
                                    seen[:, 4 * half:4 * half + 4].unsqueeze(2).to_broadcast([P, 4, BLOCK]), ALU.add)
                v.tensor_tensor(s_nat[:, PAST:KEYS_ALL], pair[3][:, 0, 0:NDEC], own[:, b, :], ALU.add)\
                    .then_inc(s_kept, 1)
                v.drain()
                v.tensor_reduce(stats[:, 24:25], s_nat[:, :], AX.X, ALU.max, negate=True).then_inc(s_max, 1)

            def rows_norm(b):
                v.wait_ge(s_exp, b + 1)
                v.reciprocal(stats[:, 25:26], stats[:, 25:26])
                v.drain()
                v.tensor_scalar(s_nat[:, :], s_nat[:, :], stats[:, 25:26], None, ALU.mult).then_inc(s_normed, 1)

            def mix_output(b):
                v.wait_ge(o_turned, b + 1)
                for part in range(2):
                    for h in range(HEADS):
                        rows = slice(HD * (h % 2), HD * (h % 2) + HD)
                        cols = slice(SEQ + 16 * b, SEQ + 16 * b + 16)
                        src = pair[3][rows, 0, P * (h // 2):P * (h // 2 + 1)]\
                            .rearrange("p (j h t) -> p j h t", j=4, t=DEC_T)[:, :, h, :]
                        hi = x_hi[rows, h // 2, cols].rearrange("p (j t) -> p j t", t=DEC_T)
                        lo = x_lo[rows, h // 2, cols].rearrange("p (j t) -> p j t", t=DEC_T)
                        if part == 0:
                            last = v.tensor_copy(hi, src)
                        else:
                            last = v.tensor_tensor(lo, src, hi.bitcast(F32), ALU.subtract)
                    if part == 0:
                        v.drain()
                last.then_inc(o_mixed, 1)

            rows_max(0)
            rows_norm(0)
            with v.Fori(TAPS // 2, TAPS) as k:
                tap(k)
            v.memset(stats[:, 56:57], 0.0).then_inc(conv_done, 1)
            rows_max(1)
            rows_norm(1)
            mix_output(0)
            reciprocal_rms(rootc_done)
            for cc in range(CC):
                last = v.scalar_tensor_tensor(conv[:, cc, :], conv[:, cc, :], conv_g[:, cc:cc + 1], rstd[:, :],
                                              ALU.mult, ALU.mult)
            last.then_inc(z_done, 1)
            for cc in range(CC):
                v.wait_ge(sigc_done, cc + 1)
                v.tensor_tensor(conv[:, cc, :], conv[:, cc, :], sig_c[:, cc, :], ALU.mult)
                v.drain()
                parts(PAIRS + cc, conv[:, cc, :])
            mix_output(1)
            v.memset(stats[:, 56:57], 0.0).then_inc(mix_ready, 1)

            for db in range(KD):
                v.wait_ge(projected, after_projection(N_IN - 1) + db + 1)
                v.tensor_tensor(two(resid[:, db, :]), two(resid[:, db, :]), halves(pair[db % 2]), ALU.add)\
                    .then_inc(h_done, 1)
            normed(g2, root2_done, x2_ready)

            with v.Fori(0, PH) as h:
                for nt in range(NT):
                    r = ROWS[nt]
                    bank = pair[2 + nt // 4][0:r, nt // 2 % 2, :]
                    m, ix = m16[0:r, nt], i16[0:r, nt]
                    score = [bank[:, 256 * (nt % 2) + P * x:256 * (nt % 2) + P * x + P] for x in range(2)]
                    v.wait_ge(scored, 3 * h + nt // 2 + 1)
                    alone(v, v_waited)
                    for x in range(2):
                        v.max(m[:, x, 0:8], score[x])
                    v.drain()
                    for x in range(2):
                        v.match_replace(rest[0:r, x, :], m[:, x, 0:8], score[x], FLOOR)
                        v.max_index(ix[:, x, 0:8], m[:, x, 0:8], score[x])
                    v.drain()
                    for x in range(2):
                        v.max(m[:, x, 8:16], rest[0:r, x, :])
                    v.drain()
                    for x in range(2):
                        v.max_index(ix[:, x, 8:16], m[:, x, 8:16], rest[0:r, x, :])
                    v.drain()
                    v.tensor_copy(best[0:r, nt, bass.ds(h, 1), :, :].rearrange("p a x k -> p (a x k)"),
                                  m.rearrange("p x k -> p (x k)"))
                    v.tensor_copy(best_i[0:r, nt, bass.ds(h, 1), :, :].rearrange("p a x k -> p (a x k)"),
                                  ix.rearrange("p x k -> p (x k)")).then_inc(ranked, 1)
            v.drain()

            for nt in range(NT):
                r = ROWS[nt]
                v.tensor_tensor(cand[0:r], best[0:r, nt, :, 0, :].unsqueeze(3).to_broadcast([r, PH, TOPK, TOPK]),
                                best[0:r, nt, :, 1, :].unsqueeze(2).to_broadcast([r, PH, TOPK, TOPK]), ALU.add)
                v.drain()
                for h0 in range(0, PH, 2):
                    sums = [cand[0:r, h0 + x].rearrange("p a b -> p (a b)") for x in range(2)]
                    for x in range(2):
                        v.max(top16[0:r, h0 + x, 0:8], sums[x])
                    v.drain()
                    for x in range(2):
                        v.match_replace(crest[0:r, x, :], top16[0:r, h0 + x, 0:8], sums[x], FLOOR)
                        v.max_index(pos16[0:r, h0 + x, 0:8], top16[0:r, h0 + x, 0:8], sums[x])
                    v.drain()
                    for x in range(2):
                        v.max(top16[0:r, h0 + x, 8:16], crest[0:r, x, :])
                    v.drain()
                    for x in range(2):
                        v.max_index(pos16[0:r, h0 + x, 8:16], top16[0:r, h0 + x, 8:16], crest[0:r, x, :])
                    v.drain()
                v.tensor_copy(den[0:r, :].unsqueeze(2), top16[0:r, :, 0:1])
                v.drain()
                v.tensor_tensor(top16[0:r], top16[0:r], den[0:r, :].unsqueeze(2).to_broadcast([r, PH, TOPK]),
                                ALU.subtract).then_inc(rt_top, 1)
                flat = pos16[0:r].rearrange("p h k -> p (h k)")
                v.tensor_scalar(digit[0:r, 0, :], flat, 4, None, ALU.logical_shift_right)
                v.tensor_scalar(digit[0:r, 1, :], flat, TOPK - 1, None, ALU.bitwise_and)
                v.drain()
                v.tensor_copy(digit_f[0:r], digit[0:r])
                wait(v, rt_turned, nt)
                v.drain()
                for x in range(2):
                    hot_h = hot[0:r].rearrange("p (h k) a -> p h k a", h=PH)
                    v.tensor_tensor(hot[0:r], digit_f[0:r, x, :].unsqueeze(2).to_broadcast([r, SLOTS, TOPK]),
                                    iota[0:r, 0:TOPK].unsqueeze(1).to_broadcast([r, SLOTS, TOPK]), ALU.is_equal)
                    v.drain()
                    v.tensor_tensor(hot_h, hot_h,
                                    best_i[0:r, nt, :, x, :].unsqueeze(2).to_broadcast([r, PH, TOPK, TOPK]), ALU.mult)
                    v.drain()
                    v.tensor_reduce(found[0:r, x, :], hot[0:r], AX.X, ALU.add)
                    v.drain()
                v.wait_ge(rt_exp, nt + 1)
                v.tensor_reduce(den[0:r, :], top16[0:r], AX.X, ALU.add)
                v.drain()
                v.reciprocal(den[0:r, :], den[0:r, :])
                v.drain()
                v.tensor_tensor(found[0:r, 2, :].rearrange("p (h k) -> p h k", h=PH), top16[0:r],
                                den[0:r, :].unsqueeze(2).to_broadcast([r, PH, TOPK]), ALU.mult).then_inc(rt_found, 1)
                v.drain()

            v.wait_ge(rt_kept, NT)

            def gate_rows(c, parity):
                wait(v, hot1_ready, GROUPS * (c - 1))
                alone(v, v_waited)
                v.drain()
                v.tensor_copy(current[:, parity, :, :], slots[:, :, bass.ds(GCHUNK * c, GCHUNK)])\
                    .then_inc(current_ready, 1)
                v.drain()
                for q in range(GROUPS):
                    wait(v, g_made, GROUPS * c + q - 1)
                    for t in range(TOK):
                        at = TOK * q + t
                        last = v.tensor_scalar(hot2[:, q % 2, t, :], iota[:, :], current[:, parity, 1, at:at + 1],
                                               current[:, parity, 2, at:at + 1], ALU.is_equal, ALU.mult)
                    last.then_inc(hot2_ready, 1)

            gate_rows(0, 0)
            gate_rows(1, 1)
            gate_rows(2, 0)
            with v.Fori(1, NG // 2) as i:
                gate_rows(2 * i + 1, 1)
                gate_rows(2 * i + 2, 0)

            def low_v(s, slot):
                v.wait_ge(v_hi_done, s + 1)
                v.tensor_tensor(v_lo[:, slot, :], v_raw[:, slot, :], v_hi[:, slot, :].bitcast(F32), ALU.subtract)\
                    .then_inc(v_lo_done, 1)

            def gated(it, k, j):
                s = 4 * it + k
                slot = k % 2
                v.wait_ge(gelu_done, 2 * s + j + 1)
                if j == 0:
                    if k % 2 == 0:
                        v.wait_ge(g_loaded[k // 2], 16 * (it + 1))
                    wait(v, down_done, KD * s - KD)
                tile = 2 * (k % 2) + j
                v.tensor_tensor(prod[:, j, :].rearrange("p (c t) -> p c t", t=GCHUNK),
                                act[:, j, :].rearrange("p (c t) -> p c t", t=GCHUNK),
                                g_in[:, k // 2, :, GCHUNK * tile:GCHUNK * (tile + 1)], ALU.mult)
                v.drain()
                v.tensor_copy(a_hi[:, slot, j, :], prod[:, j, :])
                v.drain()
                v.tensor_tensor(a_lo[:, slot, j, :], prod[:, j, :], a_hi[:, slot, j, :].bitcast(F32), ALU.subtract)\
                    .then_inc(a_done, 1)

            def add_blocks(s):
                for db in range(KD):
                    v.wait_ge(down_done, KD * s + db + 1)
                    last = v.tensor_tensor(two(resid[:, db, :]), two(resid[:, db, :]), halves(pair[2 + db % 2]), ALU.add)
                    last.then_inc(added, 1)

            def mixer(it, k):
                s = 4 * it + k
                low_v(s, k % 2)
                gated(it, k, 0)
                gated(it, k, 1)
                if not (isinstance(s, int) and s == 0):
                    add_blocks(s - 1)

            for k in range(4):
                mixer(0, k)
            with v.Fori(1, STEPS // 4) as it:
                for k in range(4):
                    mixer(it, k)
            add_blocks(STEPS - 1)

        @block.tensor
        def _(te):
            def product(out, stationary, moving, start, stop):
                (s_hi, s_lo), (m_hi, m_lo) = stationary, moving
                te.matmul(out, s_hi, m_hi, start=start, stop=False)
                te.matmul(out, s_hi, m_lo, start=False, stop=False)
                return te.matmul(out, s_lo, m_hi, start=False, stop=stop)

            def both(a, b, *index):
                return a[index], b[index]

            def sum_squares(banks, src, blocks, squared, summed):
                for kd in range(blocks):
                    te.wait_ge(squared, kd + 1)
                    for half in range(2):
                        last = te.matmul(banks[:, half, 0:HALF], ones[:, :], src[:, kd % 2, HALF * half:HALF * (half + 1)],
                                         start=kd == 0, stop=kd == blocks - 1)
                    last.then_inc(summed, 1)

            def block_product(banks, slot, cb):
                for kd in range(KD):
                    col = WCOL * kd + P * cb
                    stationary = (w_hi[:, slot, col:col + P], w_lo[:, slot, col:col + P])
                    for half in range(2):
                        cols = slice(HALF * half, HALF * (half + 1))
                        last = product(banks[:, half, 0:HALF], stationary, (x_hi[:, kd, cols], x_lo[:, kd, cols]),
                                       kd == 0, kd == KD - 1)
                return last

            te.wait_ge(const_ready, 1)
            sum_squares(pair[0], sq, KD, sq1_done, sum1_done)

            def turn_qk(chunk):
                for nt in range(NT):
                    m = NT * chunk + nt
                    r = ROWS[nt]
                    te.wait_ge(qk_ready, m + 1)
                    wait(te, qk_kept, m - 1)
                    for b in range(2):
                        last = te.transpose(pair[2][:, m % 2, P * b:P * b + r],
                                            qk_nat[0:r, chunk % 2, nt, P * b:P * (b + 1)], ident[0:r, 0:r])
                    last.then_inc(qk_turned, 1)

            te.wait_ge(x_ready, 1)
            for chunk in range(6):
                te.wait_ge(w_split, chunk + 1)
                for nt in range(NT):
                    m = NT * chunk + nt
                    r = ROWS[nt]
                    if 4 <= m < 4 * NT + 4:
                        te.wait_ge(qk_scaled, m - 3)
                    elif m >= 4:
                        te.wait_ge(v_kept, m - 3 - 4 * NT)
                    tokens = slice(P * nt, P * nt + r)
                    for kd in range(KD):
                        cols = slice(WCOL * kd, WCOL * (kd + 1))
                        last = product(pair[m % 4 // 2][0:r, m % 2, 0:WCOL],
                                       (x_hi[:, kd, tokens], x_lo[:, kd, tokens]),
                                       (w_hi[:, chunk % 2, cols], w_lo[:, chunk % 2, cols]), kd == 0, kd == KD - 1)
                    last.then_inc(projected, 1)
                if 1 <= chunk <= 4:
                    turn_qk(chunk - 1)
            for chunk in range(6, N_IN):
                te.wait_ge(w_split, chunk + 1)
                for cb in range(2):
                    banks = pair[cb if chunk % 2 == 0 else 2 + cb]
                    if chunk == 6:
                        te.wait_ge(v_kept, 2 * NT)
                    elif chunk == 7:
                        te.wait_ge(qk_kept, 4 * NT)
                    elif chunk == 8:
                        te.wait_ge(gate_sig, cb + 1)
                    else:
                        te.wait_ge(u_done, cb + 1)
                    block_product(banks, chunk % 2, cb).then_inc(projected, 1)

            def prompt_scores(u):
                i, pr, hh = unit(u)
                rows = slice(HD * hh, HD * hh + HD)
                wait(te, pe_done, u - 1)
                te.matmul(pair[0][:, u % 2, 0:P * (i + 1)], q_t[rows, pr, P * i:P * (i + 1)],
                          k_t[rows, pr, 0:P * (i + 1)], start=True, stop=True).then_inc(ps_done, 1)

            def prompt_turn(u):
                i = unit(u)[0]
                te.wait_ge(pn_done, u + 1)
                wait(te, ptc_done, u - 1)
                for kb in range(i + 1):
                    last = te.transpose(pair[1][:, u % 2, P * kb:P * (kb + 1)], p_nat[:, u % 2, P * kb:P * (kb + 1)],
                                        ident[:, :])
                last.then_inc(pt_done, 1)

            def prompt_values(u):
                i, pr, hh = unit(u)
                w = u // 2
                te.wait_ge(ptc_done, u + 1)
                wait(te, po_done, w - 1)
                head = HD * (2 * pr + hh)
                for kb in range(i + 1):
                    last = te.matmul(pair[2][HD * hh:HD * (hh + 1), w % 2, 0:P], v_nat[:, kb, head:head + HD],
                                     p_tr[:, u % 2, P * kb:P * (kb + 1)], start=kb == 0, stop=kb == i)
                last.then_inc(pv_done, 1)

            te.wait_ge(gate_sig, 4)
            te.wait_ge(u_done, 4)
            prompt_scores(0)
            for u in range(UNITS):
                if u + 1 < UNITS:
                    prompt_scores(u + 1)
                if u:
                    prompt_values(u - 1)
                prompt_turn(u)
            prompt_values(UNITS - 1)

            def score_chunk(chunk):
                s, c = chunk // 4, chunk % 4
                rows = slice(32 * (s % BATCH), 32 * (s % BATCH) + 32)
                te.wait_ge(page_kept, 4 * (chunk + 1))
                for pr in range(PAIRS):
                    last = te.matmul(pair[c // 2][rows, c % 2, :], q_blk[:, s, pr, :], page_kt[:, chunk % 2, pr, :],
                                     start=pr == 0, stop=pr == PAIRS - 1)
                last.then_inc(page_scored, 1)

            def score_batch(b):
                for chunk in range(16 * b, 16 * b + 16):
                    te.wait_ge(page_loaded[chunk % 2], 64 * (chunk // 2 + 1))
                    for p in range(4):
                        wait(te, page_kept, 4 * chunk + p - 1)
                        for pr in range(PAIRS):
                            last = te.transpose(pair[2][:, p % 2, P * pr:P * (pr + 1)],
                                                page_ring[:, chunk % 2, p, P * pr:P * (pr + 1)], ident[:, :])
                        last.then_inc(page_turned, 1)
                    if chunk > 16 * b:
                        score_chunk(chunk - 1)
                score_chunk(16 * b + 15)
                for j in range(BATCH):
                    for pr in range(PAIRS):
                        last = te.matmul(pair[3][32 * j:32 * j + 32, 0, 0:NDEC], q_blk[:, BATCH * b + j, pr, :],
                                         k_t[:, pr, SEQ:N], start=pr == 0, stop=pr == PAIRS - 1)
                last.then_inc(own_scored, 1)

            def turn_probabilities(b):
                te.wait_ge(s_normed, b + 1)
                for g in range(5):
                    if g >= 2:
                        te.wait_ge(s_turned_kept, 5 * b + g - 1)
                    for a in range(4 if g < 4 else 1):
                        key = PAGE * (4 * g + a)
                        width = PAGE if g < 4 else NDEC
                        last = te.transpose(pair[2][0:width, g % 2, P * a:P * (a + 1)], s_nat[:, key:key + width],
                                            ident[:, :])
                    last.then_inc(s_turned, 1)

            def attend_batch(b):
                te.wait_ge(s_turned_kept, 5 * (b + 1))
                wait(te, o_kept, b)
                for j in range(BATCH):
                    rows = slice(32 * j, 32 * j + 32)
                    out = pair[3][rows, 1, :]
                    for c in range(4):
                        chunk = 16 * b + 4 * j + c
                        te.wait_ge(page_loaded[chunk % 2], 64 * (CHUNKS // 2 + chunk // 2 + 1))
                        for p in range(4):
                            last = te.matmul(out, pages_pt[:, 4 * c + p, rows], page_ring[:, chunk % 2, p, :],
                                             start=c == 0 and p == 0, stop=False)
                        last.then_inc(pages_used, 1)
                    last = te.matmul(out, own_pt[:, rows], v_nat[0:NDEC, NT - 1, :], start=False, stop=True)
                last.then_inc(o_done, 1)

            def turn_output(b):
                te.wait_ge(o_kept, b + 1)
                wait(te, o_mixed, b)
                for pr in range(PAIRS):
                    last = te.transpose(pair[3][:, 0, P * pr:P * (pr + 1)], o_nat[:, P * pr:P * (pr + 1)], ident[:, :])
                last.then_inc(o_turned, 1)

            te.wait_ge(q_blk_ready, 1)
            te.wait_ge(ptc_done, UNITS)
            te.wait_ge(pe_done, UNITS)
            te.wait_ge(po_done, UNITS // 2)
            score_batch(0)
            te.wait_ge(s_kept, 1)
            score_batch(1)
            turn_probabilities(0)
            attend_batch(0)
            te.wait_ge(s_kept, 2)
            sum_squares(pair[0], sqc, CC, sqc_done, sumc_done)
            turn_output(0)
            turn_probabilities(1)
            attend_batch(1)
            turn_output(1)

            te.wait_ge(mix_ready, 1)
            for db in range(KD):
                chunk = N_IN + db // 2
                te.wait_ge(w_split, chunk + 1)
                wait(te, h_done, db - 1)
                block_product(pair[db % 2], chunk % 2, db % 2).then_inc(projected, 1)
            sum_squares(pair[2], sq, KD, sq2_done, sum2_done)

            def score_keys(h):
                te.wait_ge(qh_kept, 2 * h + 2)
                for nt in range(NT):
                    r = ROWS[nt]
                    if nt % 2 == 0:
                        wait(te, ranked, NT * (h - 1) + min(nt + 2, NT))
                    bank = pair[2 + nt // 4][0:r, nt // 2 % 2, :]
                    for x in range(2):
                        at = 256 * (nt % 2) + P * x
                        last = te.matmul(bank[:, at:at + P], qh_t[:, 0, x, P * nt:P * nt + r], keys[:, 2 * h + x, :],
                                         start=True, stop=True)
                    if nt % 2 or nt == NT - 1:
                        last.then_inc(scored, 1)

            te.wait_ge(x2_ready, 1)
            te.wait_ge(keys_loaded, 16)
            for h in range(PH):
                chunk = N_IN + N_OUT + h
                te.wait_ge(w_split, chunk + 1)
                for half in range(2):
                    wait(te, qh_kept, 2 * h + half - 1)
                    block_product(pair[half], chunk % 2, half).then_inc(projected, 1)
                score_keys(h)

            te.wait_ge(ranked, NT * PH)
            for nt in range(NT):
                r = ROWS[nt]
                te.wait_ge(rt_found, nt + 1)
                wait(te, rt_kept, nt)
                for a in range(3):
                    last = te.transpose(pair[3][:, 1, P * a:P * a + r], found[0:r, a, :], ident[0:r, 0:r])
                last.then_inc(rt_turned, 1)

            te.wait_ge(qh_kept, 2 * PH)

            def make_gates(c):
                for q in range(GROUPS):
                    g = GROUPS * c + q
                    te.wait_ge(hot1_ready, g + 1)
                    te.wait_ge(hot2_ready, g + 1)
                    wait(te, g_kept, g - 1)
                    for t in range(TOK):
                        last = te.matmul(pair[0][:, q % 2, P * t:P * (t + 1)], hot1[:, q % 2, t, :], hot2[:, q % 2, t, :],
                                         start=True, stop=True)
                    last.then_inc(g_made, 1)

            make_gates(0)
            with te.Fori(0, NG // 2) as i:
                make_gates(2 * i + 1)
                make_gates(2 * i + 2)

            def up(s, slot):
                te.wait_ge(u_lo_done, s + 1)
                for j in range(2):
                    wait(te, gelu_done, 2 * s + j - 1)
                    block_product(pair[j], slot, j).then_inc(up_done, 1)

            def down(s, slot):
                te.wait_ge(v_lo_done, s + 1)
                te.wait_ge(a_done, 2 * s + 2)
                for db in range(KD):
                    wait(te, added, KD * s + db - 1)
                    for j in range(2):
                        col = D * j + P * db
                        stationary = (v_hi[:, slot, col:col + P], v_lo[:, slot, col:col + P])
                        for half in range(2):
                            cols = slice(HALF * half, HALF * (half + 1))
                            last = product(pair[2 + db % 2][:, half, 0:HALF], stationary,
                                           (a_hi[:, slot, j, cols], a_lo[:, slot, j, cols]), j == 0, j == 1)
                    last.then_inc(down_done, 1)

            te.wait_ge(g_kept, NG * GROUPS)
            up(0, 0)
            for k in range(1, 4):
                up(k, k % 2)
                down(k - 1, (k - 1) % 2)
            with te.Fori(1, STEPS // 4) as it:
                for k in range(4):
                    up(4 * it + k, k % 2)
                    down(4 * it + k - 1, (k - 1) % 2)
            down(STEPS - 1, (STEPS - 1) % 2)


def kernel(**inputs):
    import numpy as np
    import concourse.bacc as bacc
    from concourse.bass_utils import run_bass_kernel_spmd

    a = {k: np.asarray(v) for k, v in inputs.items()}

    def columns(w, n):
        return w.reshape(KD, P, n, WCOL).transpose(2, 1, 0, 3).reshape(n, P, WC)

    def across(g):
        return g.reshape(-1, P).T

    x = np.concatenate([a["x_prompt"].reshape(SEQ, D), a["x_sample"].reshape(NDEC, D)], axis=0)
    sent = {
        "x_t": x.reshape(N, KD, P).transpose(2, 1, 0),
        "w_in": columns(a["w_in"][0], N_IN),
        "w_out": columns(a["w_out"][0], N_OUT),
        "w_query": columns(a["peer_w_query"][0], N_WQ),
        "norm1_g": across(a["norm1_g"][0]),
        "norm2_g": across(a["norm2_g"][0]),
        "q_norm_g": a["q_norm_g"][0].reshape(CH),
        "k_norm_g": a["k_norm_g"][0].reshape(CH),
        "conv_w": a["conv_w"][0].reshape(TAPS, CC, P).transpose(2, 1, 0),
        "conv_b": across(a["conv_b"][0]),
        "conv_norm_g": across(a["conv_norm_g"][0]),
        "state_t": a["state_conv"][0].reshape(DEC_B, PAD, CC, P).transpose(3, 2, 0, 1),
        "page_table": a["page_table"].reshape(1, DEC_B * PAGES),
        "cache_k": a["cache_k"][0].reshape(POOL_PAGES, PAGE, CH),
        "cache_v": a["cache_v"][0].reshape(POOL_PAGES, PAGE, CH),
        "keys_t": np.stack([a["peer_keys1"][0], a["peer_keys2"][0]], axis=1).reshape(2 * PH, P, P).transpose(2, 0, 1),
        "u_t": a["peer_u"][0].reshape(P, STEPS, 2, KD, P).transpose(1, 4, 3, 2, 0).reshape(STEPS, P, WC),
        "v_t": a["peer_v"][0].reshape(P, STEPS, WC).transpose(1, 0, 2),
    }
    sent = {k: np.ascontiguousarray(v) for k, v in sent.items()}
    shapes = {"y_t": (P, KD, N), "k_out": (N, CH), "v_out": (N, CH), "conv_p_out": (P, CC, PAD),
              "conv_s_out": (P, CC, DEC_B, PAD)}
    nc = bacc.Bacc("TRN2", target_bir_lowering=False, num_devices=1)
    io = {k: nc.dram_tensor("in_" + k, v.shape, mybir.dt.from_np(v.dtype), kind="ExternalInput").ap()
          for k, v in sent.items()}
    io.update({k: nc.dram_tensor("out_" + k, s, F32, kind="ExternalOutput").ap() for k, s in shapes.items()})
    build_layer(nc, io)
    run = run_bass_kernel_spmd(nc, [{"in_" + k: v for k, v in sent.items()}], core_ids=[0])
    got = {k: np.asarray(run.results[0]["out_" + k]) for k in shapes}
    y = got["y_t"].transpose(2, 1, 0).reshape(N, D)
    heads = (HEADS, HD)
    return (
        y[:SEQ].reshape(1, SEQ, D),
        y[SEQ:].reshape(DEC_B, DEC_T, D),
        got["k_out"][:SEQ].reshape(1, 1, SEQ, *heads),
        got["v_out"][:SEQ].reshape(1, 1, SEQ, *heads),
        got["conv_p_out"].transpose(2, 1, 0).reshape(1, 1, PAD, CH),
        got["k_out"][SEQ:].reshape(1, DEC_B, DEC_T, *heads),
        got["v_out"][SEQ:].reshape(1, DEC_B, DEC_T, *heads),
        got["conv_s_out"].transpose(2, 3, 1, 0).reshape(1, DEC_B, PAD, CH),
    )
```

```python
import concourse.bass as bass
from concourse import mybir

F32 = mybir.dt.float32
F32R = mybir.dt.float32r
I32 = mybir.dt.int32
U32 = mybir.dt.uint32
ALU = mybir.AluOpType
ACT = mybir.ActivationFunctionType
AX = mybir.AxisListType

P = 128
D = 1024
KD = D // P
SEQ = 512
DEC_B, DEC_T = 8, 4
NDEC = DEC_B * DEC_T
N = SEQ + NDEC
HALF = N // 2
NT = (N + P - 1) // P
ROWS = [min(P, N - P * t) for t in range(NT)]
HEADS, HD = 8, 64
PAIRS = HEADS // 2
CH = 512
CC = CH // P
TAPS = 31
PAD = TAPS - 1
PAGES, PAGE = 16, 128
POOL_PAGES = 160
BLOCK, TOPB = 256, 3
BATCH = 4
PAST = PAGES * PAGE
NBLK = PAST // BLOCK
KEYS_ALL = PAST + NDEC
PH = 8
TOPK = 16
SLOTS = PH * TOPK
EPS = 1e-6
NEG = -1.0e30
FLOOR = -3.0e38

WC = 2048
WCOL = WC // KD
N_IN, N_OUT, N_WQ = 10, 4, 8
W_CHUNKS = N_IN + N_OUT + N_WQ
STEPS = 64
GCHUNK = 32
NG = N // GCHUNK
TOK = 4
GROUPS = GCHUNK // TOK
RANK_STEPS = 15
EARLY = RANK_STEPS + NG


def halves(ap):
    return ap[:, :, 0:HALF]


def two(ap):
    return ap.rearrange("p (b n) -> p b n", b=2)


def wait(engine, semaphore, value):
    if not isinstance(value, int) or value > 0:
        engine.wait_ge(semaphore, value)


def alone(engine, ready):
    engine.sem_inc(ready, 1)


def after_projection(chunk):
    return sum(5 if c < 6 else 2 for c in range(chunk + 1))


def build_layer(nc, io):
    base = nc.sbuf_base + 31 & ~31
    top = nc.sbuf_usable_end
    place = {"at": base}

    def sb(name, shape, dtype=F32, at=None):
        size = 4
        for s in shape[1:]:
            size *= s
        if at is None:
            at = place["at"]
        place["at"] = at + size + 31 & ~31
        assert place["at"] <= top, (name, place["at"], top)
        return nc.alloc_sbuf_tensor_at(name, shape, dtype, offset=at)

    resid = sb("resid", [P, KD, N])
    x_hi = sb("x_hi", [P, KD, N], F32R)
    x_lo = sb("x_lo", [P, KD, N], F32R)
    w_raw_1 = place["at"] + 4 * WC
    w_raw = sb("w_raw", [P, 2, WC])
    w_hi = sb("w_hi", [P, 2, WC], F32R)
    w_lo = sb("w_lo", [P, 2, WC], F32R)
    ident = sb("ident", [P, P])
    ones = sb("ones", [P, P])
    iota = sb("iota", [P, P])
    rstd = sb("rstd", [P, N])
    g1 = sb("g1", [P, KD])
    g2 = sb("g2", [P, KD])
    eps = sb("eps", [P, 1])
    stats = sb("stats", [P, 64])
    overlay = place["at"]

    v_nat = sb("v_nat", [P, NT, CH])
    q_t = sb("q_t", [P, PAIRS, N])
    k_t = sb("k_t", [P, PAIRS, N])
    u_p = sb("u_p", [P, CC, PAD + SEQ])
    u_s = sb("u_s", [P, CC, DEC_B, PAD + DEC_T])
    conv = sb("conv", [P, CC, N])
    q_blk = sb("q_blk", [P, DEC_B, PAIRS, HEADS * DEC_T])
    gq = sb("gq", [P, CH])
    gk = sb("gk", [P, CH])
    taps = sb("taps", [P, CC, TAPS])
    conv_b = sb("conv_b", [P, CC])
    conv_g = sb("conv_g", [P, CC])
    causal = sb("causal", [P, P])
    own = sb("own", [P, 2, NDEC])
    page_row = sb("page_row", [1, DEC_B * PAGES], I32)
    page_ring = sb("page_ring", [P, 2, 4, CH])
    sq = sb("sq", [P, 2, N])
    at_keys = place["at"]
    page_kt = sb("page_kt", [P, 2, BATCH, PAIRS, PAGE])
    end_keys = place["at"]
    qk_nat = sb("qk_nat", [P, 2, NT, WCOL], at=at_keys)
    s_nat = sb("s_nat", [P, KEYS_ALL], at=end_keys)
    o_nat = sb("o_nat", [P, CH])
    at_q = overlay + 4 * NT * CH
    p_nat = sb("p_nat", [P, 2, SEQ], at=w_raw_1)
    p_tr = sb("p_tr", [P, 2, SEQ])
    pages_pt = sb("pages_pt", [P, PAGES, P], at=at_q)
    own_pt = sb("own_pt", [NDEC, P])
    sqc = sb("sqc", [P, 2, N], at=at_q + 4 * PAIRS * N)
    sig_c = sb("sig_c", [P, CC, N], at=at_q + 8 * PAIRS * N)

    keys = sb("keys", [P, 2 * PH, P], at=overlay)
    qh_t = sb("qh_t", [P, 2, 2, N])
    best = sb("best", [P, NT, PH, 2, TOPK])
    best_i = sb("best_i", [P, NT, PH, 2, TOPK])
    m16 = sb("m16", [P, NT, 2, TOPK])
    i16 = sb("i16", [P, NT, 2, TOPK], U32)
    rest = sb("rest", [P, 2, P])
    slots = sb("slots", [P, 3, N])
    at_cand = place["at"]
    cand = sb("cand", [P, PH, TOPK, TOPK])
    crest = sb("crest", [P, 2, TOPK * TOPK])
    hot = sb("hot", [P, SLOTS, TOPK])
    top16 = sb("top16", [P, PH, TOPK])
    pos16 = sb("pos16", [P, PH, TOPK], U32)
    digit = sb("digit", [P, 2, SLOTS], U32)
    digit_f = sb("digit_f", [P, 2, SLOTS])
    found = sb("found", [P, 3, SLOTS])
    den = sb("den", [P, PH])
    current = sb("current", [P, 2, 3, GCHUNK], at=at_cand)
    hot1 = sb("hot1", [P, 2, TOK, P])
    hot2 = sb("hot2", [P, 2, TOK, P])
    g_out = sb("g_out", [P, 2, P, GCHUNK])
    act_out = sb("act_out", [P, 2, 2, N])

    v_raw = sb("v_raw", [P, 2, WC], at=overlay)
    v_hi = sb("v_hi", [P, 2, WC], F32R)
    v_lo = sb("v_lo", [P, 2, WC], F32R)
    g_in = sb("g_in", [P, 2, NG, 4 * GCHUNK])
    act = sb("act", [P, 2, 2, N])
    a_hi = sb("a_hi", [P, 2, 2, N], F32R)
    a_lo = sb("a_lo", [P, 2, 2, N], F32R)

    pair = [nc.alloc_psum_tensor(f"pair{i}", [P, 2, 512], F32) for i in range(4)]

    gates = nc.dram_tensor("gates", [NG, P, P, GCHUNK], F32).ap()
    acts = nc.dram_tensor("acts", [EARLY, P, 2 * N], F32).ap()

    def bank(b):
        return pair[b // 2][:, b % 2, :]

    TURN, P_SCORES, P_TURN, P_OUT = 4, 5, 6, 7

    names = {}

    def sem(name):
        if name not in names:
            names[name] = nc.alloc_semaphore(name)
        return names[name]

    state_loaded = sem("state_loaded")
    v_waited = sem("v_waited")
    x_loaded = [sem(f"x_loaded{part}") for part in range(4)]
    small_loaded, pages_known = sem("small_loaded"), sem("pages_known")
    w_loaded = [sem("w_loaded0"), sem("w_loaded1")]
    w_high, w_split, projected = sem("w_high"), sem("w_split"), sem("projected")
    scaled1, high1, scaled2, high2 = sem("scaled1"), sem("high1"), sem("scaled2"), sem("high2")
    const_ready = sem("const_ready")
    sq1_done, sum1_done, root1_done, x_ready = sem("sq1_done"), sem("sum1_done"), sem("root1_done"), sem("x_ready")
    qk_sq, qk_sum, qk_root, qk_scaled, qk_ready = sem("qk_sq"), sem("qk_sum"), sem("qk_root"), sem("qk_scaled"), sem("qk_ready")
    qk_turned, qk_kept, v_kept = sem("qk_turned"), sem("qk_kept"), sem("v_kept")
    gate_sig, u_done = sem("gate_sig"), sem("u_done")
    stored = sem("stored")
    ps_done, pm_done, pe_done, pn_done = sem("ps_done"), sem("pm_done"), sem("pe_done"), sem("pn_done")
    pt_done, ptc_done, pv_done, po_done = sem("pt_done"), sem("ptc_done"), sem("pv_done"), sem("po_done")
    q_blk_ready = sem("q_blk_ready")
    page_loaded = [sem("page_loaded0"), sem("page_loaded1")]
    page_turned, page_kept, page_scored, own_scored = sem("page_turned"), sem("page_kept"), sem("page_scored"), sem("own_scored")
    s_kept, s_max, s_exp, s_normed = sem("s_kept"), sem("s_max"), sem("s_exp"), sem("s_normed")
    s_turned, s_turned_kept, pages_used, o_done = sem("s_turned"), sem("s_turned_kept"), sem("pages_used"), sem("o_done")
    o_kept, o_turned, o_mixed = sem("o_kept"), sem("o_turned"), sem("o_mixed")
    conv_done, sqc_done, sumc_done, rootc_done, z_done, sigc_done = (
        sem("conv_done"), sem("sqc_done"), sem("sumc_done"), sem("rootc_done"), sem("z_done"), sem("sigc_done"))
    mix_ready, h_done = sem("mix_ready"), sem("h_done")
    sq2_done, sum2_done, root2_done, x2_ready = sem("sq2_done"), sem("sum2_done"), sem("root2_done"), sem("x2_ready")
    keys_loaded, qh_kept, scored, ranked = sem("keys_loaded"), sem("qh_kept"), sem("scored"), sem("ranked")
    rt_top, rt_exp, rt_found, rt_turned, rt_kept = sem("rt_top"), sem("rt_exp"), sem("rt_found"), sem("rt_turned"), sem("rt_kept")
    hot_ready = sem("hot_ready")
    acts_stored = [sem("acts_stored0"), sem("acts_stored1")]
    acts_loaded = [sem("acts_loaded0"), sem("acts_loaded1")]
    gated, a_high = sem("gated"), sem("a_high")
    g_made, g_kept = sem("g_made"), sem("g_kept")
    g_stored = [sem("g_stored0"), sem("g_stored1")]
    u_loaded = [sem("u_loaded0"), sem("u_loaded1")]
    v_loaded = [sem("v_loaded0"), sem("v_loaded1")]
    g_loaded = [sem("g_loaded0"), sem("g_loaded1")]
    u_hi_done, u_lo_done, v_hi_done, v_lo_done = sem("u_hi_done"), sem("u_lo_done"), sem("v_hi_done"), sem("v_lo_done")
    up_done, gelu_done, a_done, down_done, added = sem("up_done"), sem("gelu_done"), sem("a_done"), sem("down_done"), sem("added")

    SMALL_LOADS = 7
    STORES = 4 + 2 + 1 + CC
    CHUNKS = DEC_B * PAGES // 4
    UNITS = HEADS * (SEQ // P)

    def unit(u):
        return u // HEADS, u // 2 % PAIRS, u % 2

    ORDER = [0, 1, 2, 3, 4, 5, 8, 6, 9, 7]

    with nc.Block() as block:

        @block.sync
        def _(sp):
            def load_pages(cache, batch, values):
                def load(p, half):
                    chunk = PAGES * batch + p
                    numbers = [sp.value_load(page_row[0:1, bass.ds(PAGES * (BATCH * batch + j) + p, 1)],
                                             min_val=0, max_val=POOL_PAGES - 1) for j in range(BATCH)]
                    if values:
                        wait(sp, pages_used, chunk - 1)
                    else:
                        wait(sp, page_turned, 4 * chunk - 4)
                    for j in range(BATCH):
                        sp.dma_start(page_ring[:, half, j, :], cache[numbers[j], :, :])\
                            .then_inc(page_loaded[half], 16)

                load(0, 0)
                load(1, 1)
                with sp.Fori(1, PAGES // 2) as i:
                    load(2 * i, 0)
                    load(2 * i + 1, 1)

            def load_weights(chunk):
                wait(sp, w_split, chunk - 1)
                if chunk < N_IN:
                    src = io["w_in"][ORDER[chunk]]
                elif chunk < N_IN + N_OUT:
                    src = io["w_out"][chunk - N_IN]
                else:
                    src = io["w_query"][chunk - N_IN - N_OUT]
                sp.dma_start(w_raw[:, chunk % 2, :], src).then_inc(w_loaded[chunk % 2], 16)

            for part in range(4):
                two_blocks = slice(2 * part, 2 * part + 2)
                sp.dma_start(resid[:, two_blocks, :], io["x_t"][:, two_blocks, :]).then_inc(x_loaded[part], 16)
            for chunk in range(N_IN + 1):
                load_weights(chunk)
            sp.wait_ge(pages_known, 16)
            for batch in range(2):
                load_pages(io["cache_k"], batch, values=False)
            sp.wait_ge(page_turned, 4 * CHUNKS)
            for batch in range(2):
                load_pages(io["cache_v"], batch, values=True)
            sp.wait_ge(pt_done, UNITS)
            sp.wait_ge(pv_done, UNITS)
            for chunk in range(N_IN + 1, N_IN + N_OUT):
                load_weights(chunk)
            sp.wait_ge(mix_ready, 1)
            sp.wait_ge(stored, 16 * STORES)
            sp.dma_start(keys[:, :, :], io["keys_t"]).then_inc(keys_loaded, 16)
            for chunk in range(N_IN + N_OUT, W_CHUNKS):
                load_weights(chunk)

            def store_gates(c, parity):
                sp.wait_ge(g_kept, GROUPS * (c + 1))
                sp.dma_start(gates[c], g_out[:, parity, :, :]).then_inc(g_stored[parity], 16)

            def load_u(s, slot):
                sp.dma_start(w_raw[:, slot, :], io["u_t"][s]).then_inc(u_loaded[slot], 16)

            def load_v(s, slot):
                sp.dma_start(v_raw[:, slot, :], io["v_t"][s]).then_inc(v_loaded[slot], 16)

            def store_acts(s, slot):
                sp.wait_ge(gelu_done, 2 * s + 2)
                sp.dma_start(acts[s], act_out[:, slot, :, :].rearrange("p j n -> p (j n)"))\
                    .then_inc(acts_stored[slot], 16)

            def early(s, slot):
                sp.wait_ge(u_lo_done, s + 1)
                load_u(s + 2, slot)
                store_acts(s, slot)

            for slot in range(2):
                sp.wait_ge(w_split, W_CHUNKS - 1 + slot)
                load_u(slot, slot)
            early(0, 0)
            with sp.Fori(0, RANK_STEPS // 2) as i:
                early(2 * i + 1, 1)
                early(2 * i + 2, 0)
            early(RANK_STEPS, 1)
            store_gates(0, 0)
            with sp.Fori(0, NG // 2) as i:
                early(2 * i + RANK_STEPS + 1, 0)
                store_gates(2 * i + 1, 1)
                early(2 * i + RANK_STEPS + 2, 1)
                store_gates(2 * i + 2, 0)
            sp.wait_ge(g_stored[0], 16 * (NG // 2 + 1))
            sp.wait_ge(g_stored[1], 16 * (NG // 2))
            sp.wait_ge(acts_stored[0], 16 * (EARLY // 2))
            sp.wait_ge(acts_stored[1], 16 * (EARLY // 2))
            sp.wait_ge(g_made, NG * GROUPS)

            by_tiles = gates.rearrange("c p (g i) t -> g p c (i t)", i=4)

            def load_step(it, k, stored_acts, more_u):
                s = 4 * it + k
                slot = k % 2
                wait(sp, v_lo_done, s - 1)
                load_v(s, slot)
                if stored_acts:
                    wait(sp, a_done, 2 * s - 2)
                    sp.dma_start(act[:, slot, :, :].rearrange("p j n -> p (j n)"), acts[s]).then_inc(acts_loaded[slot], 16)
                if k % 2 == 0:
                    wait(sp, gated, 2 * s - 4)
                    sp.dma_start(g_in[:, k // 2, :, :], by_tiles[2 * it + k // 2])\
                        .then_inc(g_loaded[k // 2], 16)
                if more_u:
                    sp.wait_ge(u_lo_done, s + 1)
                    load_u(s + 2, slot)

            for k in range(4):
                load_step(0, k, True, False)
            with sp.Fori(1, EARLY // 4) as it:
                for k in range(4):
                    load_step(it, k, True, False)
            with sp.Fori(EARLY // 4, STEPS // 4 - 1) as it:
                for k in range(4):
                    load_step(it, k, False, True)
            for k in range(4):
                load_step(STEPS // 4 - 1, k, False, k < 2)
            sp.wait_ge(added, KD * STEPS)
            sp.dma_start(io["y_t"], resid[:, :, :]).then_inc(stored, 16)
            sp.wait_ge(stored, 16 * (STORES + 1))

        @block.gpsimd
        def _(pool):
            pool.memset(ones[:, :], 1.0)
            pool.memset(ident[:, :], 0.0)
            pool.memset(causal[:, :], 0.0)
            pool.memset(own[:, :, :], 0.0)
            pool.memset(eps[:, :], EPS)
            pool.memset(u_p[:, :, 0:PAD], 0.0)
            pool.memset(q_blk[:, :, :, :], 0.0)
            pool.iota(iota[:, :], [[1, P]], base=0, channel_multiplier=0, allow_small_or_imprecise_dtypes=True)
            pool.iota(stats[:, 32:33].bitcast(I32), [[0, 1]], base=0, channel_multiplier=1)
            pool.iota(s_nat[:, 0:NDEC], [[0, DEC_B], [1, DEC_T]], base=0, channel_multiplier=0,
                      allow_small_or_imprecise_dtypes=True)
            pool.drain()
            pool.affine_select(out=ident[:, :], in_=ident[:, :], compare_op=ALU.not_equal, fill=1.0,
                               base=0, pattern=[[-1, P]], channel_multiplier=1)
            pool.affine_select(out=causal[:, :], in_=causal[:, :], compare_op=ALU.is_ge, fill=NEG,
                               base=0, pattern=[[-1, P]], channel_multiplier=1)
            for b in range(2):
                for sign in (1, -1):
                    pool.affine_select(out=own[:, b, :], in_=own[:, b, :], compare_op=ALU.is_ge, fill=NEG,
                                       base=sign * P * b + (0 if sign == 1 else 31),
                                       pattern=[[-32 * sign, DEC_B], [0, DEC_T]], channel_multiplier=sign)
                    pool.drain()
            pool.memset(stats[:, 48:49], 0.0).then_inc(const_ready, 1)

            for chunk in range(W_CHUNKS):
                pool.wait_ge(w_high, chunk + 1)
                pool.tensor_tensor(w_lo[:, chunk % 2, :], w_raw[:, chunk % 2, :],
                                   w_hi[:, chunk % 2, :].bitcast(F32), ALU.subtract).then_inc(w_split, 1)

            def split_u(s, slot):
                pool.wait_ge(u_hi_done, s + 1)
                pool.tensor_tensor(w_lo[:, slot, :], w_raw[:, slot, :], w_hi[:, slot, :].bitcast(F32),
                                   ALU.subtract).then_inc(u_lo_done, 1)

            def split_v(s, slot):
                pool.wait_ge(v_hi_done, s + 1)
                pool.tensor_tensor(v_lo[:, slot, :], v_raw[:, slot, :], v_hi[:, slot, :].bitcast(F32),
                                   ALU.subtract).then_inc(v_lo_done, 1)

            with pool.Fori(0, EARLY // 2) as i:
                for slot in range(2):
                    split_u(2 * i + slot, slot)
            split_u(EARLY, 0)
            with pool.Fori(0, EARLY // 2) as i:
                for slot in range(2):
                    split_v(2 * i + slot, slot)
            with pool.Fori(EARLY // 2, STEPS // 2 - 1) as i:
                for slot in range(2):
                    split_v(2 * i + slot, slot)
                    split_u(2 * i + slot + 1, 1 - slot)
            split_v(STEPS - 2, 0)
            split_u(STEPS - 1, 1)
            split_v(STEPS - 1, 1)

        @block.scalar
        def _(sc):
            sc.dma_start(g1[:, :], io["norm1_g"]).then_inc(small_loaded, 16)
            sc.dma_start(g2[:, :], io["norm2_g"]).then_inc(small_loaded, 16)
            sc.dma_start(gq[:, :], io["q_norm_g"].partition_broadcast(P)).then_inc(small_loaded, 16)
            sc.dma_start(gk[:, :], io["k_norm_g"].partition_broadcast(P)).then_inc(small_loaded, 16)
            sc.dma_start(taps[:, :, :], io["conv_w"]).then_inc(small_loaded, 16)
            sc.dma_start(conv_b[:, :], io["conv_b"]).then_inc(small_loaded, 16)
            sc.dma_start(conv_g[:, :], io["conv_norm_g"]).then_inc(small_loaded, 16)
            for cc in range(CC):
                sc.dma_start(u_s[:, cc, :, 0:PAD], io["state_t"][:, cc]).then_inc(state_loaded, 16)
            sc.dma_start(page_row[:, :], io["page_table"]).then_inc(pages_known, 16)

            def squares(dst, src, block_count, loaded, summed, done):
                for kd in range(block_count):
                    loaded(kd)
                    wait(sc, summed, kd - 1)
                    sc.activation(dst[:, kd % 2, :], src[:, kd, :], ACT.Square).then_inc(done, 1)

            def root(banks, width, summed, count, done):
                sc.wait_ge(summed, count)
                sc.activation(two(rstd[:, :]), halves(banks), ACT.Sqrt, bias=eps[:, 0:1], scale=1.0 / width)\
                    .then_inc(done, 1)

            def high_w(chunk):
                sc.wait_ge(w_loaded[chunk % 2], 16 * (chunk // 2 + 1))
                if chunk >= 2:
                    sc.wait_ge(projected, after_projection(chunk - 2))
                sc.activation(w_hi[:, chunk % 2, :], w_raw[:, chunk % 2, :], ACT.Copy).then_inc(w_high, 1)

            def high_x(scaled, done):
                for kd in range(KD):
                    sc.wait_ge(scaled, kd + 1)
                    sc.activation(x_hi[:, kd, :], conv[:, kd % 4, :], ACT.Copy).then_inc(done, 1)

            sc.wait_ge(const_ready, 1)
            squares(sq, resid, KD, lambda kd: sc.wait_ge(x_loaded[kd // 2], 16), sum1_done, sq1_done)
            root(pair[0], D, sum1_done, KD, root1_done)
            high_w(0)
            high_x(scaled1, high1)
            high_w(1)

            def keep_turned(chunk):
                dst = q_t if chunk < 2 else k_t
                for nt in range(NT):
                    m = NT * chunk + nt
                    sc.wait_ge(qk_turned, m + 1)
                    first = 2 * (chunk % 2)
                    sc.activation(dst[:, first:first + 2, P * nt:P * nt + ROWS[nt]],
                                  pair[2][:, m % 2, 0:2 * P].rearrange("p (b n) -> p b n", b=2)[:, :, 0:ROWS[nt]],
                                  ACT.Copy, scale=HD ** -0.5 if chunk < 2 else 1.0).then_inc(qk_kept, 1)

            for chunk in range(6):
                for nt in range(NT):
                    m = NT * chunk + nt
                    r = ROWS[nt]
                    src = pair[m % 4 // 2][0:r, m % 2, 0:WCOL]
                    if chunk and nt == 0:
                        high_w(chunk + 1)
                    sc.wait_ge(projected, m + 1)
                    if chunk < 4:
                        sc.activation(sq[0:r, m % 2, 0:WCOL], src, ACT.Square).then_inc(qk_sq, 1)
                        sc.wait_ge(qk_sum, m + 1)
                        sc.activation(stats[0:r, 4 * (m % 4):4 * (m % 4) + 4], stats[0:r, 4 * (m % 4):4 * (m % 4) + 4],
                                      ACT.Sqrt, bias=eps[0:r, 0:1], scale=1.0 / HD).then_inc(qk_root, 1)
                    else:
                        sc.activation(v_nat[0:r, nt, WCOL * (chunk - 4):WCOL * (chunk - 3)], src, ACT.Copy)\
                            .then_inc(v_kept, 1)
                if 1 <= chunk <= 4:
                    keep_turned(chunk - 1)
            sc.wait_ge(qk_ready, 4 * NT)
            sc.wait_ge(v_kept, 2 * NT)
            for dst, src in ((io["k_out"], None), (io["v_out"], v_nat)):
                whole = dst[0:SEQ, :].rearrange("(t p) f -> p t f", p=P)
                for c in range(2):
                    cols = slice(WCOL * c, WCOL * c + WCOL)
                    if src is None:
                        sc.dma_start(whole[:, :, cols], qk_nat[:, c, 0:NT - 1, :]).then_inc(stored, 16)
                        sc.dma_start(dst[SEQ:N, cols], qk_nat[0:NDEC, c, NT - 1, :]).then_inc(stored, 16)
                if src is not None:
                    sc.dma_start(whole, v_nat[:, 0:NT - 1, :]).then_inc(stored, 16)
                    sc.dma_start(dst[SEQ:N, :], v_nat[0:NDEC, NT - 1, :]).then_inc(stored, 16)
            for n, chunk in enumerate((6, 8)):
                for cb in range(2):
                    if cb == 0:
                        high_w(chunk + 1)
                    sc.wait_ge(projected, after_projection(chunk - 1) + cb + 1)
                    if n:
                        sc.wait_ge(u_done, cb + 1)
                    sc.activation(two(sq[:, cb, :]), halves(pair[cb]), ACT.Sigmoid).then_inc(gate_sig, 1)
                high_w(chunk + 2)
            sc.wait_ge(u_done, 4)
            sc.wait_ge(state_loaded, 16 * CC)
            sc.wait_ge(small_loaded, 16 * SMALL_LOADS)
            sc.dma_start(io["conv_p_out"], u_p[:, :, SEQ:SEQ + PAD]).then_inc(stored, 16)
            for cc in range(CC):
                sc.dma_start(io["conv_s_out"][:, cc], u_s[:, cc, :, DEC_T:DEC_T + PAD])\
                    .then_inc(stored, 16)

            def prompt_exp(u):
                i = unit(u)[0]
                sc.wait_ge(pm_done, u + 1)
                wait(sc, pt_done, u - 1)
                sc.activation(p_nat[:, u % 2, 0:P * (i + 1)], bank(P_SCORES)[:, 0:P * (i + 1)], ACT.Exp,
                              bias=stats[:, 16 + u % 2:17 + u % 2],
                              accum_out=stats[:, 20 + u % 2:21 + u % 2]).then_inc(pe_done, 1)

            def prompt_keep(u):
                i = unit(u)[0]
                sc.wait_ge(pt_done, u + 1)
                wait(sc, pv_done, u - 1)
                sc.activation(p_tr[:, u % 2, 0:P * (i + 1)], bank(P_TURN)[:, 0:P * (i + 1)], ACT.Copy)\
                    .then_inc(ptc_done, 1)

            sc.wait_ge(stored, 16 * STORES)

            def keep_page(chunk, j):
                if j == 0:
                    wait(sc, page_scored, chunk - 1)
                sc.wait_ge(page_turned, 4 * chunk + j + 1)
                sc.activation(page_kt[:, chunk % 2, j, :, :], bank(TURN).rearrange("p (a k) -> p a k", a=PAIRS),
                              ACT.Copy).then_inc(page_kept, 1)

            def exp_rows(b):
                sc.wait_ge(s_max, b + 1)
                sc.activation(s_nat[:, :], s_nat[:, :], ACT.Exp, bias=stats[:, 24:25], accum_out=stats[:, 25:26])\
                    .then_inc(s_exp, 1)

            def keep_probabilities(b):
                for g in range(5):
                    sc.wait_ge(s_turned, 5 * b + g + 1)
                    if g < 4:
                        sc.activation(pages_pt[:, 4 * g:4 * g + 4, :],
                                      bank(TURN + 2 * (g % 2)).rearrange("p (a k) -> p a k", a=4), ACT.Copy)\
                            .then_inc(s_turned_kept, 1)
                    else:
                        sc.activation(own_pt[:, :], bank(TURN)[0:NDEC, 0:P], ACT.Copy).then_inc(s_turned_kept, 1)

            def keep_output(b):
                sc.wait_ge(o_done, b + 1)
                wait(sc, o_turned, b)
                sc.activation(o_nat[:, :], bank(P_OUT), ACT.Copy).then_inc(o_kept, 1)

            for u in range(CHUNKS + 1):
                if u < CHUNKS:
                    keep_page(u, 0)
                    keep_page(u, 1)
                    prompt_exp(u)
                if u:
                    prompt_keep(u - 1)
                if u < CHUNKS:
                    keep_page(u, 2)
                    keep_page(u, 3)
                if u == 18:
                    exp_rows(0)
            keep_probabilities(0)
            exp_rows(1)
            squares(sqc, conv, CC, lambda kd: sc.wait_ge(conv_done, 1) if kd == 0 else None, sumc_done, sqc_done)
            keep_output(0)
            root(pair[0], CH, sumc_done, CC, rootc_done)
            keep_probabilities(1)
            sc.wait_ge(z_done, 1)
            for cc in range(CC):
                sc.activation(sig_c[:, cc, :], conv[:, cc, :], ACT.Sigmoid).then_inc(sigc_done, 1)
            keep_output(1)

            high_w(N_IN + 1)

            def block_done(db):
                sc.wait_ge(h_done, db + 1)
                if db % 2:
                    high_w(N_IN + db // 2 + 2)

            squares(sq, resid, KD, block_done, sum2_done, sq2_done)
            root(pair[2], D, sum2_done, KD, root2_done)
            high_x(scaled2, high2)

            for h in range(PH):
                if 1 <= h < PH - 1:
                    high_w(N_IN + N_OUT + h + 1)
                for half in range(2):
                    sc.wait_ge(projected, 2 * h + half + 1 + after_projection(N_IN + N_OUT - 1))
                    if half == 0:
                        wait(sc, scored, 3 * (h - 1))
                    sc.activation(two(qh_t[:, h % 2, half, :]), halves(pair[half]), ACT.Copy).then_inc(qh_kept, 1)

            def high_u(s, slot, loads):
                sc.wait_ge(u_loaded[slot], loads)
                wait(sc, up_done, 2 * s - 2)
                sc.activation(w_hi[:, slot, :], w_raw[:, slot, :], ACT.Copy).then_inc(u_hi_done, 1)

            def gelu_out(s, slot, j, stores):
                sc.wait_ge(up_done, 2 * s + j + 1)
                if j == 0:
                    wait(sc, acts_stored[slot], stores)
                sc.activation(two(act_out[:, slot, j, :]), halves(pair[j]), ACT.Gelu).then_inc(gelu_done, 1)

            sc.wait_ge(projected, after_projection(W_CHUNKS - 1))
            high_u(0, 0, 16)
            ranked_tiles = 0
            for s in range(RANK_STEPS):
                high_u(s + 1, (s + 1) % 2, 16 * ((s + 1) // 2 + 1))
                for j in range(2):
                    gelu_out(s, s % 2, j, 16 * (s // 2))
                while ranked_tiles < NT and s == min(3 * ranked_tiles + 3, RANK_STEPS - 1):
                    r = ROWS[ranked_tiles]
                    sc.wait_ge(rt_top, ranked_tiles + 1)
                    sc.activation(top16[0:r, :, :], top16[0:r, :, :], ACT.Exp).then_inc(rt_exp, 1)
                    ranked_tiles += 1

            def keep_gates(c, parity, half):
                for q in range(GROUPS // 2 * half, GROUPS // 2 * (half + 1)):
                    sc.wait_ge(g_made, GROUPS * c + q + 1)
                    sc.activation(g_out[:, parity, :, TOK * q:TOK * q + TOK].rearrange("p i t -> p t i"),
                                  bank(TURN + q % 2).rearrange("p (t i) -> p t i", t=TOK), ACT.Copy)\
                        .then_inc(g_kept, 1)

            def chunk_and_step(c, parity, stores_of_gates, stores_of_acts, loads):
                s = c + RANK_STEPS
                high_u(s + 1, parity, loads)
                wait(sc, g_stored[parity], stores_of_gates)
                for j in range(2):
                    keep_gates(c, parity, j)
                    gelu_out(s, 1 - parity, j, stores_of_acts)

            chunk_and_step(0, 0, 0, 16 * (RANK_STEPS // 2), 16 * ((RANK_STEPS + 1) // 2 + 1))
            for c, parity in ((1, 1), (2, 0)):
                s = c + RANK_STEPS
                chunk_and_step(c, parity, 16 * (c // 2), 16 * (s // 2), 16 * ((s + 1) // 2 + 1))
            with sc.Fori(1, NG // 2) as i:
                for c, parity in ((1, 1), (2, 0)):
                    s = c + RANK_STEPS
                    chunk_and_step(2 * i + c, parity, 16 * i + 16 * (c // 2), 16 * i + 16 * (s // 2),
                                   16 * i + 16 * ((s + 1) // 2 + 1))

            def high_v(s, slot, loads):
                sc.wait_ge(v_loaded[slot], loads)
                wait(sc, down_done, KD * s - KD)
                sc.activation(v_hi[:, slot, :], v_raw[:, slot, :], ACT.Copy).then_inc(v_hi_done, 1)

            def high_a(s, slot):
                wait(sc, down_done, KD * s - KD)
                for j in range(2):
                    sc.wait_ge(gated, 2 * s + j + 1)
                    sc.activation(a_hi[:, slot, j, :], act[:, slot, j, :], ACT.Copy).then_inc(a_high, 1)

            def mixer(it, k, own_gelu, more_u):
                s = 4 * it + k
                slot = k % 2
                if own_gelu and more_u:
                    high_u(s + 1, 1 - slot, 16 * (2 * it + (k + 1) // 2 + 1))
                high_v(s, slot, 16 * (2 * it + k // 2 + 1))
                if own_gelu:
                    for j in range(2):
                        sc.wait_ge(up_done, 2 * s + j + 1)
                        if j == 0:
                            sc.wait_ge(a_done, 2 * s - 2)
                        sc.activation(two(act[:, slot, j, :]), halves(pair[j]), ACT.Gelu).then_inc(gelu_done, 1)
                high_a(s, slot)

            for k in range(4):
                mixer(0, k, False, False)
            with sc.Fori(1, EARLY // 4) as it:
                for k in range(4):
                    mixer(it, k, False, False)
            with sc.Fori(EARLY // 4, STEPS // 4 - 1) as it:
                for k in range(4):
                    mixer(it, k, True, True)
            for k in range(4):
                mixer(STEPS // 4 - 1, k, True, k < 3)

        @block.vector
        def _(v):
            def reciprocal_rms(rooted):
                v.wait_ge(rooted, 1)
                v.reciprocal(rstd[:, :], rstd[:, :])
                v.drain()

            def parts(kd, src):
                v.tensor_copy(x_hi[:, kd, :], src)
                v.drain()
                return v.tensor_tensor(x_lo[:, kd, :], src, x_hi[:, kd, :].bitcast(F32), ALU.subtract)

            def normed(gain, rooted, scaled, high, ready):
                reciprocal_rms(rooted)

                def low(kd):
                    v.wait_ge(high, kd + 1)
                    v.tensor_tensor(x_lo[:, kd, :], conv[:, kd % 4, :], x_hi[:, kd, :].bitcast(F32), ALU.subtract)\
                        .then_inc(ready, 1)

                for kd in range(KD):
                    v.scalar_tensor_tensor(conv[:, kd % 4, :], resid[:, kd, :], gain[:, kd:kd + 1], rstd[:, :],
                                           ALU.mult, ALU.mult).then_inc(scaled, 1)
                    if kd:
                        low(kd - 1)
                    if kd % 2:
                        v.drain()
                low(KD - 1)

            v.wait_ge(const_ready, 1)
            v.tensor_scalar(stats[:, 33:34].bitcast(I32), stats[:, 32:33].bitcast(I32), DEC_T - 1, None, ALU.bitwise_and)
            v.drain()
            v.tensor_copy(stats[:, 34:35], stats[:, 33:34].bitcast(I32))
            v.drain()
            v.tensor_scalar(s_nat[:, 0:NDEC], s_nat[:, 0:NDEC], stats[:, 34:35], NEG, ALU.is_gt, ALU.mult)
            v.drain()
            for b in range(2):
                v.tensor_tensor(own[:, b, :], own[:, b, :], s_nat[:, 0:NDEC], ALU.add)
            v.wait_ge(small_loaded, 16 * SMALL_LOADS)

            normed(g1, root1_done, scaled1, high1, x_ready)

            for chunk in range(4):
                for nt in range(NT):
                    m = NT * chunk + nt
                    r = ROWS[nt]
                    ss = stats[0:r, 4 * (m % 4):4 * (m % 4) + 4]
                    v.wait_ge(qk_sq, m + 1)
                    v.tensor_reduce(ss, sq[0:r, m % 2, 0:WCOL].rearrange("p (h d) -> p h d", d=HD), AX.X, ALU.add)\
                        .then_inc(qk_sum, 1)
                    v.wait_ge(qk_root, m + 1)
                    v.reciprocal(ss, ss)
                    if chunk >= 2:
                        v.wait_ge(qk_turned, NT * (chunk - 2) + nt + 1)
                    v.drain()
                    dst = qk_nat[0:r, chunk % 2, nt, :]
                    v.tensor_tensor(dst.rearrange("p (h d) -> p h d", d=HD),
                                    pair[m % 4 // 2][0:r, m % 2, 0:WCOL].rearrange("p (h d) -> p h d", d=HD),
                                    ss.unsqueeze(2).to_broadcast([r, 4, HD]), ALU.mult).then_inc(qk_scaled, 1)
                    v.drain()
                    gain = (gq if chunk < 2 else gk)[0:r, WCOL * (chunk % 2):WCOL * (chunk % 2 + 1)]
                    v.tensor_tensor(dst, dst, gain, ALU.mult).then_inc(qk_ready, 1)

            for n in range(2):
                for cb in range(2):
                    cc = 2 * n + cb
                    v.wait_ge(projected, after_projection(6 + 2 * n) + cb + 1)
                    v.wait_ge(gate_sig, 2 * n + cb + 1)
                    src = pair[2 + cb]
                    mid = PAD + HALF
                    v.tensor_tensor(u_p[:, cc, PAD:mid], src[:, 0, 0:HALF], sq[:, cb, 0:HALF], ALU.mult)
                    v.tensor_tensor(u_p[:, cc, mid:PAD + SEQ], src[:, 1, 0:SEQ - HALF], sq[:, cb, HALF:SEQ], ALU.mult)
                    v.tensor_tensor(u_s[:, cc, :, PAD:PAD + DEC_T],
                                    src[:, 1, SEQ - HALF:HALF].rearrange("p (s t) -> p s t", t=DEC_T),
                                    sq[:, cb, SEQ:N].rearrange("p (s t) -> p s t", t=DEC_T), ALU.mult).then_inc(u_done, 1)

            v.wait_ge(qk_kept, 4 * NT)
            for pr in range(PAIRS):
                for hh in range(2):
                    rows = slice(HD * hh, HD * hh + HD)
                    h = 2 * pr + hh
                    last = v.tensor_copy(q_blk[rows, :, pr, DEC_T * h:DEC_T * (h + 1)],
                                         q_t[rows, pr, SEQ:N].rearrange("p (s t) -> p s t", t=DEC_T))
            last.then_inc(q_blk_ready, 1)

            def prompt_max(u):
                i = unit(u)[0]
                v.wait_ge(ps_done, u + 1)
                diagonal = bank(P_SCORES)[:, P * i:P * (i + 1)]
                v.tensor_tensor(diagonal, diagonal, causal[:, :], ALU.add)
                v.drain()
                v.tensor_reduce(stats[:, 16 + u % 2:17 + u % 2], bank(P_SCORES)[:, 0:P * (i + 1)], AX.X, ALU.max,
                                negate=True).then_inc(pm_done, 1)

            def prompt_norm(u):
                i = unit(u)[0]
                v.wait_ge(pe_done, u + 1)
                total = stats[:, 20 + u % 2:21 + u % 2]
                v.reciprocal(total, total)
                v.drain()
                v.tensor_scalar(p_nat[:, u % 2, 0:P * (i + 1)], p_nat[:, u % 2, 0:P * (i + 1)], total, None, ALU.mult)\
                    .then_inc(pn_done, 1)

            def prompt_mix(w):
                i, pr, _ = unit(2 * w)
                v.wait_ge(pv_done, 2 * w + 2)
                src = bank(P_OUT)[:, 0:P]
                cols = slice(P * i, P * (i + 1))
                v.tensor_copy(x_hi[:, pr, cols], src)
                v.drain()
                v.tensor_tensor(x_lo[:, pr, cols], src, x_hi[:, pr, cols].bitcast(F32), ALU.subtract)\
                    .then_inc(po_done, 1)

            new = conv[:, :, SEQ:N].rearrange("p c (s t) -> p c s t", t=DEC_T)

            def tap(k, blocks):
                for cc in blocks:
                    for dst, src in ((conv[:, cc, 0:SEQ], u_p[:, cc, k:k + SEQ]), (new[:, cc], u_s[:, cc, :, k:k + DEC_T])):
                        if k == 0:
                            v.tensor_scalar(dst, src, taps[:, cc, 0:1], conv_b[:, cc:cc + 1], ALU.mult, ALU.add)
                        else:
                            v.scalar_tensor_tensor(dst, src, taps[:, cc, k:k + 1], dst, ALU.mult, ALU.add)

            v.wait_ge(projected, after_projection(N_IN - 1))
            v.wait_ge(state_loaded, 16 * CC)

            def rows_max(b):
                v.wait_ge(page_scored, PAGES * (b + 1))
                v.wait_ge(own_scored, b + 1)
                gate, seen = stats[:, 0:8], stats[:, 8:16]
                largest, which = stats[:, 40:48], stats[:, 48:56]
                for half in range(2):
                    v.tensor_reduce(gate[:, 4 * half:4 * half + 4],
                                    pair[half][:, :, :].rearrange("p b (n k) -> p (b n) k", k=BLOCK), AX.X, ALU.add)
                v.drain()
                v.max(largest, gate)
                v.drain()
                v.max_index(which.bitcast(U32), largest, gate)
                v.drain()
                v.tensor_copy(largest, which.bitcast(U32))
                v.drain()
                v.tensor_scalar(seen, iota[:, 0:NBLK], largest[:, 0:1], None, ALU.is_equal)
                v.drain()
                for n in range(1, TOPB):
                    v.scalar_tensor_tensor(seen, iota[:, 0:NBLK], largest[:, n:n + 1], seen, ALU.is_equal, ALU.add)
                    v.drain()
                v.tensor_scalar(seen, seen, 1.0, -NEG, ALU.subtract, ALU.mult)
                v.drain()
                wait(v, s_turned, 5 * b)
                for half in range(2):
                    v.tensor_tensor(s_nat[:, PAST // 2 * half:PAST // 2 * (half + 1)].rearrange("p (n k) -> p n k", k=BLOCK),
                                    pair[half][:, :, :].rearrange("p b (n k) -> p (b n) k", k=BLOCK),
                                    seen[:, 4 * half:4 * half + 4].unsqueeze(2).to_broadcast([P, 4, BLOCK]), ALU.add)
                v.tensor_tensor(s_nat[:, PAST:KEYS_ALL], bank(P_SCORES)[:, 0:NDEC], own[:, b, :], ALU.add)\
                    .then_inc(s_kept, 1)
                v.drain()
                v.tensor_reduce(stats[:, 24:25], s_nat[:, :], AX.X, ALU.max, negate=True).then_inc(s_max, 1)

            def rows_norm(b):
                v.wait_ge(s_exp, b + 1)
                v.reciprocal(stats[:, 25:26], stats[:, 25:26])
                v.drain()
                v.tensor_scalar(s_nat[:, :], s_nat[:, :], stats[:, 25:26], None, ALU.mult).then_inc(s_normed, 1)

            def mix_output(b):
                v.wait_ge(o_turned, b + 1)
                for part in range(2):
                    for h in range(HEADS):
                        rows = slice(HD * (h % 2), HD * (h % 2) + HD)
                        cols = slice(SEQ + 16 * b, SEQ + 16 * b + 16)
                        src = bank(P_TURN)[rows, P * (h // 2):P * (h // 2 + 1)]\
                            .rearrange("p (j h t) -> p j h t", j=4, t=DEC_T)[:, :, h, :]
                        hi = x_hi[rows, h // 2, cols].rearrange("p (j t) -> p j t", t=DEC_T)
                        lo = x_lo[rows, h // 2, cols].rearrange("p (j t) -> p j t", t=DEC_T)
                        if part == 0:
                            last = v.tensor_copy(hi, src)
                        else:
                            last = v.tensor_tensor(lo, src, hi.bitcast(F32), ALU.subtract)
                    if part == 0:
                        v.drain()
                last.then_inc(o_mixed, 1)

            for u in range(CHUNKS):
                if u == PAGES:
                    rows_max(0)
                prompt_max(u)
                if u < TAPS:
                    tap(u, (0, 1))
                prompt_norm(u)
                if u < TAPS:
                    tap(u, (2, 3))
                if u % 2 == 0 and u:
                    prompt_mix(u // 2 - 1)
                if u == PAGES + 2:
                    rows_norm(0)
            v.drain()
            v.memset(stats[:, 56:57], 0.0).then_inc(conv_done, 1)
            prompt_mix(UNITS // 2 - 1)
            rows_max(1)
            rows_norm(1)
            mix_output(0)
            reciprocal_rms(rootc_done)
            for cc in range(CC):
                last = v.scalar_tensor_tensor(conv[:, cc, :], conv[:, cc, :], conv_g[:, cc:cc + 1], rstd[:, :],
                                              ALU.mult, ALU.mult)
            last.then_inc(z_done, 1)
            for cc in range(CC):
                v.wait_ge(sigc_done, cc + 1)
                v.tensor_tensor(conv[:, cc, :], conv[:, cc, :], sig_c[:, cc, :], ALU.mult)
                v.drain()
                parts(PAIRS + cc, conv[:, cc, :])
            mix_output(1)
            v.memset(stats[:, 56:57], 0.0).then_inc(mix_ready, 1)

            for db in range(KD):
                v.wait_ge(projected, after_projection(N_IN - 1) + db + 1)
                v.tensor_tensor(two(resid[:, db, :]), two(resid[:, db, :]), halves(pair[db % 2]), ALU.add)\
                    .then_inc(h_done, 1)
            normed(g2, root2_done, scaled2, high2, x2_ready)

            with v.Fori(0, PH) as h:
                for nt in range(NT):
                    r = ROWS[nt]
                    held = pair[2 + nt // 4][0:r, nt // 2 % 2, :]
                    m, ix = m16[0:r, nt], i16[0:r, nt]
                    score = [held[:, 256 * (nt % 2) + P * x:256 * (nt % 2) + P * x + P] for x in range(2)]
                    v.wait_ge(scored, 3 * h + nt // 2 + 1)
                    alone(v, v_waited)
                    for x in range(2):
                        v.max(m[:, x, 0:8], score[x])
                    v.drain()
                    for x in range(2):
                        v.match_replace(rest[0:r, x, :], m[:, x, 0:8], score[x], FLOOR)
                        v.max_index(ix[:, x, 0:8], m[:, x, 0:8], score[x])
                    v.drain()
                    for x in range(2):
                        v.max(m[:, x, 8:16], rest[0:r, x, :])
                    v.drain()
                    for x in range(2):
                        v.max_index(ix[:, x, 8:16], m[:, x, 8:16], rest[0:r, x, :])
                    v.drain()
                    v.tensor_copy(best[0:r, nt, bass.ds(h, 1), :, :].rearrange("p a x k -> p (a x k)"),
                                  m.rearrange("p x k -> p (x k)"))
                    v.tensor_copy(best_i[0:r, nt, bass.ds(h, 1), :, :].rearrange("p a x k -> p (a x k)"),
                                  ix.rearrange("p x k -> p (x k)")).then_inc(ranked, 1)
            v.drain()

            def experts(nt, r):
                mine, mine_i = best[0:r, nt, :, :, :], best_i[0:r, nt, :, :, :]
                v.tensor_tensor(cand[0:r], mine[:, :, 0, :].unsqueeze(3).to_broadcast([r, PH, TOPK, TOPK]),
                                mine[:, :, 1, :].unsqueeze(2).to_broadcast([r, PH, TOPK, TOPK]), ALU.add)
                v.drain()
                for h0 in range(0, PH, 2):
                    sums = [cand[0:r, h0 + x].rearrange("p a b -> p (a b)") for x in range(2)]
                    for x in range(2):
                        v.max(top16[0:r, h0 + x, 0:8], sums[x])
                    v.drain()
                    for x in range(2):
                        v.match_replace(crest[0:r, x, :], top16[0:r, h0 + x, 0:8], sums[x], FLOOR)
                        v.max_index(pos16[0:r, h0 + x, 0:8], top16[0:r, h0 + x, 0:8], sums[x])
                    v.drain()
                    for x in range(2):
                        v.max(top16[0:r, h0 + x, 8:16], crest[0:r, x, :])
                    v.drain()
                    for x in range(2):
                        v.max_index(pos16[0:r, h0 + x, 8:16], top16[0:r, h0 + x, 8:16], crest[0:r, x, :])
                    v.drain()
                v.tensor_copy(den[0:r, :].unsqueeze(2), top16[0:r, :, 0:1])
                v.drain()
                v.tensor_tensor(top16[0:r], top16[0:r], den[0:r, :].unsqueeze(2).to_broadcast([r, PH, TOPK]),
                                ALU.subtract).then_inc(rt_top, 1)
                flat = pos16[0:r].rearrange("p h k -> p (h k)")
                v.tensor_scalar(digit[0:r, 0, :], flat, 4, None, ALU.logical_shift_right)
                v.tensor_scalar(digit[0:r, 1, :], flat, TOPK - 1, None, ALU.bitwise_and)
                v.drain()
                wait(v, rt_turned, nt)
                v.tensor_copy(digit_f[0:r], digit[0:r])
                v.drain()
                for x in range(2):
                    hot_h = hot[0:r].rearrange("p (h k) a -> p h k a", h=PH)
                    v.tensor_tensor(hot[0:r], digit_f[0:r, x, :].unsqueeze(2).to_broadcast([r, SLOTS, TOPK]),
                                    iota[0:r, 0:TOPK].unsqueeze(1).to_broadcast([r, SLOTS, TOPK]), ALU.is_equal)
                    v.drain()
                    v.tensor_tensor(hot_h, hot_h, mine_i[:, :, x, :].unsqueeze(2).to_broadcast([r, PH, TOPK, TOPK]),
                                    ALU.mult)
                    v.drain()
                    v.tensor_reduce(found[0:r, x, :], hot[0:r], AX.X, ALU.add)
                    v.drain()
                v.wait_ge(rt_exp, nt + 1)
                v.tensor_reduce(den[0:r, :], top16[0:r], AX.X, ALU.add)
                v.drain()
                v.reciprocal(den[0:r, :], den[0:r, :])
                v.drain()
                v.tensor_tensor(found[0:r, 2, :].rearrange("p (h k) -> p h k", h=PH), top16[0:r],
                                den[0:r, :].unsqueeze(2).to_broadcast([r, PH, TOPK]), ALU.mult).then_inc(rt_found, 1)
                v.drain()

            def keep_slots(nt, r):
                v.wait_ge(rt_turned, nt + 1)
                v.tensor_copy(slots[:, :, P * nt:P * nt + r],
                              bank(P_OUT)[:, 0:3 * P].rearrange("p (a n) -> p a n", a=3)[:, :, 0:r]).then_inc(rt_kept, 1)

            for nt in range(NT):
                experts(nt, ROWS[nt])
                if nt:
                    keep_slots(nt - 1, ROWS[nt - 1])
            keep_slots(NT - 1, ROWS[NT - 1])

            def gate_rows(c, parity):
                v.drain()
                v.tensor_copy(current[:, parity, :, :], slots[:, :, bass.ds(GCHUNK * c, GCHUNK)])
                v.drain()
                for q in range(GROUPS):
                    wait(v, g_made, GROUPS * c + q - 1)
                    if not isinstance(c, int):
                        alone(v, v_waited)
                    for t in range(TOK):
                        at = TOK * q + t
                        i1, i2, gate = (current[:, parity, x, at:at + 1] for x in range(3))
                        v.tensor_scalar(hot1[:, q % 2, t, :], iota[:, :], i1, None, ALU.is_equal)
                        last = v.tensor_scalar(hot2[:, q % 2, t, :], iota[:, :], i2, gate, ALU.is_equal, ALU.mult)
                    last.then_inc(hot_ready, 1)

            gate_rows(0, 0)
            with v.Fori(0, NG // 2) as i:
                gate_rows(2 * i + 1, 1)
                gate_rows(2 * i + 2, 0)

            def add_blocks(s, blocks):
                for db in blocks:
                    v.wait_ge(down_done, KD * s + db + 1)
                    v.tensor_tensor(two(resid[:, db, :]), two(resid[:, db, :]), halves(pair[2 + db % 2]), ALU.add)\
                        .then_inc(added, 1)

            def mixer(it, k, own_gelu):
                s = 4 * it + k
                slot = k % 2
                first = isinstance(s, int) and s == 0
                for j in range(2):
                    if own_gelu:
                        v.wait_ge(gelu_done, 2 * s + j + 1)
                    elif j == 0:
                        v.wait_ge(acts_loaded[slot], 16 * (2 * it + k // 2 + 1))
                    if j == 0 and k % 2 == 0:
                        v.wait_ge(g_loaded[k // 2], 16 * (it + 1))
                    tile = 2 * (k % 2) + j
                    mine = act[:, slot, j, :].rearrange("p (c t) -> p c t", t=GCHUNK)
                    v.tensor_tensor(mine, mine, g_in[:, k // 2, :, GCHUNK * tile:GCHUNK * (tile + 1)], ALU.mult)\
                        .then_inc(gated, 1)
                if not first:
                    add_blocks(s - 1, range(4))
                for j in range(2):
                    v.wait_ge(a_high, 2 * s + j + 1)
                    v.tensor_tensor(a_lo[:, slot, j, :], act[:, slot, j, :], a_hi[:, slot, j, :].bitcast(F32),
                                    ALU.subtract).then_inc(a_done, 1)
                if not first:
                    add_blocks(s - 1, range(4, KD))

            for k in range(4):
                mixer(0, k, False)
            with v.Fori(1, EARLY // 4) as it:
                for k in range(4):
                    mixer(it, k, False)
            with v.Fori(EARLY // 4, STEPS // 4) as it:
                for k in range(4):
                    mixer(it, k, True)
            add_blocks(STEPS - 1, range(KD))

        @block.tensor
        def _(te):
            def product(out, stationary, moving, start, stop):
                (s_hi, s_lo), (m_hi, m_lo) = stationary, moving
                te.matmul(out, s_hi, m_hi, start=start, stop=False)
                te.matmul(out, s_hi, m_lo, start=False, stop=False)
                return te.matmul(out, s_lo, m_hi, start=False, stop=stop)

            def both(a, b, *index):
                return a[index], b[index]

            def sum_block(banks, src, kd, blocks, squared, summed):
                te.wait_ge(squared, kd + 1)
                for half in range(2):
                    last = te.matmul(banks[:, half, 0:HALF], ones[:, :], src[:, kd % 2, HALF * half:HALF * (half + 1)],
                                     start=kd == 0, stop=kd == blocks - 1)
                last.then_inc(summed, 1)

            def sum_squares(banks, src, blocks, squared, summed):
                for kd in range(blocks):
                    sum_block(banks, src, kd, blocks, squared, summed)

            def block_product(banks, slot, cb, ready=None, between=None):
                for kd in range(KD):
                    if ready is not None:
                        te.wait_ge(ready, kd + 1)
                    if between is not None and kd % 2 == 0 and kd:
                        between(kd // 2 - 1)
                    col = WCOL * kd + P * cb
                    stationary = (w_hi[:, slot, col:col + P], w_lo[:, slot, col:col + P])
                    for half in range(2):
                        cols = slice(HALF * half, HALF * (half + 1))
                        last = product(banks[:, half, 0:HALF], stationary, (x_hi[:, kd, cols], x_lo[:, kd, cols]),
                                       kd == 0, kd == KD - 1)
                return last

            te.wait_ge(const_ready, 1)
            sum_squares(pair[0], sq, KD, sq1_done, sum1_done)

            def turn_qk(chunk):
                for nt in range(NT):
                    m = NT * chunk + nt
                    r = ROWS[nt]
                    te.wait_ge(qk_ready, m + 1)
                    wait(te, qk_kept, m - 1)
                    for b in range(2):
                        last = te.transpose(pair[2][:, m % 2, P * b:P * b + r],
                                            qk_nat[0:r, chunk % 2, nt, P * b:P * (b + 1)], ident[0:r, 0:r])
                    last.then_inc(qk_turned, 1)

            for chunk in range(6):
                te.wait_ge(w_split, chunk + 1)
                for nt in range(NT):
                    m = NT * chunk + nt
                    r = ROWS[nt]
                    if 4 <= m < 4 * NT + 4:
                        te.wait_ge(qk_scaled, m - 3)
                    elif m >= 4:
                        te.wait_ge(v_kept, m - 3 - 4 * NT)
                    tokens = slice(P * nt, P * nt + r)
                    for kd in range(KD):
                        if m == 0:
                            te.wait_ge(x_ready, kd + 1)
                        cols = slice(WCOL * kd, WCOL * (kd + 1))
                        last = product(pair[m % 4 // 2][0:r, m % 2, 0:WCOL],
                                       (x_hi[:, kd, tokens], x_lo[:, kd, tokens]),
                                       (w_hi[:, chunk % 2, cols], w_lo[:, chunk % 2, cols]), kd == 0, kd == KD - 1)
                    last.then_inc(projected, 1)
                if 1 <= chunk <= 4:
                    turn_qk(chunk - 1)
            for chunk in range(6, N_IN):
                te.wait_ge(w_split, chunk + 1)
                for cb in range(2):
                    banks = pair[cb if chunk % 2 == 0 else 2 + cb]
                    if chunk == 6:
                        te.wait_ge(v_kept, 2 * NT)
                    elif chunk == 7:
                        te.wait_ge(qk_kept, 4 * NT)
                    elif chunk == 8:
                        te.wait_ge(gate_sig, cb + 1)
                    else:
                        te.wait_ge(u_done, cb + 1)
                    block_product(banks, chunk % 2, cb).then_inc(projected, 1)

            def prompt_scores(u):
                i, pr, hh = unit(u)
                rows = slice(HD * hh, HD * hh + HD)
                wait(te, pe_done, u)
                te.matmul(bank(P_SCORES)[:, 0:P * (i + 1)], q_t[rows, pr, P * i:P * (i + 1)],
                          k_t[rows, pr, 0:P * (i + 1)], start=True, stop=True).then_inc(ps_done, 1)

            def prompt_turn(u):
                i = unit(u)[0]
                te.wait_ge(pn_done, u + 1)
                wait(te, ptc_done, u)
                for kb in range(i + 1):
                    last = te.transpose(bank(P_TURN)[:, P * kb:P * (kb + 1)], p_nat[:, u % 2, P * kb:P * (kb + 1)],
                                        ident[:, :])
                last.then_inc(pt_done, 1)

            def prompt_values(u):
                i, pr, hh = unit(u)
                te.wait_ge(ptc_done, u + 1)
                if hh == 0:
                    wait(te, po_done, u // 2)
                head = HD * (2 * pr + hh)
                for kb in range(i + 1):
                    last = te.matmul(bank(P_OUT)[HD * hh:HD * (hh + 1), 0:P], v_nat[:, kb, head:head + HD],
                                     p_tr[:, u % 2, P * kb:P * (kb + 1)], start=kb == 0, stop=kb == i)
                last.then_inc(pv_done, 1)

            def turn_page(chunk, j):
                if j == 0:
                    te.wait_ge(page_loaded[chunk % 2], 64 * (chunk // 2 + 1))
                wait(te, page_kept, 4 * chunk + j)
                for pr in range(PAIRS):
                    last = te.transpose(bank(TURN)[:, P * pr:P * (pr + 1)],
                                        page_ring[:, chunk % 2, j, P * pr:P * (pr + 1)], ident[:, :])
                last.then_inc(page_turned, 1)

            def score_chunk(chunk, pr):
                b, p = chunk // PAGES, chunk % PAGES
                if pr == 0:
                    te.wait_ge(page_kept, 4 * (chunk + 1))
                for j in range(BATCH):
                    last = te.matmul(bank(p // 4)[32 * j:32 * j + 32, PAGE * (p % 4):PAGE * (p % 4 + 1)],
                                     q_blk[:, BATCH * b + j, pr, :], page_kt[:, chunk % 2, j, pr, :],
                                     start=pr == 0, stop=pr == PAIRS - 1)
                if pr == PAIRS - 1:
                    last.then_inc(page_scored, 1)

            def score_own(b):
                wait(te, pe_done, PAGES * (b + 1))
                for pr in range(PAIRS):
                    for j in range(BATCH):
                        last = te.matmul(bank(P_SCORES)[32 * j:32 * j + 32, 0:NDEC], q_blk[:, BATCH * b + j, pr, :],
                                         k_t[:, pr, SEQ:N], start=pr == 0, stop=pr == PAIRS - 1)
                last.then_inc(own_scored, 1)

            def turn_probabilities(b):
                te.wait_ge(s_normed, b + 1)
                wait(te, o_mixed, b)
                for g in range(5):
                    if g >= 2:
                        te.wait_ge(s_turned_kept, 5 * b + g - 1)
                    for a in range(4 if g < 4 else 1):
                        key = PAGE * (4 * g + a)
                        width = PAGE if g < 4 else NDEC
                        last = te.transpose(bank(TURN + 2 * (g % 2))[0:width, P * a:P * (a + 1)], s_nat[:, key:key + width],
                                            ident[:, :])
                    last.then_inc(s_turned, 1)

            def attend_batch(b):
                te.wait_ge(s_turned_kept, 5 * (b + 1))
                wait(te, o_kept, b)
                for p in range(PAGES):
                    chunk = PAGES * b + p
                    te.wait_ge(page_loaded[chunk % 2], 64 * (CHUNKS // 2 + chunk // 2 + 1))
                    for j in range(BATCH):
                        rows = slice(32 * j, 32 * j + 32)
                        last = te.matmul(bank(P_OUT)[rows, :], pages_pt[:, p, rows], page_ring[:, chunk % 2, j, :],
                                         start=p == 0, stop=False)
                    last.then_inc(pages_used, 1)
                for j in range(BATCH):
                    rows = slice(32 * j, 32 * j + 32)
                    last = te.matmul(bank(P_OUT)[rows, :], own_pt[:, rows], v_nat[0:NDEC, NT - 1, :],
                                     start=False, stop=True)
                last.then_inc(o_done, 1)

            def turn_output(b):
                te.wait_ge(o_kept, b + 1)
                wait(te, o_mixed, b)
                for pr in range(PAIRS):
                    last = te.transpose(bank(P_TURN)[:, P * pr:P * (pr + 1)], o_nat[:, P * pr:P * (pr + 1)], ident[:, :])
                last.then_inc(o_turned, 1)

            te.wait_ge(gate_sig, 4)
            te.wait_ge(u_done, 4)
            te.wait_ge(q_blk_ready, 1)
            for u in range(CHUNKS + 1):
                mine, before = u < CHUNKS, u and u % PAGES
                if mine:
                    turn_page(u, 0)
                if u and not before:
                    for pr in range(PAIRS):
                        score_chunk(u - 1, pr)
                    score_own(u // PAGES - 1)
                    if mine:
                        te.wait_ge(s_kept, u // PAGES)
                if mine:
                    prompt_scores(u)
                if before:
                    score_chunk(u - 1, 0)
                if mine:
                    turn_page(u, 1)
                if u:
                    prompt_turn(u - 1)
                if before:
                    score_chunk(u - 1, 1)
                if mine:
                    turn_page(u, 2)
                if before:
                    score_chunk(u - 1, 2)
                if mine:
                    turn_page(u, 3)
                if u:
                    prompt_values(u - 1)
                if before:
                    score_chunk(u - 1, 3)
            te.wait_ge(ptc_done, UNITS)
            te.wait_ge(po_done, UNITS // 2)
            turn_probabilities(0)
            attend_batch(0)
            te.wait_ge(s_kept, 2)
            sum_squares(pair[0], sqc, CC, sqc_done, sumc_done)
            turn_output(0)
            turn_probabilities(1)
            attend_batch(1)
            turn_output(1)

            te.wait_ge(mix_ready, 1)
            for db in range(KD):
                chunk = N_IN + db // 2
                te.wait_ge(w_split, chunk + 1)
                wait(te, h_done, db - 1)
                block_product(pair[db % 2], chunk % 2, db % 2).then_inc(projected, 1)
                if db >= 2:
                    sum_block(pair[2], sq, db - 2, KD, sq2_done, sum2_done)
            for db in range(KD - 2, KD):
                sum_block(pair[2], sq, db, KD, sq2_done, sum2_done)

            def score_keys(h):
                te.wait_ge(qh_kept, 2 * h + 2)
                for nt in range(NT):
                    r = ROWS[nt]
                    if nt % 2 == 0:
                        wait(te, ranked, NT * (h - 1) + min(nt + 2, NT))
                    held = pair[2 + nt // 4][0:r, nt // 2 % 2, :]
                    for x in range(2):
                        at = 256 * (nt % 2) + P * x
                        last = te.matmul(held[:, at:at + P], qh_t[:, h % 2, x, P * nt:P * nt + r], keys[:, 2 * h + x, :],
                                         start=True, stop=True)
                    if nt % 2 or nt == NT - 1:
                        last.then_inc(scored, 1)

            te.wait_ge(keys_loaded, 16)
            for h in range(PH):
                chunk = N_IN + N_OUT + h
                te.wait_ge(w_split, chunk + 1)
                for half in range(2):
                    wait(te, qh_kept, 2 * h + half - 1)
                    block_product(pair[half], chunk % 2, half, ready=x2_ready if h == 0 and half == 0 else None)\
                        .then_inc(projected, 1)
                if h:
                    score_keys(h - 1)
            def up(s, slot, between=None, after=None):
                te.wait_ge(u_lo_done, s + 1)
                for j in range(2):
                    wait(te, gelu_done, 2 * s + j - 1)
                    block_product(pair[j], slot, j, between=between and (lambda n: between(4 * j + n)))\
                        .then_inc(up_done, 1)
                    if between:
                        between(4 * j + 3)

            def turn_slots(nt):
                r = ROWS[nt]
                te.wait_ge(rt_found, nt + 1)
                wait(te, rt_kept, nt)
                for a in range(3):
                    last = te.transpose(bank(P_OUT)[:, P * a:P * a + r], found[0:r, a, :], ident[0:r, 0:r])
                last.then_inc(rt_turned, 1)

            score_keys(PH - 1)
            turned_tiles = 0
            for s in range(RANK_STEPS):
                up(s, s % 2)
                while turned_tiles < NT and s == min(3 * turned_tiles + 3, RANK_STEPS - 1):
                    turn_slots(turned_tiles)
                    turned_tiles += 1

            def make_gates(c, q):
                g = GROUPS * c + q
                te.wait_ge(hot_ready, g + 1)
                wait(te, g_kept, g - 1)
                for t in range(TOK):
                    last = te.matmul(bank(TURN + q % 2)[:, P * t:P * (t + 1)], hot1[:, q % 2, t, :], hot2[:, q % 2, t, :],
                                     start=True, stop=True)
                last.then_inc(g_made, 1)

            te.wait_ge(ranked, NT * PH)
            up(RANK_STEPS, 1, between=lambda q: make_gates(0, q))
            with te.Fori(0, NG // 2) as i:
                up(2 * i + RANK_STEPS + 1, 0, between=lambda q: make_gates(2 * i + 1, q))
                up(2 * i + RANK_STEPS + 2, 1, between=lambda q: make_gates(2 * i + 2, q))

            def down(s, slot):
                te.wait_ge(v_lo_done, s + 1)
                te.wait_ge(a_done, 2 * s + 2)
                for db in range(KD):
                    wait(te, added, KD * s + db - 1)
                    for j in range(2):
                        col = D * j + P * db
                        stationary = (v_hi[:, slot, col:col + P], v_lo[:, slot, col:col + P])
                        for half in range(2):
                            cols = slice(HALF * half, HALF * (half + 1))
                            last = product(pair[2 + db % 2][:, half, 0:HALF], stationary,
                                           (a_hi[:, slot, j, cols], a_lo[:, slot, j, cols]), j == 0, j == 1)
                    last.then_inc(down_done, 1)

            te.wait_ge(g_kept, NG * GROUPS)
            for s in range(3):
                down(s, s % 2)
            with te.Fori(1, EARLY // 4) as it:
                for k in range(4):
                    down(4 * it + k - 1, (k - 1) % 2)
            with te.Fori(EARLY // 4, STEPS // 4) as it:
                for k in range(4):
                    up(4 * it + k, k % 2)
                    down(4 * it + k - 1, (k - 1) % 2)
            down(STEPS - 1, (STEPS - 1) % 2)


def kernel(**inputs):
    import numpy as np
    import concourse.bacc as bacc
    from concourse.bass_utils import run_bass_kernel_spmd

    a = {k: np.asarray(v) for k, v in inputs.items()}

    def columns(w, n):
        return w.reshape(KD, P, n, WCOL).transpose(2, 1, 0, 3).reshape(n, P, WC)

    def across(g):
        return g.reshape(-1, P).T

    x = np.concatenate([a["x_prompt"].reshape(SEQ, D), a["x_sample"].reshape(NDEC, D)], axis=0)
    sent = {
        "x_t": x.reshape(N, KD, P).transpose(2, 1, 0),
        "w_in": columns(a["w_in"][0], N_IN),
        "w_out": columns(a["w_out"][0], N_OUT),
        "w_query": columns(a["peer_w_query"][0], N_WQ),
        "norm1_g": across(a["norm1_g"][0]),
        "norm2_g": across(a["norm2_g"][0]),
        "q_norm_g": a["q_norm_g"][0].reshape(CH),
        "k_norm_g": a["k_norm_g"][0].reshape(CH),
        "conv_w": a["conv_w"][0].reshape(TAPS, CC, P).transpose(2, 1, 0),
        "conv_b": across(a["conv_b"][0]),
        "conv_norm_g": across(a["conv_norm_g"][0]),
        "state_t": a["state_conv"][0].reshape(DEC_B, PAD, CC, P).transpose(3, 2, 0, 1),
        "page_table": a["page_table"].reshape(1, DEC_B * PAGES),
        "cache_k": a["cache_k"][0].reshape(POOL_PAGES, PAGE, CH),
        "cache_v": a["cache_v"][0].reshape(POOL_PAGES, PAGE, CH),
        "keys_t": np.stack([a["peer_keys1"][0], a["peer_keys2"][0]], axis=1).reshape(2 * PH, P, P).transpose(2, 0, 1),
        "u_t": a["peer_u"][0].reshape(P, STEPS, 2, KD, P).transpose(1, 4, 3, 2, 0).reshape(STEPS, P, WC),
        "v_t": a["peer_v"][0].reshape(P, STEPS, WC).transpose(1, 0, 2),
    }
    sent = {k: np.ascontiguousarray(v) for k, v in sent.items()}
    shapes = {"y_t": (P, KD, N), "k_out": (N, CH), "v_out": (N, CH), "conv_p_out": (P, CC, PAD),
              "conv_s_out": (P, CC, DEC_B, PAD)}
    nc = bacc.Bacc("TRN2", target_bir_lowering=False, num_devices=1)
    io = {k: nc.dram_tensor("in_" + k, v.shape, mybir.dt.from_np(v.dtype), kind="ExternalInput").ap()
          for k, v in sent.items()}
    io.update({k: nc.dram_tensor("out_" + k, s, F32, kind="ExternalOutput").ap() for k, s in shapes.items()})
    build_layer(nc, io)
    run = run_bass_kernel_spmd(nc, [{"in_" + k: v for k, v in sent.items()}], core_ids=[0])
    got = {k: np.asarray(run.results[0]["out_" + k]) for k in shapes}
    y = got["y_t"].transpose(2, 1, 0).reshape(N, D)
    heads = (HEADS, HD)
    return (
        y[:SEQ].reshape(1, SEQ, D),
        y[SEQ:].reshape(DEC_B, DEC_T, D),
        got["k_out"][:SEQ].reshape(1, 1, SEQ, *heads),
        got["v_out"][:SEQ].reshape(1, 1, SEQ, *heads),
        got["conv_p_out"].transpose(2, 1, 0).reshape(1, 1, PAD, CH),
        got["k_out"][SEQ:].reshape(1, DEC_B, DEC_T, *heads),
        got["v_out"][SEQ:].reshape(1, DEC_B, DEC_T, *heads),
        got["conv_s_out"].transpose(2, 3, 1, 0).reshape(1, DEC_B, PAD, CH),
    )
```

```python
import concourse.bass as bass
from concourse import mybir

F32 = mybir.dt.float32
F32R = mybir.dt.float32r
I32 = mybir.dt.int32
U32 = mybir.dt.uint32
ALU = mybir.AluOpType
ACT = mybir.ActivationFunctionType
AX = mybir.AxisListType

P = 128
D = 1024
KD = D // P
SEQ = 512
DEC_B, DEC_T = 8, 4
NDEC = DEC_B * DEC_T
N = SEQ + NDEC
HALF = N // 2
NT = (N + P - 1) // P
ROWS = [min(P, N - P * t) for t in range(NT)]
HEADS, HD = 8, 64
PAIRS = HEADS // 2
CH = 512
CC = CH // P
TAPS = 31
PAD = TAPS - 1
PAGES, PAGE = 16, 128
POOL_PAGES = 160
BLOCK, TOPB = 256, 3
BATCH = 4
PAST = PAGES * PAGE
NBLK = PAST // BLOCK
KEYS_ALL = PAST + NDEC
PH = 8
TOPK = 16
SLOTS = PH * TOPK
EPS = 1e-6
NEG = -1.0e30
FLOOR = -3.0e38

WC = 2048
WCOL = WC // KD
N_IN, N_OUT, N_WQ = 10, 4, 8
W_CHUNKS = N_IN + N_OUT + N_WQ
N_CONV = 4
STEPS = 64
GCHUNK = 32
NG = N // GCHUNK
TOK = 4
GROUPS = GCHUNK // TOK
RANK_STEPS = 19
EXP_AFTER = (3, 6, 9, 13, 16)
TURN_AFTER = (4, 8, 11, 14, 18)
EARLY = RANK_STEPS + NG


def halves(ap):
    return ap[:, :, 0:HALF]


def two(ap):
    return ap.rearrange("p (b n) -> p b n", b=2)


def wait(engine, semaphore, value):
    if not isinstance(value, int) or value > 0:
        engine.wait_ge(semaphore, value)


def alone(engine, ready):
    engine.sem_inc(ready, 1)


def after_projection(chunk):
    return sum(NT if N_CONV <= c < N_IN else 2 for c in range(chunk + 1))


def build_layer(nc, io):
    base = nc.sbuf_base + 31 & ~31
    top = nc.sbuf_usable_end
    place = {"at": base}

    def sb(name, shape, dtype=F32, at=None):
        size = 4
        for s in shape[1:]:
            size *= s
        if at is None:
            at = place["at"]
        place["at"] = at + size + 31 & ~31
        assert place["at"] <= top, (name, place["at"], top)
        return nc.alloc_sbuf_tensor_at(name, shape, dtype, offset=at)

    resid = sb("resid", [P, KD, N])
    x_hi = sb("x_hi", [P, KD, N], F32R)
    x_lo = sb("x_lo", [P, KD, N], F32R)
    w_raw_1 = place["at"] + 4 * WC
    w_raw = sb("w_raw", [P, 2, WC])
    w_hi = sb("w_hi", [P, 2, WC], F32R)
    w_lo = sb("w_lo", [P, 2, WC], F32R)
    ident = sb("ident", [P, P])
    ones = sb("ones", [P, P])
    iota = sb("iota", [P, P])
    rstd = sb("rstd", [P, N])
    g1 = sb("g1", [P, KD])
    g2 = sb("g2", [P, KD])
    eps = sb("eps", [P, 1])
    stats = sb("stats", [P, 96])
    overlay = place["at"]

    v_nat = sb("v_nat", [P, NT, CH])
    q_t = sb("q_t", [P, PAIRS, N])
    k_t = sb("k_t", [P, PAIRS, N])
    u_p = sb("u_p", [P, CC, PAD + SEQ])
    u_s = sb("u_s", [P, CC, DEC_B, PAD + DEC_T])
    conv = sb("conv", [P, CC, N])
    q_blk = sb("q_blk", [P, DEC_B, PAIRS, HEADS * DEC_T])
    taps = sb("taps", [P, CC, TAPS])
    conv_b = sb("conv_b", [P, CC])
    conv_g = sb("conv_g", [P, CC])
    causal = sb("causal", [P, P])
    own = sb("own", [P, 2, NDEC])
    page_row = sb("page_row", [1, DEC_B * PAGES], I32)
    at_gains = place["at"]
    gq = sb("gq", [P, CH])
    gk = sb("gk", [P, CH])
    sq = sb("sq", [P, 2, N])
    s_nat_1 = sb("s_nat_1", [P, KEYS_ALL], at=at_gains)
    place["at"] = at_gains + 4 * (2 * CH + 2 * N) + 31 & ~31
    at_ring = place["at"]
    page_ring = sb("page_ring", [P, 2, BATCH, CH])
    at_keys = place["at"]
    page_kt = sb("page_kt", [P, 2, BATCH, PAIRS, PAGE])
    end_keys = place["at"]
    qk_nat = sb("qk_nat", [P, 2, NT, WCOL], at=at_keys)
    v_ring = sb("v_ring", [P, 4, BATCH, CH], at=at_ring)
    assert place["at"] == end_keys
    s_nat = [sb("s_nat_0", [P, KEYS_ALL]), s_nat_1]
    o_nat = sb("o_nat", [P, CH])
    at_q = overlay + 4 * NT * CH
    p_nat = sb("p_nat", [P, 2, SEQ], at=w_raw_1)
    p_tr = sb("p_tr", [P, 2, SEQ])
    pages_pt = sb("pages_pt", [P, PAGES, P], at=at_q)
    own_pt = sb("own_pt", [NDEC, P])
    sqc = sb("sqc", [P, 2, N], at=at_q + 4 * PAIRS * N)
    sig_c = sb("sig_c", [P, CC, N], at=at_q + 8 * PAIRS * N)

    keys = sb("keys", [P, 2 * PH, P], at=overlay)
    qh_t = sb("qh_t", [P, 2, 2, N])
    best = sb("best", [P, NT, PH, 2, TOPK])
    best_i = sb("best_i", [P, NT, PH, 2, TOPK])
    m16 = sb("m16", [P, NT, 2, TOPK])
    i16 = sb("i16", [P, NT, 2, TOPK], U32)
    rest = sb("rest", [P, 2, P])
    slots = sb("slots", [P, 3, N])
    at_cand = place["at"]
    cand = sb("cand", [P, PH, TOPK, TOPK])
    crest = sb("crest", [P, 2, TOPK * TOPK])
    hot = sb("hot", [P, SLOTS, TOPK])
    top16 = sb("top16", [P, PH, TOPK])
    pos16 = sb("pos16", [P, PH, TOPK], U32)
    digit = sb("digit", [P, 2, SLOTS], U32)
    digit_f = sb("digit_f", [P, 2, SLOTS])
    found = sb("found", [P, 3, SLOTS])
    den = sb("den", [P, PH])
    current = sb("current", [P, 2, 3, GCHUNK], at=at_cand)
    hot1 = sb("hot1", [P, 2, TOK, P])
    hot2 = sb("hot2", [P, 2, TOK, P])
    g_out = sb("g_out", [P, 2, P, GCHUNK])
    act_out = sb("act_out", [P, 2, 2, N])

    v_raw = sb("v_raw", [P, 2, WC], at=overlay)
    v_hi = sb("v_hi", [P, 2, WC], F32R)
    v_lo = sb("v_lo", [P, 2, WC], F32R)
    g_in = sb("g_in", [P, 2, NG, 4 * GCHUNK])
    act = sb("act", [P, 2, 2, N])
    a_hi = sb("a_hi", [P, 2, 2, N], F32R)
    a_lo = sb("a_lo", [P, 2, 2, N], F32R)

    pair = [nc.alloc_psum_tensor(f"pair{i}", [P, 2, 512], F32) for i in range(4)]

    gates = nc.dram_tensor("gates", [NG, P, P, GCHUNK], F32).ap()
    acts = nc.dram_tensor("acts", [EARLY, P, 2 * N], F32).ap()

    def bank(b):
        return pair[b // 2][:, b % 2, :]

    SCORES, PAGE_TURN, P_SCORES, P_TURN, P_OUT = (0, 1), (4, 2), (3, 5), 6, 7
    TURN = 4

    names = {}

    def sem(name):
        if name not in names:
            names[name] = nc.alloc_semaphore(name)
        return names[name]

    state_loaded = sem("state_loaded")
    v_waited = sem("v_waited")
    x_loaded = [sem(f"x_loaded{part}") for part in range(4)]
    small_loaded, pages_known = sem("small_loaded"), sem("pages_known")
    w_loaded = [sem("w_loaded0"), sem("w_loaded1")]
    w_high, w_split, projected = sem("w_high"), sem("w_split"), sem("projected")
    scaled1, high1, scaled2, high2 = sem("scaled1"), sem("high1"), sem("scaled2"), sem("high2")
    const_ready = sem("const_ready")
    sq1_done, sum1_done, root1_done, x_ready = sem("sq1_done"), sem("sum1_done"), sem("root1_done"), sem("x_ready")
    qk_sq, qk_sum, qk_root, qk_scaled, qk_ready = sem("qk_sq"), sem("qk_sum"), sem("qk_root"), sem("qk_scaled"), sem("qk_ready")
    qk_turned, qk_kept, v_kept = sem("qk_turned"), sem("qk_kept"), sem("v_kept")
    gate_sig, u_done = sem("gate_sig"), sem("u_done")
    stored = sem("stored")
    ps_done, pm_done, pe_done, pn_done = sem("ps_done"), sem("pm_done"), sem("pe_done"), sem("pn_done")
    pt_done, ptc_done, pv_done, po_done = sem("pt_done"), sem("ptc_done"), sem("pv_done"), sem("po_done")
    q_blk_ready = sem("q_blk_ready")
    page_loaded = [sem("page_loaded0"), sem("page_loaded1")]
    page_loaded_pool = [sem("page_loaded_pool0"), sem("page_loaded_pool1")]
    values_loaded = [sem(f"values_loaded{slot}") for slot in range(4)]
    values_loaded_pool = [sem(f"values_loaded_pool{slot}") for slot in range(4)]
    page_turned, page_kept, page_scored, own_scored = sem("page_turned"), sem("page_kept"), sem("page_scored"), sem("own_scored")
    own_kept, s_kept, s_max, s_exp, s_normed = sem("own_kept"), sem("s_kept"), sem("s_max"), sem("s_exp"), sem("s_normed")
    s_turned, s_turned_kept, pages_used, o_done = sem("s_turned"), sem("s_turned_kept"), sem("pages_used"), sem("o_done")
    o_kept, o_turned, o_mixed = sem("o_kept"), sem("o_turned"), sem("o_mixed")
    conv_done, sqc_done, sumc_done, rootc_done, z_done, sigc_done = (
        sem("conv_done"), sem("sqc_done"), sem("sumc_done"), sem("rootc_done"), sem("z_done"), sem("sigc_done"))
    mix_ready, h_done = sem("mix_ready"), sem("h_done")
    sq2_done, sum2_done, root2_done, x2_ready = sem("sq2_done"), sem("sum2_done"), sem("root2_done"), sem("x2_ready")
    keys_loaded, qh_kept, scored, ranked = sem("keys_loaded"), sem("qh_kept"), sem("scored"), sem("ranked")
    rt_top, rt_exp, rt_found, rt_turned, rt_kept = sem("rt_top"), sem("rt_exp"), sem("rt_found"), sem("rt_turned"), sem("rt_kept")
    hot_ready = sem("hot_ready")
    acts_stored = [sem("acts_stored0"), sem("acts_stored1")]
    acts_loaded = [sem("acts_loaded0"), sem("acts_loaded1")]
    gated, a_high = sem("gated"), sem("a_high")
    g_made, g_kept = sem("g_made"), sem("g_kept")
    g_stored = [sem("g_stored0"), sem("g_stored1")]
    u_loaded = [sem("u_loaded0"), sem("u_loaded1")]
    v_loaded = [sem("v_loaded0"), sem("v_loaded1")]
    g_loaded = [sem("g_loaded0"), sem("g_loaded1")]
    u_hi_done, u_lo_done, v_hi_done, v_lo_done = sem("u_hi_done"), sem("u_lo_done"), sem("v_hi_done"), sem("v_lo_done")
    up_done, gelu_done, a_done, down_done, added = sem("up_done"), sem("gelu_done"), sem("a_done"), sem("down_done"), sem("added")

    SMALL_LOADS = 7
    STORES = 4 + 2 + 1 + CC
    CHUNKS = DEC_B * PAGES // 4
    FIRST_TAPS, TAPS_BESIDE_VALUES = 14, 9
    UNITS = HEADS * (SEQ // P)

    def unit(u):
        return u // HEADS, u // 2 % PAIRS, u % 2

    ORDER = [8, 6, 9, 7, 0, 1, 2, 3, 4, 5]

    def page_numbers(engine, chunk_batch, p, mine):
        return [engine.value_load(page_row[0:1, bass.ds(PAGES * (BATCH * chunk_batch + j) + p, 1)],
                                  min_val=0, max_val=POOL_PAGES - 1) for j in mine]

    def load_keys(engine, batch, mine, loaded):
        def load(p, half):
            numbers = page_numbers(engine, batch, p, mine)
            wait(engine, page_turned, 4 * (PAGES * batch + p) - 4)
            for number, j in zip(numbers, mine):
                engine.dma_start(page_ring[:, half, j, :], io["cache_k"][number, :, :]).then_inc(loaded[half], 16)

        load(0, 0)
        load(1, 1)
        with engine.Fori(1, PAGES // 2) as i:
            load(2 * i, 0)
            load(2 * i + 1, 1)

    def load_values(engine, batch, mine, loaded):
        def load(p, slot):
            numbers = page_numbers(engine, batch, p, mine)
            chunk = PAGES * batch + p
            if isinstance(p, int) and chunk in (0, 2):
                if chunk == 0:
                    engine.wait_ge(page_turned, 4 * CHUNKS)
                else:
                    engine.wait_ge(page_scored, CHUNKS)
            wait(engine, pages_used, chunk - 3)
            for number, j in zip(numbers, mine):
                engine.dma_start(v_ring[:, slot, j, :], io["cache_v"][number, :, :]).then_inc(loaded[slot], 16)

        for slot in range(4):
            load(slot, slot)
        with engine.Fori(1, PAGES // 4) as i:
            for slot in range(4):
                load(4 * i + slot, slot)

    def load_all_pages(engine, mine, keys_in, values_in):
        engine.wait_ge(pages_known, 16)
        for batch in range(2):
            load_keys(engine, batch, mine, keys_in)
        for batch in range(2):
            load_values(engine, batch, mine, values_in)

    with nc.Block() as block:

        @block.sync
        def _(sp):
            def load_weights(chunk):
                wait(sp, w_split, chunk - 1)
                if chunk < N_IN:
                    src = io["w_in"][ORDER[chunk]]
                elif chunk < N_IN + N_OUT:
                    src = io["w_out"][chunk - N_IN]
                else:
                    src = io["w_query"][chunk - N_IN - N_OUT]
                sp.dma_start(w_raw[:, chunk % 2, :], src).then_inc(w_loaded[chunk % 2], 16)

            for part in range(4):
                two_blocks = slice(2 * part, 2 * part + 2)
                sp.dma_start(resid[:, two_blocks, :], io["x_t"][:, two_blocks, :]).then_inc(x_loaded[part], 16)
            load_weights(0)
            load_weights(1)
            sp.dma_start(g1[:, :], io["norm1_g"]).then_inc(small_loaded, 16)
            sp.dma_start(g2[:, :], io["norm2_g"]).then_inc(small_loaded, 16)
            sp.dma_start(gq[:, :], io["q_norm_g"].partition_broadcast(P)).then_inc(small_loaded, 16)
            sp.dma_start(gk[:, :], io["k_norm_g"].partition_broadcast(P)).then_inc(small_loaded, 16)
            sp.dma_start(taps[:, :, :], io["conv_w"]).then_inc(small_loaded, 16)
            sp.dma_start(conv_b[:, :], io["conv_b"]).then_inc(small_loaded, 16)
            sp.dma_start(conv_g[:, :], io["conv_norm_g"]).then_inc(small_loaded, 16)
            for cc in range(CC):
                sp.dma_start(u_s[:, cc, :, 0:PAD], io["state_t"][:, cc]).then_inc(state_loaded, 16)
            sp.dma_start(page_row[:, :], io["page_table"]).then_inc(pages_known, 16)
            for chunk in range(2, N_IN + 1):
                load_weights(chunk)
            load_all_pages(sp, (0, 1), page_loaded, values_loaded)
            sp.wait_ge(pt_done, UNITS)
            sp.wait_ge(pv_done, UNITS)
            for chunk in range(N_IN + 1, N_IN + N_OUT):
                load_weights(chunk)
            sp.wait_ge(mix_ready, 1)
            sp.wait_ge(stored, 16 * STORES)
            sp.dma_start(keys[:, :, :], io["keys_t"]).then_inc(keys_loaded, 16)
            for chunk in range(N_IN + N_OUT, W_CHUNKS):
                load_weights(chunk)

            def store_gates(c, parity):
                sp.wait_ge(g_kept, GROUPS * (c + 1))
                sp.dma_start(gates[c], g_out[:, parity, :, :]).then_inc(g_stored[parity], 16)

            def load_u(s, slot):
                sp.dma_start(w_raw[:, slot, :], io["u_t"][s]).then_inc(u_loaded[slot], 16)

            def load_v(s, slot):
                sp.dma_start(v_raw[:, slot, :], io["v_t"][s]).then_inc(v_loaded[slot], 16)

            def store_acts(s, slot):
                sp.wait_ge(gelu_done, 2 * s + 2)
                sp.dma_start(acts[s], act_out[:, slot, :, :].rearrange("p j n -> p (j n)"))\
                    .then_inc(acts_stored[slot], 16)

            def early(s, slot):
                sp.wait_ge(u_lo_done, s + 1)
                load_u(s + 2, slot)
                store_acts(s, slot)

            for slot in range(2):
                sp.wait_ge(w_split, W_CHUNKS - 1 + slot)
                load_u(slot, slot)
            early(0, 0)
            with sp.Fori(0, RANK_STEPS // 2) as i:
                early(2 * i + 1, 1)
                early(2 * i + 2, 0)
            early(RANK_STEPS, 1)
            store_gates(0, 0)
            with sp.Fori(0, NG // 2) as i:
                early(2 * i + RANK_STEPS + 1, 0)
                store_gates(2 * i + 1, 1)
                early(2 * i + RANK_STEPS + 2, 1)
                store_gates(2 * i + 2, 0)
            sp.wait_ge(g_stored[0], 16 * (NG // 2 + 1))
            sp.wait_ge(g_stored[1], 16 * (NG // 2))
            sp.wait_ge(acts_stored[0], 16 * (EARLY // 2))
            sp.wait_ge(acts_stored[1], 16 * (EARLY // 2))
            sp.wait_ge(g_made, NG * GROUPS)

            by_tiles = gates.rearrange("c p (g i) t -> g p c (i t)", i=4)

            def load_step(it, k, stored_acts, more_u):
                s = 4 * it + k
                slot = k % 2
                wait(sp, v_lo_done, s - 1)
                load_v(s, slot)
                if stored_acts:
                    wait(sp, a_done, 2 * s - 2)
                    sp.dma_start(act[:, slot, :, :].rearrange("p j n -> p (j n)"), acts[s]).then_inc(acts_loaded[slot], 16)
                if k % 2 == 0:
                    wait(sp, gated, 2 * s - 4)
                    sp.dma_start(g_in[:, k // 2, :, :], by_tiles[2 * it + k // 2])\
                        .then_inc(g_loaded[k // 2], 16)
                if more_u:
                    sp.wait_ge(u_lo_done, s + 2)
                    load_u(s + 3, 1 - slot)

            for k in range(4):
                load_step(0, k, True, False)
            sp.wait_ge(u_lo_done, EARLY + 1)
            load_u(EARLY + 2, 0)
            with sp.Fori(1, EARLY // 4) as it:
                for k in range(4):
                    load_step(it, k, True, False)
            with sp.Fori(EARLY // 4, STEPS // 4 - 1) as it:
                for k in range(4):
                    load_step(it, k, False, True)
            for k in range(4):
                load_step(STEPS // 4 - 1, k, False, k < 1)
            for db in range(KD):
                sp.wait_ge(added, KD * (STEPS - 1) + db + 1)
                sp.dma_start(io["y_t"][:, db, :], resid[:, db, :]).then_inc(stored, 16)
            sp.wait_ge(stored, 16 * (STORES + KD))

        @block.gpsimd
        def _(pool):
            pool.memset(ones[:, :], 1.0)
            pool.memset(ident[:, :], 0.0)
            pool.memset(causal[:, :], 0.0)
            pool.memset(own[:, :, :], 0.0)
            pool.memset(eps[:, :], EPS)
            pool.memset(u_p[:, :, 0:PAD], 0.0)
            pool.memset(q_blk[:, :, :, :], 0.0)
            pool.iota(iota[:, :], [[1, P]], base=0, channel_multiplier=0, allow_small_or_imprecise_dtypes=True)
            pool.iota(stats[:, 32:33].bitcast(I32), [[0, 1]], base=0, channel_multiplier=1)
            pool.iota(s_nat[0][:, 0:NDEC], [[0, DEC_B], [1, DEC_T]], base=0, channel_multiplier=0,
                      allow_small_or_imprecise_dtypes=True)
            pool.drain()
            pool.affine_select(out=ident[:, :], in_=ident[:, :], compare_op=ALU.not_equal, fill=1.0,
                               base=0, pattern=[[-1, P]], channel_multiplier=1)
            pool.affine_select(out=causal[:, :], in_=causal[:, :], compare_op=ALU.is_ge, fill=NEG,
                               base=0, pattern=[[-1, P]], channel_multiplier=1)
            for b in range(2):
                for sign in (1, -1):
                    pool.affine_select(out=own[:, b, :], in_=own[:, b, :], compare_op=ALU.is_ge, fill=NEG,
                                       base=sign * P * b + (0 if sign == 1 else 31),
                                       pattern=[[-32 * sign, DEC_B], [0, DEC_T]], channel_multiplier=sign)
                    pool.drain()
            pool.memset(stats[:, 48:49], 0.0).then_inc(const_ready, 1)

            def low_w(chunk):
                pool.wait_ge(w_high, chunk + 1)
                pool.tensor_tensor(w_lo[:, chunk % 2, :], w_raw[:, chunk % 2, :],
                                   w_hi[:, chunk % 2, :].bitcast(F32), ALU.subtract).then_inc(w_split, 1)

            for chunk in range(N_IN + 1):
                low_w(chunk)
            load_all_pages(pool, (2, 3), page_loaded_pool, values_loaded_pool)
            for chunk in range(N_IN + 1, W_CHUNKS):
                low_w(chunk)

            def split_u(s, slot):
                pool.wait_ge(u_hi_done, s + 1)
                pool.tensor_tensor(w_lo[:, slot, :], w_raw[:, slot, :], w_hi[:, slot, :].bitcast(F32),
                                   ALU.subtract).then_inc(u_lo_done, 1)

            def split_v(s, slot):
                pool.wait_ge(v_hi_done, s + 1)
                pool.tensor_tensor(v_lo[:, slot, :], v_raw[:, slot, :], v_hi[:, slot, :].bitcast(F32),
                                   ALU.subtract).then_inc(v_lo_done, 1)

            with pool.Fori(0, EARLY // 2) as i:
                for slot in range(2):
                    split_u(2 * i + slot, slot)
            split_u(EARLY, 0)
            split_u(EARLY + 1, 1)
            with pool.Fori(0, EARLY // 2) as i:
                for slot in range(2):
                    split_v(2 * i + slot, slot)
            with pool.Fori(EARLY // 2, STEPS // 2 - 1) as i:
                for slot in range(2):
                    split_v(2 * i + slot, slot)
                    split_u(2 * i + slot + 2, slot)
            split_v(STEPS - 2, 0)
            split_v(STEPS - 1, 1)

        @block.scalar
        def _(sc):
            def squares(dst, src, block_count, loaded, summed, done):
                for kd in range(block_count):
                    loaded(kd)
                    wait(sc, summed, kd - 1)
                    sc.activation(dst[:, kd % 2, :], src[:, kd, :], ACT.Square).then_inc(done, 1)

            def root(banks, width, summed, count, done):
                sc.wait_ge(summed, count)
                sc.activation(two(rstd[:, :]), halves(banks), ACT.Sqrt, bias=eps[:, 0:1], scale=1.0 / width)\
                    .then_inc(done, 1)

            def high_w(chunk):
                sc.wait_ge(w_loaded[chunk % 2], 16 * (chunk // 2 + 1))
                if chunk >= 2:
                    sc.wait_ge(projected, after_projection(chunk - 2))
                sc.activation(w_hi[:, chunk % 2, :], w_raw[:, chunk % 2, :], ACT.Copy).then_inc(w_high, 1)

            def high_x(scaled, done):
                for kd in range(KD):
                    sc.wait_ge(scaled, kd + 1)
                    sc.activation(x_hi[:, kd, :], conv[:, kd % 4, :], ACT.Copy).then_inc(done, 1)

            sc.wait_ge(const_ready, 1)
            squares(sq, resid, KD, lambda kd: sc.wait_ge(x_loaded[kd // 2], 16), sum1_done, sq1_done)
            root(pair[0], D, sum1_done, KD, root1_done)
            high_w(0)
            high_x(scaled1, high1)
            high_w(1)

            for n, chunk in enumerate((0, 2)):
                if n:
                    high_w(chunk + 1)
                for cb in range(2):
                    sc.wait_ge(projected, 2 * chunk + cb + 1)
                    if n:
                        sc.wait_ge(u_done, cb + 1)
                    sc.activation(two(sq[:, cb, :]), halves(pair[cb]), ACT.Sigmoid).then_inc(gate_sig, 1)
                high_w(chunk + 2)

            def keep_turned(chunk):
                dst = q_t if chunk < 2 else k_t
                for nt in range(NT):
                    m = NT * chunk + nt
                    sc.wait_ge(qk_turned, m + 1)
                    first = 2 * (chunk % 2)
                    sc.activation(dst[:, first:first + 2, P * nt:P * nt + ROWS[nt]],
                                  pair[2][:, m % 2, 0:2 * P].rearrange("p (b n) -> p b n", b=2)[:, :, 0:ROWS[nt]],
                                  ACT.Copy, scale=HD ** -0.5 if chunk < 2 else 1.0).then_inc(qk_kept, 1)

            for chunk in range(N_IN - N_CONV):
                for nt in range(NT):
                    m = NT * chunk + nt
                    r = ROWS[nt]
                    src = pair[m % 4 // 2][0:r, m % 2, 0:WCOL]
                    if nt == 0:
                        high_w(N_CONV + chunk + 1)
                    sc.wait_ge(projected, 2 * N_CONV + m + 1)
                    if chunk < 4:
                        if m == 0:
                            sc.wait_ge(u_done, 4)
                        sc.activation(sq[0:r, m % 2, 0:WCOL], src, ACT.Square).then_inc(qk_sq, 1)
                        sc.wait_ge(qk_sum, m + 1)
                        sc.activation(stats[0:r, 4 * (m % 4):4 * (m % 4) + 4], stats[0:r, 4 * (m % 4):4 * (m % 4) + 4],
                                      ACT.Sqrt, bias=eps[0:r, 0:1], scale=1.0 / HD).then_inc(qk_root, 1)
                    else:
                        sc.activation(v_nat[0:r, nt, WCOL * (chunk - 4):WCOL * (chunk - 3)], src, ACT.Copy)\
                            .then_inc(v_kept, 1)
                if chunk == 0:
                    sc.wait_ge(state_loaded, 16 * CC)
                    sc.wait_ge(small_loaded, 16 * SMALL_LOADS)
                    sc.dma_start(io["conv_p_out"], u_p[:, :, SEQ:SEQ + PAD]).then_inc(stored, 16)
                    for cc in range(CC):
                        sc.dma_start(io["conv_s_out"][:, cc], u_s[:, cc, :, DEC_T:DEC_T + PAD])\
                            .then_inc(stored, 16)
                if 1 <= chunk <= 4:
                    keep_turned(chunk - 1)
                if chunk == 4:
                    sc.wait_ge(qk_ready, 4 * NT)
                    whole = io["k_out"][0:SEQ, :].rearrange("(t p) f -> p t f", p=P)
                    for c in range(2):
                        cols = slice(WCOL * c, WCOL * c + WCOL)
                        sc.dma_start(whole[:, :, cols], qk_nat[:, c, 0:NT - 1, :]).then_inc(stored, 16)
                        sc.dma_start(io["k_out"][SEQ:N, cols], qk_nat[0:NDEC, c, NT - 1, :]).then_inc(stored, 16)
            sc.wait_ge(v_kept, 2 * NT)
            sc.dma_start(io["v_out"][0:SEQ, :].rearrange("(t p) f -> p t f", p=P), v_nat[:, 0:NT - 1, :])\
                .then_inc(stored, 16)
            sc.dma_start(io["v_out"][SEQ:N, :], v_nat[0:NDEC, NT - 1, :]).then_inc(stored, 16)

            def prompt_exp(u):
                i = unit(u)[0]
                sc.wait_ge(pm_done, u + 1)
                wait(sc, pt_done, u - 1)
                sc.activation(p_nat[:, u % 2, 0:P * (i + 1)], bank(P_SCORES[u % 2])[:, 0:P * (i + 1)], ACT.Exp,
                              bias=stats[:, 16 + u % 2:17 + u % 2],
                              accum_out=stats[:, 20 + u % 2:21 + u % 2]).then_inc(pe_done, 1)

            def prompt_keep(u):
                i = unit(u)[0]
                sc.wait_ge(pt_done, u + 1)
                wait(sc, pv_done, u - 1)
                sc.activation(p_tr[:, u % 2, 0:P * (i + 1)], bank(P_TURN)[:, 0:P * (i + 1)], ACT.Copy)\
                    .then_inc(ptc_done, 1)

            sc.wait_ge(stored, 16 * STORES)

            def keep_page(chunk, j):
                if j == 0:
                    wait(sc, page_scored, chunk - 1)
                sc.wait_ge(page_turned, 4 * chunk + j + 1)
                sc.activation(page_kt[:, chunk % 2, j, :, :], bank(PAGE_TURN[j % 2]).rearrange("p (a k) -> p a k", a=PAIRS),
                              ACT.Copy).then_inc(page_kept, 1)

            def keep_scores(g):
                sc.wait_ge(page_scored, 4 * (g + 1))
                b, q = g // 4, g % 4
                for n in range(2):
                    block = 2 * q + n
                    last = sc.activation(s_nat[b][:, BLOCK * block:BLOCK * (block + 1)],
                                         bank(SCORES[g % 2])[:, BLOCK * n:BLOCK * (n + 1)], ACT.Copy,
                                         accum_out=stats[:, 64 + 8 * b + block:65 + 8 * b + block])
                last.then_inc(s_kept, 1)

            def exp_rows(b):
                sc.wait_ge(s_max, b + 1)
                sc.activation(s_nat[b][:, :], s_nat[b][:, :], ACT.Exp, bias=stats[:, 24:25], accum_out=stats[:, 25:26])\
                    .then_inc(s_exp, 1)

            def keep_probabilities(b):
                for g in range(5):
                    sc.wait_ge(s_turned, 5 * b + g + 1)
                    if g < 4:
                        sc.activation(pages_pt[:, 4 * g:4 * g + 4, :],
                                      bank(TURN + 2 * (g % 2)).rearrange("p (a k) -> p a k", a=4), ACT.Copy)\
                            .then_inc(s_turned_kept, 1)
                    else:
                        sc.activation(own_pt[:, :], bank(TURN)[0:NDEC, 0:P], ACT.Copy).then_inc(s_turned_kept, 1)

            def keep_output(b):
                sc.wait_ge(o_done, b + 1)
                wait(sc, o_turned, b)
                sc.activation(o_nat[:, :], bank(P_OUT), ACT.Copy).then_inc(o_kept, 1)

            for u in range(CHUNKS + 1):
                if u < CHUNKS:
                    keep_page(u, 0)
                    keep_page(u, 1)
                if u % 4 == 1 and u > 1:
                    keep_scores(u // 4 - 1)
                if u < CHUNKS:
                    keep_page(u, 2)
                    keep_page(u, 3)
                    prompt_exp(u)
                if u:
                    prompt_keep(u - 1)
                if u == PAGES + 4:
                    exp_rows(0)
            keep_scores(2 * PAGES // 4 - 1)
            keep_probabilities(0)
            exp_rows(1)
            squares(sqc, conv, CC, lambda kd: sc.wait_ge(conv_done, 1) if kd == 0 else None, sumc_done, sqc_done)
            root(pair[0], CH, sumc_done, CC, rootc_done)
            sc.wait_ge(z_done, 1)
            for cc in range(CC):
                sc.activation(sig_c[:, cc, :], conv[:, cc, :], ACT.Sigmoid).then_inc(sigc_done, 1)
            keep_output(0)
            keep_probabilities(1)
            keep_output(1)

            high_w(N_IN + 1)

            def block_done(db):
                sc.wait_ge(h_done, db + 1)
                if db % 2:
                    high_w(N_IN + db // 2 + 2)

            squares(sq, resid, KD, block_done, sum2_done, sq2_done)
            root(pair[2], D, sum2_done, KD, root2_done)
            high_x(scaled2, high2)

            for h in range(PH):
                if 1 <= h < PH - 1:
                    high_w(N_IN + N_OUT + h + 1)
                for half in range(2):
                    sc.wait_ge(projected, 2 * h + half + 1 + after_projection(N_IN + N_OUT - 1))
                    if half == 0:
                        wait(sc, scored, 3 * (h - 1))
                    sc.activation(two(qh_t[:, h % 2, half, :]), halves(pair[half]), ACT.Copy).then_inc(qh_kept, 1)

            def high_u(s, slot, loads):
                sc.wait_ge(u_loaded[slot], loads)
                wait(sc, up_done, 2 * s - 2)
                sc.activation(w_hi[:, slot, :], w_raw[:, slot, :], ACT.Copy).then_inc(u_hi_done, 1)

            def gelu_out(s, slot, j, stores):
                sc.wait_ge(up_done, 2 * s + j + 1)
                if j == 0:
                    wait(sc, acts_stored[slot], stores)
                sc.activation(two(act_out[:, slot, j, :]), halves(pair[j]), ACT.Gelu).then_inc(gelu_done, 1)

            sc.wait_ge(projected, after_projection(W_CHUNKS - 1))
            high_u(0, 0, 16)
            for s in range(RANK_STEPS):
                high_u(s + 1, (s + 1) % 2, 16 * ((s + 1) // 2 + 1))
                for j in range(2):
                    gelu_out(s, s % 2, j, 16 * (s // 2))
                if s in EXP_AFTER:
                    nt = EXP_AFTER.index(s)
                    r = ROWS[nt]
                    sc.wait_ge(rt_top, nt + 1)
                    sc.activation(top16[0:r, :, :], top16[0:r, :, :], ACT.Exp).then_inc(rt_exp, 1)

            def keep_gates(c, parity, half):
                for q in range(GROUPS // 2 * half, GROUPS // 2 * (half + 1)):
                    sc.wait_ge(g_made, GROUPS * c + q + 1)
                    sc.activation(g_out[:, parity, :, TOK * q:TOK * q + TOK].rearrange("p i t -> p t i"),
                                  bank(TURN + q % 2).rearrange("p (t i) -> p t i", t=TOK), ACT.Copy)\
                        .then_inc(g_kept, 1)

            def chunk_and_step(c, parity, stores_of_gates, stores_of_acts, loads):
                s = c + RANK_STEPS
                high_u(s + 1, parity, loads)
                wait(sc, g_stored[parity], stores_of_gates)
                for j in range(2):
                    keep_gates(c, parity, j)
                    gelu_out(s, 1 - parity, j, stores_of_acts)

            chunk_and_step(0, 0, 0, 16 * (RANK_STEPS // 2), 16 * ((RANK_STEPS + 1) // 2 + 1))
            for c, parity in ((1, 1), (2, 0)):
                s = c + RANK_STEPS
                chunk_and_step(c, parity, 16 * (c // 2), 16 * (s // 2), 16 * ((s + 1) // 2 + 1))
            with sc.Fori(1, NG // 2) as i:
                for c, parity in ((1, 1), (2, 0)):
                    s = c + RANK_STEPS
                    chunk_and_step(2 * i + c, parity, 16 * i + 16 * (c // 2), 16 * i + 16 * (s // 2),
                                   16 * i + 16 * ((s + 1) // 2 + 1))

            def high_v(s, slot, loads):
                sc.wait_ge(v_loaded[slot], loads)
                wait(sc, down_done, KD * s - KD)
                sc.activation(v_hi[:, slot, :], v_raw[:, slot, :], ACT.Copy).then_inc(v_hi_done, 1)

            def high_a(s, slot):
                wait(sc, down_done, KD * s - KD)
                for j in range(2):
                    sc.wait_ge(gated, 2 * s + j + 1)
                    sc.activation(a_hi[:, slot, j, :], act[:, slot, j, :], ACT.Copy).then_inc(a_high, 1)

            def mixer(it, k, own_gelu, more_u):
                s = 4 * it + k
                slot = k % 2
                high_v(s, slot, 16 * (2 * it + k // 2 + 1))
                if own_gelu:
                    for j in range(2):
                        sc.wait_ge(up_done, 2 * s + j + 1)
                        if j == 0:
                            sc.wait_ge(a_done, 2 * s - 2)
                        sc.activation(two(act[:, slot, j, :]), halves(pair[j]), ACT.Gelu).then_inc(gelu_done, 1)
                if own_gelu and more_u:
                    high_u(s + 2, slot, 16 * (2 * it + k // 2 + 2))
                high_a(s, slot)

            high_u(EARLY + 1, 1, 16 * (EARLY // 2 + 1))
            for k in range(4):
                mixer(0, k, False, False)
            with sc.Fori(1, EARLY // 4) as it:
                for k in range(4):
                    mixer(it, k, False, False)
            with sc.Fori(EARLY // 4, STEPS // 4 - 1) as it:
                for k in range(4):
                    mixer(it, k, True, True)
            for k in range(4):
                mixer(STEPS // 4 - 1, k, True, k < 2)

        @block.vector
        def _(v):
            def reciprocal_rms(rooted):
                v.wait_ge(rooted, 1)
                v.reciprocal(rstd[:, :], rstd[:, :])
                v.drain()

            def parts(kd, src):
                v.tensor_copy(x_hi[:, kd, :], src)
                v.drain()
                return v.tensor_tensor(x_lo[:, kd, :], src, x_hi[:, kd, :].bitcast(F32), ALU.subtract)

            def normed(gain, rooted, scaled, high, ready):
                reciprocal_rms(rooted)

                def low(kd):
                    v.wait_ge(high, kd + 1)
                    v.tensor_tensor(x_lo[:, kd, :], conv[:, kd % 4, :], x_hi[:, kd, :].bitcast(F32), ALU.subtract)\
                        .then_inc(ready, 1)

                for kd in range(KD):
                    v.scalar_tensor_tensor(conv[:, kd % 4, :], resid[:, kd, :], gain[:, kd:kd + 1], rstd[:, :],
                                           ALU.mult, ALU.mult).then_inc(scaled, 1)
                    if kd:
                        low(kd - 1)
                    if kd % 2:
                        v.drain()
                low(KD - 1)

            v.wait_ge(const_ready, 1)
            v.tensor_scalar(stats[:, 33:34].bitcast(I32), stats[:, 32:33].bitcast(I32), DEC_T - 1, None, ALU.bitwise_and)
            v.drain()
            v.tensor_copy(stats[:, 34:35], stats[:, 33:34].bitcast(I32))
            v.drain()
            v.tensor_scalar(s_nat[0][:, 0:NDEC], s_nat[0][:, 0:NDEC], stats[:, 34:35], NEG, ALU.is_gt, ALU.mult)
            v.drain()
            for b in range(2):
                v.tensor_tensor(own[:, b, :], own[:, b, :], s_nat[0][:, 0:NDEC], ALU.add)
            v.wait_ge(small_loaded, 16 * SMALL_LOADS)

            normed(g1, root1_done, scaled1, high1, x_ready)

            new = conv[:, :, SEQ:N].rearrange("p c (s t) -> p c s t", t=DEC_T)
            next_tap = [0, 0]

            def taps_of(blocks, count=1):
                for _ in range(count):
                    k = next_tap[blocks]
                    if k == TAPS:
                        return
                    next_tap[blocks] += 1
                    v.drain()
                    for cc in (2 * blocks, 2 * blocks + 1):
                        for dst, src in ((conv[:, cc, 0:SEQ], u_p[:, cc, k:k + SEQ]),
                                         (new[:, cc], u_s[:, cc, :, k:k + DEC_T])):
                            if k == 0:
                                v.tensor_scalar(dst, src, taps[:, cc, 0:1], conv_b[:, cc:cc + 1], ALU.mult, ALU.add)
                            else:
                                v.scalar_tensor_tensor(dst, src, taps[:, cc, k:k + 1], dst, ALU.mult, ALU.add)

            def some_taps():
                taps_of(0 if next_tap[0] <= next_tap[1] else 1)

            v.wait_ge(state_loaded, 16 * CC)
            for n in range(2):
                for cb in range(2):
                    cc = 2 * n + cb
                    v.wait_ge(projected, after_projection(2 * n) + cb + 1)
                    v.wait_ge(gate_sig, 2 * n + cb + 1)
                    src = pair[2 + cb]
                    mid = PAD + HALF
                    v.tensor_tensor(u_p[:, cc, PAD:mid], src[:, 0, 0:HALF], sq[:, cb, 0:HALF], ALU.mult)
                    v.tensor_tensor(u_p[:, cc, mid:PAD + SEQ], src[:, 1, 0:SEQ - HALF], sq[:, cb, HALF:SEQ], ALU.mult)
                    v.tensor_tensor(u_s[:, cc, :, PAD:PAD + DEC_T],
                                    src[:, 1, SEQ - HALF:HALF].rearrange("p (s t) -> p s t", t=DEC_T),
                                    sq[:, cb, SEQ:N].rearrange("p (s t) -> p s t", t=DEC_T), ALU.mult).then_inc(u_done, 1)
                if n == 0:
                    taps_of(0, FIRST_TAPS)

            for chunk in range(4):
                for nt in range(NT):
                    m = NT * chunk + nt
                    r = ROWS[nt]
                    ss = stats[0:r, 4 * (m % 4):4 * (m % 4) + 4]
                    v.wait_ge(qk_sq, m + 1)
                    v.tensor_reduce(ss, sq[0:r, m % 2, 0:WCOL].rearrange("p (h d) -> p h d", d=HD), AX.X, ALU.add)\
                        .then_inc(qk_sum, 1)
                    if m % 4 == 3:
                        some_taps()
                    v.wait_ge(qk_root, m + 1)
                    v.reciprocal(ss, ss)
                    if chunk >= 2:
                        v.wait_ge(qk_turned, NT * (chunk - 2) + nt + 1)
                    v.drain()
                    dst = qk_nat[0:r, chunk % 2, nt, :]
                    v.tensor_tensor(dst.rearrange("p (h d) -> p h d", d=HD),
                                    pair[m % 4 // 2][0:r, m % 2, 0:WCOL].rearrange("p (h d) -> p h d", d=HD),
                                    ss.unsqueeze(2).to_broadcast([r, 4, HD]), ALU.mult).then_inc(qk_scaled, 1)
                    v.drain()
                    gain = (gq if chunk < 2 else gk)[0:r, WCOL * (chunk % 2):WCOL * (chunk % 2 + 1)]
                    v.tensor_tensor(dst, dst, gain, ALU.mult).then_inc(qk_ready, 1)

            for _ in range(TAPS_BESIDE_VALUES):
                some_taps()
            v.wait_ge(qk_kept, 4 * NT)
            for pr in range(PAIRS):
                for hh in range(2):
                    rows = slice(HD * hh, HD * hh + HD)
                    h = 2 * pr + hh
                    last = v.tensor_copy(q_blk[rows, :, pr, DEC_T * h:DEC_T * (h + 1)],
                                         q_t[rows, pr, SEQ:N].rearrange("p (s t) -> p s t", t=DEC_T))
            last.then_inc(q_blk_ready, 1)
            for _ in range(TAPS_BESIDE_VALUES):
                some_taps()

            def prompt_max(u):
                i = unit(u)[0]
                v.wait_ge(ps_done, u + 1)
                diagonal = bank(P_SCORES[u % 2])[:, P * i:P * (i + 1)]
                v.tensor_tensor(diagonal, diagonal, causal[:, :], ALU.add)
                v.drain()
                v.tensor_reduce(stats[:, 16 + u % 2:17 + u % 2], bank(P_SCORES[u % 2])[:, 0:P * (i + 1)], AX.X, ALU.max,
                                negate=True).then_inc(pm_done, 1)

            def prompt_norm(u):
                i = unit(u)[0]
                v.wait_ge(pe_done, u + 1)
                total = stats[:, 20 + u % 2:21 + u % 2]
                v.reciprocal(total, total)
                v.drain()
                v.tensor_scalar(p_nat[:, u % 2, 0:P * (i + 1)], p_nat[:, u % 2, 0:P * (i + 1)], total, None, ALU.mult)\
                    .then_inc(pn_done, 1)

            def prompt_mix(w):
                i, pr, _ = unit(2 * w)
                v.wait_ge(pv_done, 2 * w + 2)
                src = bank(P_OUT)[:, 0:P]
                cols = slice(P * i, P * (i + 1))
                v.tensor_copy(x_hi[:, pr, cols], src)
                v.drain()
                v.tensor_tensor(x_lo[:, pr, cols], src, x_hi[:, pr, cols].bitcast(F32), ALU.subtract)\
                    .then_inc(po_done, 1)

            v.wait_ge(projected, after_projection(N_IN - 1))

            def rows_mask(b):
                v.wait_ge(s_kept, 4 * (b + 1))
                gate, seen = stats[:, 64 + 8 * b:72 + 8 * b], stats[:, 8:16]
                largest, which = stats[:, 40:48], stats[:, 48:56]
                v.max(largest, gate)
                v.drain()
                v.max_index(which.bitcast(U32), largest, gate)
                v.drain()
                v.tensor_copy(largest, which.bitcast(U32))
                v.drain()
                v.tensor_scalar(seen, iota[:, 0:NBLK], largest[:, 0:1], None, ALU.is_equal)
                v.drain()
                for n in range(1, TOPB):
                    v.scalar_tensor_tensor(seen, iota[:, 0:NBLK], largest[:, n:n + 1], seen, ALU.is_equal, ALU.add)
                    v.drain()
                v.tensor_scalar(seen, seen, 1.0, -NEG, ALU.subtract, ALU.mult)
                v.drain()
                blocks = s_nat[b][:, 0:PAST].rearrange("p (n k) -> p n k", k=BLOCK)
                v.tensor_tensor(blocks, blocks, seen.unsqueeze(2).to_broadcast([P, NBLK, BLOCK]), ALU.add)

            def rows_max(b):
                v.drain()
                v.tensor_reduce(stats[:, 24:25], s_nat[b][:, :], AX.X, ALU.max, negate=True).then_inc(s_max, 1)

            def rows_norm(b):
                v.wait_ge(s_exp, b + 1)
                v.reciprocal(stats[:, 25:26], stats[:, 25:26])
                v.drain()
                v.tensor_scalar(s_nat[b][:, :], s_nat[b][:, :], stats[:, 25:26], None, ALU.mult).then_inc(s_normed, 1)

            def mix_output(b):
                v.wait_ge(o_turned, b + 1)
                for part in range(2):
                    for h in range(HEADS):
                        rows = slice(HD * (h % 2), HD * (h % 2) + HD)
                        cols = slice(SEQ + 16 * b, SEQ + 16 * b + 16)
                        src = bank(P_TURN)[rows, P * (h // 2):P * (h // 2 + 1)]\
                            .rearrange("p (j h t) -> p j h t", j=4, t=DEC_T)[:, :, h, :]
                        hi = x_hi[rows, h // 2, cols].rearrange("p (j t) -> p j t", t=DEC_T)
                        lo = x_lo[rows, h // 2, cols].rearrange("p (j t) -> p j t", t=DEC_T)
                        if part == 0:
                            last = v.tensor_copy(hi, src)
                        else:
                            last = v.tensor_tensor(lo, src, hi.bitcast(F32), ALU.subtract)
                    if part == 0:
                        v.drain()
                last.then_inc(o_mixed, 1)

            for b in range(2):
                v.wait_ge(own_scored, 1)
                v.tensor_tensor(s_nat[b][:, PAST:KEYS_ALL], bank(P_OUT)[:, NDEC * b:NDEC * (b + 1)], own[:, b, :],
                                ALU.add).then_inc(own_kept, 1)
            for u in range(CHUNKS + 2):
                if u % 2 == 0 and u >= 4:
                    prompt_mix(u // 2 - 2)
                if 1 <= u <= CHUNKS:
                    prompt_norm(u - 1)
                some_taps()
                if u < CHUNKS:
                    prompt_max(u)
                if u == PAGES + 2:
                    rows_mask(0)
                elif u == PAGES + 3:
                    rows_max(0)
                elif u == PAGES + 5:
                    rows_norm(0)
            assert next_tap == [TAPS, TAPS]
            v.drain()
            v.memset(stats[:, 56:57], 0.0).then_inc(conv_done, 1)
            prompt_mix(UNITS // 2 - 1)
            rows_mask(1)
            rows_max(1)
            rows_norm(1)
            reciprocal_rms(rootc_done)
            for cc in range(CC):
                last = v.scalar_tensor_tensor(conv[:, cc, :], conv[:, cc, :], conv_g[:, cc:cc + 1], rstd[:, :],
                                              ALU.mult, ALU.mult)
            last.then_inc(z_done, 1)
            for cc in range(CC):
                v.wait_ge(sigc_done, cc + 1)
                v.tensor_tensor(conv[:, cc, :], conv[:, cc, :], sig_c[:, cc, :], ALU.mult)
                v.drain()
                parts(PAIRS + cc, conv[:, cc, :])
            mix_output(0)
            mix_output(1)
            v.memset(stats[:, 56:57], 0.0).then_inc(mix_ready, 1)

            for db in range(KD):
                v.wait_ge(projected, after_projection(N_IN - 1) + db + 1)
                v.tensor_tensor(two(resid[:, db, :]), two(resid[:, db, :]), halves(pair[db % 2]), ALU.add)\
                    .then_inc(h_done, 1)
            normed(g2, root2_done, scaled2, high2, x2_ready)

            with v.Fori(0, PH) as h:
                for nt in range(NT):
                    r = ROWS[nt]
                    held = pair[2 + nt // 4][0:r, nt // 2 % 2, :]
                    m, ix = m16[0:r, nt], i16[0:r, nt]
                    score = [held[:, 256 * (nt % 2) + P * x:256 * (nt % 2) + P * x + P] for x in range(2)]
                    v.wait_ge(scored, 3 * h + nt // 2 + 1)
                    alone(v, v_waited)
                    for x in range(2):
                        v.max(m[:, x, 0:8], score[x])
                    v.drain()
                    for x in range(2):
                        v.match_replace(rest[0:r, x, :], m[:, x, 0:8], score[x], FLOOR)
                        v.max_index(ix[:, x, 0:8], m[:, x, 0:8], score[x])
                    v.drain()
                    for x in range(2):
                        v.max(m[:, x, 8:16], rest[0:r, x, :])
                    v.drain()
                    for x in range(2):
                        v.max_index(ix[:, x, 8:16], m[:, x, 8:16], rest[0:r, x, :])
                    v.drain()
                    v.tensor_copy(best[0:r, nt, bass.ds(h, 1), :, :].rearrange("p a x k -> p (a x k)"),
                                  m.rearrange("p x k -> p (x k)"))
                    v.tensor_copy(best_i[0:r, nt, bass.ds(h, 1), :, :].rearrange("p a x k -> p (a x k)"),
                                  ix.rearrange("p x k -> p (x k)")).then_inc(ranked, 1)
            v.drain()

            def experts(nt, r):
                mine, mine_i = best[0:r, nt, :, :, :], best_i[0:r, nt, :, :, :]
                v.tensor_tensor(cand[0:r], mine[:, :, 0, :].unsqueeze(3).to_broadcast([r, PH, TOPK, TOPK]),
                                mine[:, :, 1, :].unsqueeze(2).to_broadcast([r, PH, TOPK, TOPK]), ALU.add)
                v.drain()
                for h0 in range(0, PH, 2):
                    sums = [cand[0:r, h0 + x].rearrange("p a b -> p (a b)") for x in range(2)]
                    for x in range(2):
                        v.max(top16[0:r, h0 + x, 0:8], sums[x])
                    v.drain()
                    for x in range(2):
                        v.match_replace(crest[0:r, x, :], top16[0:r, h0 + x, 0:8], sums[x], FLOOR)
                        v.max_index(pos16[0:r, h0 + x, 0:8], top16[0:r, h0 + x, 0:8], sums[x])
                    v.drain()
                    for x in range(2):
                        v.max(top16[0:r, h0 + x, 8:16], crest[0:r, x, :])
                    v.drain()
                    for x in range(2):
                        v.max_index(pos16[0:r, h0 + x, 8:16], top16[0:r, h0 + x, 8:16], crest[0:r, x, :])
                    v.drain()
                v.tensor_copy(den[0:r, :].unsqueeze(2), top16[0:r, :, 0:1])
                v.drain()
                v.tensor_tensor(top16[0:r], top16[0:r], den[0:r, :].unsqueeze(2).to_broadcast([r, PH, TOPK]),
                                ALU.subtract).then_inc(rt_top, 1)
                flat = pos16[0:r].rearrange("p h k -> p (h k)")
                v.tensor_scalar(digit[0:r, 0, :], flat, 4, None, ALU.logical_shift_right)
                v.tensor_scalar(digit[0:r, 1, :], flat, TOPK - 1, None, ALU.bitwise_and)
                v.drain()
                wait(v, rt_turned, nt)
                v.tensor_copy(digit_f[0:r], digit[0:r])
                v.drain()
                for x in range(2):
                    hot_h = hot[0:r].rearrange("p (h k) a -> p h k a", h=PH)
                    v.tensor_tensor(hot[0:r], digit_f[0:r, x, :].unsqueeze(2).to_broadcast([r, SLOTS, TOPK]),
                                    iota[0:r, 0:TOPK].unsqueeze(1).to_broadcast([r, SLOTS, TOPK]), ALU.is_equal)
                    v.drain()
                    v.tensor_tensor(hot_h, hot_h, mine_i[:, :, x, :].unsqueeze(2).to_broadcast([r, PH, TOPK, TOPK]),
                                    ALU.mult)
                    v.drain()
                    v.tensor_reduce(found[0:r, x, :], hot[0:r], AX.X, ALU.add)
                    v.drain()
                v.wait_ge(rt_exp, nt + 1)
                v.tensor_reduce(den[0:r, :], top16[0:r], AX.X, ALU.add)
                v.drain()
                v.reciprocal(den[0:r, :], den[0:r, :])
                v.drain()
                v.tensor_tensor(found[0:r, 2, :].rearrange("p (h k) -> p h k", h=PH), top16[0:r],
                                den[0:r, :].unsqueeze(2).to_broadcast([r, PH, TOPK]), ALU.mult).then_inc(rt_found, 1)
                v.drain()

            def keep_slots(nt, r):
                v.wait_ge(rt_turned, nt + 1)
                v.tensor_copy(slots[:, :, P * nt:P * nt + r],
                              bank(P_OUT)[:, 0:3 * P].rearrange("p (a n) -> p a n", a=3)[:, :, 0:r]).then_inc(rt_kept, 1)

            for nt in range(NT):
                experts(nt, ROWS[nt])
                if nt:
                    keep_slots(nt - 1, ROWS[nt - 1])
            keep_slots(NT - 1, ROWS[NT - 1])

            def gate_rows(c, parity):
                v.drain()
                v.tensor_copy(current[:, parity, :, :], slots[:, :, bass.ds(GCHUNK * c, GCHUNK)])
                v.drain()
                for q in range(GROUPS):
                    wait(v, g_made, GROUPS * c + q - 1)
                    if not isinstance(c, int):
                        alone(v, v_waited)
                    for t in range(TOK):
                        at = TOK * q + t
                        i1, i2, gate = (current[:, parity, x, at:at + 1] for x in range(3))
                        v.tensor_scalar(hot1[:, q % 2, t, :], iota[:, :], i1, None, ALU.is_equal)
                        last = v.tensor_scalar(hot2[:, q % 2, t, :], iota[:, :], i2, gate, ALU.is_equal, ALU.mult)
                    last.then_inc(hot_ready, 1)

            gate_rows(0, 0)
            with v.Fori(0, NG // 2) as i:
                gate_rows(2 * i + 1, 1)
                gate_rows(2 * i + 2, 0)

            def add_blocks(s, blocks):
                for db in blocks:
                    v.wait_ge(down_done, KD * s + db + 1)
                    v.tensor_tensor(two(resid[:, db, :]), two(resid[:, db, :]), halves(pair[2 + db % 2]), ALU.add)\
                        .then_inc(added, 1)

            def mixer(it, k, own_gelu):
                s = 4 * it + k
                slot = k % 2
                first = isinstance(s, int) and s == 0
                for j in range(2):
                    if own_gelu:
                        v.wait_ge(gelu_done, 2 * s + j + 1)
                    elif j == 0:
                        v.wait_ge(acts_loaded[slot], 16 * (2 * it + k // 2 + 1))
                    if j == 0 and k % 2 == 0:
                        v.wait_ge(g_loaded[k // 2], 16 * (it + 1))
                    tile = 2 * (k % 2) + j
                    mine = act[:, slot, j, :].rearrange("p (c t) -> p c t", t=GCHUNK)
                    v.tensor_tensor(mine, mine, g_in[:, k // 2, :, GCHUNK * tile:GCHUNK * (tile + 1)], ALU.mult)\
                        .then_inc(gated, 1)
                if not first:
                    add_blocks(s - 1, range(4))
                for j in range(2):
                    v.wait_ge(a_high, 2 * s + j + 1)
                    v.tensor_tensor(a_lo[:, slot, j, :], act[:, slot, j, :], a_hi[:, slot, j, :].bitcast(F32),
                                    ALU.subtract).then_inc(a_done, 1)
                if not first:
                    add_blocks(s - 1, range(4, KD))

            for k in range(4):
                mixer(0, k, False)
            with v.Fori(1, EARLY // 4) as it:
                for k in range(4):
                    mixer(it, k, False)
            with v.Fori(EARLY // 4, STEPS // 4) as it:
                for k in range(4):
                    mixer(it, k, True)
            add_blocks(STEPS - 1, range(KD))

        @block.tensor
        def _(te):
            def product(out, stationary, moving, start, stop):
                (s_hi, s_lo), (m_hi, m_lo) = stationary, moving
                te.matmul(out, s_hi, m_hi, start=start, stop=False)
                te.matmul(out, s_hi, m_lo, start=False, stop=False)
                return te.matmul(out, s_lo, m_hi, start=False, stop=stop)

            def both(a, b, *index):
                return a[index], b[index]

            def sum_block(banks, src, kd, blocks, squared, summed):
                te.wait_ge(squared, kd + 1)
                for half in range(2):
                    last = te.matmul(banks[:, half, 0:HALF], ones[:, :], src[:, kd % 2, HALF * half:HALF * (half + 1)],
                                     start=kd == 0, stop=kd == blocks - 1)
                last.then_inc(summed, 1)

            def sum_squares(banks, src, blocks, squared, summed):
                for kd in range(blocks):
                    sum_block(banks, src, kd, blocks, squared, summed)

            def chunk_product(slot, ready):
                for kd in range(KD):
                    te.wait_ge(ready, kd + 1)
                    for cb in range(2):
                        col = WCOL * kd + P * cb
                        stationary = (w_hi[:, slot, col:col + P], w_lo[:, slot, col:col + P])
                        for half in range(2):
                            cols = slice(HALF * half, HALF * (half + 1))
                            last = product(pair[cb][:, half, 0:HALF], stationary, (x_hi[:, kd, cols], x_lo[:, kd, cols]),
                                           kd == 0, kd == KD - 1)
                        if kd == KD - 1:
                            last.then_inc(projected, 1)

            def block_product(banks, slot, cb, between=None):
                for kd in range(KD):
                    if between is not None and kd % 2 == 0 and kd:
                        between(kd // 2 - 1)
                    col = WCOL * kd + P * cb
                    stationary = (w_hi[:, slot, col:col + P], w_lo[:, slot, col:col + P])
                    for half in range(2):
                        cols = slice(HALF * half, HALF * (half + 1))
                        last = product(banks[:, half, 0:HALF], stationary, (x_hi[:, kd, cols], x_lo[:, kd, cols]),
                                       kd == 0, kd == KD - 1)
                return last

            te.wait_ge(const_ready, 1)
            sum_squares(pair[0], sq, KD, sq1_done, sum1_done)

            def turn_qk(chunk):
                for nt in range(NT):
                    m = NT * chunk + nt
                    r = ROWS[nt]
                    te.wait_ge(qk_ready, m + 1)
                    wait(te, qk_kept, m - 1)
                    for b in range(2):
                        last = te.transpose(pair[2][:, m % 2, P * b:P * b + r],
                                            qk_nat[0:r, chunk % 2, nt, P * b:P * (b + 1)], ident[0:r, 0:r])
                    last.then_inc(qk_turned, 1)

            for chunk in range(N_CONV):
                te.wait_ge(w_split, chunk + 1)
                if chunk == 0:
                    te.wait_ge(root1_done, 1)
                    chunk_product(0, x_ready)
                    continue
                for cb in range(2):
                    banks = pair[cb if chunk % 2 == 0 else 2 + cb]
                    if chunk == 2:
                        te.wait_ge(gate_sig, cb + 1)
                    elif chunk == 3:
                        te.wait_ge(u_done, cb + 1)
                    block_product(banks, chunk % 2, cb).then_inc(projected, 1)
            for chunk in range(N_IN - N_CONV):
                te.wait_ge(w_split, N_CONV + chunk + 1)
                for nt in range(NT):
                    m = NT * chunk + nt
                    r = ROWS[nt]
                    if m == 0:
                        te.wait_ge(gate_sig, 4)
                    elif 4 <= m < 4 * NT + 4:
                        te.wait_ge(qk_scaled, m - 3)
                    elif m >= 4:
                        te.wait_ge(v_kept, m - 3 - 4 * NT)
                    tokens = slice(P * nt, P * nt + r)
                    for kd in range(KD):
                        cols = slice(WCOL * kd, WCOL * (kd + 1))
                        last = product(pair[m % 4 // 2][0:r, m % 2, 0:WCOL],
                                       (x_hi[:, kd, tokens], x_lo[:, kd, tokens]),
                                       (w_hi[:, chunk % 2, cols], w_lo[:, chunk % 2, cols]), kd == 0, kd == KD - 1)
                    last.then_inc(projected, 1)
                if 1 <= chunk <= 4:
                    if chunk == 1:
                        te.wait_ge(u_done, 4)
                    turn_qk(chunk - 1)

            def prompt_scores(u):
                i, pr, hh = unit(u)
                rows = slice(HD * hh, HD * hh + HD)
                wait(te, pe_done, u - 1)
                te.matmul(bank(P_SCORES[u % 2])[:, 0:P * (i + 1)], q_t[rows, pr, P * i:P * (i + 1)],
                          k_t[rows, pr, 0:P * (i + 1)], start=True, stop=True).then_inc(ps_done, 1)

            def prompt_turn(u):
                i = unit(u)[0]
                te.wait_ge(pn_done, u + 1)
                wait(te, ptc_done, u)
                for kb in range(i + 1):
                    last = te.transpose(bank(P_TURN)[:, P * kb:P * (kb + 1)], p_nat[:, u % 2, P * kb:P * (kb + 1)],
                                        ident[:, :])
                last.then_inc(pt_done, 1)

            def prompt_values(u):
                i, pr, hh = unit(u)
                te.wait_ge(ptc_done, u + 1)
                if hh == 0:
                    wait(te, po_done, u // 2)
                if u == 0:
                    te.wait_ge(own_kept, 2)
                head = HD * (2 * pr + hh)
                for kb in range(i + 1):
                    last = te.matmul(bank(P_OUT)[HD * hh:HD * (hh + 1), 0:P], v_nat[:, kb, head:head + HD],
                                     p_tr[:, u % 2, P * kb:P * (kb + 1)], start=kb == 0, stop=kb == i)
                last.then_inc(pv_done, 1)

            def turn_page(chunk, j):
                if j == 0:
                    te.wait_ge(page_loaded[chunk % 2], 32 * (chunk // 2 + 1))
                    te.wait_ge(page_loaded_pool[chunk % 2], 32 * (chunk // 2 + 1))
                wait(te, page_kept, 4 * chunk + j - 1)
                for pr in range(PAIRS):
                    last = te.transpose(bank(PAGE_TURN[j % 2])[:, P * pr:P * (pr + 1)],
                                        page_ring[:, chunk % 2, j, P * pr:P * (pr + 1)], ident[:, :])
                last.then_inc(page_turned, 1)

            def score_chunk(chunk):
                b, p = chunk // PAGES, chunk % PAGES
                te.wait_ge(page_kept, 4 * (chunk + 1))
                if p % 4 == 0:
                    wait(te, s_kept, chunk // 4 - 1)
                for pr in range(PAIRS):
                    for j in range(BATCH):
                        last = te.matmul(bank(SCORES[chunk // 4 % 2])[32 * j:32 * j + 32, PAGE * (p % 4):PAGE * (p % 4 + 1)],
                                         q_blk[:, BATCH * b + j, pr, :], page_kt[:, chunk % 2, j, pr, :],
                                         start=pr == 0, stop=pr == PAIRS - 1)
                last.then_inc(page_scored, 1)

            def score_own():
                for b in range(2):
                    for pr in range(PAIRS):
                        for j in range(BATCH):
                            last = te.matmul(bank(P_OUT)[32 * j:32 * j + 32, NDEC * b:NDEC * (b + 1)],
                                             q_blk[:, BATCH * b + j, pr, :], k_t[:, pr, SEQ:N],
                                             start=pr == 0, stop=pr == PAIRS - 1)
                last.then_inc(own_scored, 1)

            def turn_probabilities(b):
                te.wait_ge(s_normed, b + 1)
                for g in range(5):
                    if g >= 2:
                        te.wait_ge(s_turned_kept, 5 * b + g - 1)
                    for a in range(4 if g < 4 else 1):
                        key = PAGE * (4 * g + a)
                        width = PAGE if g < 4 else NDEC
                        last = te.transpose(bank(TURN + 2 * (g % 2))[0:width, P * a:P * (a + 1)], s_nat[b][:, key:key + width],
                                            ident[:, :])
                    last.then_inc(s_turned, 1)

            def attend_batch(b, beside):
                te.wait_ge(s_turned_kept, 5 * (b + 1))
                wait(te, o_kept, b)
                for p in range(PAGES):
                    if p in beside:
                        beside[p]()
                    chunk = PAGES * b + p
                    te.wait_ge(values_loaded[chunk % 4], 32 * (chunk // 4 + 1))
                    te.wait_ge(values_loaded_pool[chunk % 4], 32 * (chunk // 4 + 1))
                    for j in range(BATCH):
                        rows = slice(32 * j, 32 * j + 32)
                        last = te.matmul(bank(P_OUT)[rows, :], pages_pt[:, p, rows], v_ring[:, chunk % 4, j, :],
                                         start=p == 0, stop=False)
                    last.then_inc(pages_used, 1)
                for j in range(BATCH):
                    rows = slice(32 * j, 32 * j + 32)
                    last = te.matmul(bank(P_OUT)[rows, :], own_pt[:, rows], v_nat[0:NDEC, NT - 1, :],
                                     start=False, stop=True)
                last.then_inc(o_done, 1)

            def turn_output(b):
                te.wait_ge(o_kept, b + 1)
                wait(te, o_mixed, b)
                for pr in range(PAIRS):
                    last = te.transpose(bank(P_TURN)[:, P * pr:P * (pr + 1)], o_nat[:, P * pr:P * (pr + 1)], ident[:, :])
                last.then_inc(o_turned, 1)

            te.wait_ge(v_kept, 2 * NT)
            te.wait_ge(qk_kept, 4 * NT)
            te.wait_ge(q_blk_ready, 1)
            score_own()
            for u in range(CHUNKS + 2):
                if u < CHUNKS:
                    turn_page(u, 0)
                    turn_page(u, 1)
                    prompt_scores(u)
                if 1 <= u <= CHUNKS:
                    score_chunk(u - 1)
                    prompt_turn(u - 1)
                if u < CHUNKS:
                    turn_page(u, 2)
                    turn_page(u, 3)
                if u >= 2:
                    prompt_values(u - 2)
            te.wait_ge(ptc_done, UNITS)
            te.wait_ge(po_done, UNITS // 2)
            turn_probabilities(0)
            te.wait_ge(s_kept, 2 * PAGES // 4)
            attend_batch(0, {4 + 2 * cc: lambda cc=cc: sum_block(pair[0], sqc, cc, CC, sqc_done, sumc_done)
                             for cc in range(CC)})
            turn_probabilities(1)
            attend_batch(1, {2: lambda: turn_output(0)})
            turn_output(1)

            te.wait_ge(mix_ready, 1)
            for db in range(KD):
                chunk = N_IN + db // 2
                te.wait_ge(w_split, chunk + 1)
                wait(te, h_done, db - 1)
                block_product(pair[db % 2], chunk % 2, db % 2).then_inc(projected, 1)
                if db >= 2:
                    sum_block(pair[2], sq, db - 2, KD, sq2_done, sum2_done)
            for db in range(KD - 2, KD):
                sum_block(pair[2], sq, db, KD, sq2_done, sum2_done)

            def score_keys(h):
                te.wait_ge(qh_kept, 2 * h + 2)
                for nt in range(NT):
                    r = ROWS[nt]
                    if nt % 2 == 0:
                        wait(te, ranked, NT * (h - 1) + min(nt + 2, NT))
                    held = pair[2 + nt // 4][0:r, nt // 2 % 2, :]
                    for x in range(2):
                        at = 256 * (nt % 2) + P * x
                        last = te.matmul(held[:, at:at + P], qh_t[:, h % 2, x, P * nt:P * nt + r], keys[:, 2 * h + x, :],
                                         start=True, stop=True)
                    if nt % 2 or nt == NT - 1:
                        last.then_inc(scored, 1)

            te.wait_ge(keys_loaded, 16)
            for h in range(PH):
                chunk = N_IN + N_OUT + h
                te.wait_ge(w_split, chunk + 1)
                if h == 0:
                    te.wait_ge(h_done, KD)
                    chunk_product(chunk % 2, x2_ready)
                    continue
                for half in range(2):
                    te.wait_ge(qh_kept, 2 * h + half - 1)
                    block_product(pair[half], chunk % 2, half).then_inc(projected, 1)
                score_keys(h - 1)
            def up(s, slot, between=None, after=None):
                te.wait_ge(u_lo_done, s + 1)
                for j in range(2):
                    wait(te, gelu_done, 2 * s + j - 1)
                    block_product(pair[j], slot, j, between=between and (lambda n: between(4 * j + n)))\
                        .then_inc(up_done, 1)
                    if between:
                        between(4 * j + 3)

            def turn_slots(nt):
                r = ROWS[nt]
                te.wait_ge(rt_found, nt + 1)
                wait(te, rt_kept, nt)
                for a in range(3):
                    last = te.transpose(bank(P_OUT)[:, P * a:P * a + r], found[0:r, a, :], ident[0:r, 0:r])
                last.then_inc(rt_turned, 1)

            for s in range(RANK_STEPS):
                up(s, s % 2)
                if s == 0:
                    score_keys(PH - 1)
                if s in TURN_AFTER:
                    turn_slots(TURN_AFTER.index(s))

            def make_gates(c, q):
                g = GROUPS * c + q
                te.wait_ge(hot_ready, g + 1)
                wait(te, g_kept, g - 1)
                for t in range(TOK):
                    last = te.matmul(bank(TURN + q % 2)[:, P * t:P * (t + 1)], hot1[:, q % 2, t, :], hot2[:, q % 2, t, :],
                                     start=True, stop=True)
                last.then_inc(g_made, 1)

            te.wait_ge(ranked, NT * PH)
            up(RANK_STEPS, 1, between=lambda q: make_gates(0, q))
            with te.Fori(0, NG // 2) as i:
                up(2 * i + RANK_STEPS + 1, 0, between=lambda q: make_gates(2 * i + 1, q))
                up(2 * i + RANK_STEPS + 2, 1, between=lambda q: make_gates(2 * i + 2, q))

            def down(s, slot):
                te.wait_ge(v_lo_done, s + 1)
                te.wait_ge(a_done, 2 * s + 2)
                for db in range(KD):
                    wait(te, added, KD * s + db - 1)
                    for j in range(2):
                        col = D * j + P * db
                        stationary = (v_hi[:, slot, col:col + P], v_lo[:, slot, col:col + P])
                        for half in range(2):
                            cols = slice(HALF * half, HALF * (half + 1))
                            last = product(pair[2 + db % 2][:, half, 0:HALF], stationary,
                                           (a_hi[:, slot, j, cols], a_lo[:, slot, j, cols]), j == 0, j == 1)
                    last.then_inc(down_done, 1)

            up(EARLY, 0)
            te.wait_ge(g_kept, NG * GROUPS)
            for s in range(3):
                down(s, s % 2)
            with te.Fori(1, EARLY // 4) as it:
                for k in range(4):
                    down(4 * it + k - 1, (k - 1) % 2)
            with te.Fori(EARLY // 4, STEPS // 4 - 1) as it:
                for k in range(4):
                    down(4 * it + k - 1, (k - 1) % 2)
                    up(4 * it + k + 1, (k + 1) % 2)
            for s in range(STEPS - 4, STEPS):
                down(s - 1, (s - 1) % 2)
                if s + 1 < STEPS:
                    up(s + 1, (s + 1) % 2)
            down(STEPS - 1, (STEPS - 1) % 2)


def kernel(**inputs):
    import numpy as np
    import concourse.bacc as bacc
    from concourse.bass_utils import run_bass_kernel_spmd

    a = {k: np.asarray(v) for k, v in inputs.items()}

    def columns(w, n):
        return w.reshape(KD, P, n, WCOL).transpose(2, 1, 0, 3).reshape(n, P, WC)

    def across(g):
        return g.reshape(-1, P).T

    x = np.concatenate([a["x_prompt"].reshape(SEQ, D), a["x_sample"].reshape(NDEC, D)], axis=0)
    sent = {
        "x_t": x.reshape(N, KD, P).transpose(2, 1, 0),
        "w_in": columns(a["w_in"][0], N_IN),
        "w_out": columns(a["w_out"][0], N_OUT),
        "w_query": columns(a["peer_w_query"][0], N_WQ),
        "norm1_g": across(a["norm1_g"][0]),
        "norm2_g": across(a["norm2_g"][0]),
        "q_norm_g": a["q_norm_g"][0].reshape(CH),
        "k_norm_g": a["k_norm_g"][0].reshape(CH),
        "conv_w": a["conv_w"][0].reshape(TAPS, CC, P).transpose(2, 1, 0),
        "conv_b": across(a["conv_b"][0]),
        "conv_norm_g": across(a["conv_norm_g"][0]),
        "state_t": a["state_conv"][0].reshape(DEC_B, PAD, CC, P).transpose(3, 2, 0, 1),
        "page_table": a["page_table"].reshape(1, DEC_B * PAGES),
        "cache_k": a["cache_k"][0].reshape(POOL_PAGES, PAGE, CH),
        "cache_v": a["cache_v"][0].reshape(POOL_PAGES, PAGE, CH),
        "keys_t": np.stack([a["peer_keys1"][0], a["peer_keys2"][0]], axis=1).reshape(2 * PH, P, P).transpose(2, 0, 1),
        "u_t": a["peer_u"][0].reshape(P, STEPS, 2, KD, P).transpose(1, 4, 3, 2, 0).reshape(STEPS, P, WC),
        "v_t": a["peer_v"][0].reshape(P, STEPS, WC).transpose(1, 0, 2),
    }
    sent = {k: np.ascontiguousarray(v) for k, v in sent.items()}
    shapes = {"y_t": (P, KD, N), "k_out": (N, CH), "v_out": (N, CH), "conv_p_out": (P, CC, PAD),
              "conv_s_out": (P, CC, DEC_B, PAD)}
    nc = bacc.Bacc("TRN2", target_bir_lowering=False, num_devices=1)
    io = {k: nc.dram_tensor("in_" + k, v.shape, mybir.dt.from_np(v.dtype), kind="ExternalInput").ap()
          for k, v in sent.items()}
    io.update({k: nc.dram_tensor("out_" + k, s, F32, kind="ExternalOutput").ap() for k, s in shapes.items()})
    build_layer(nc, io)
    run = run_bass_kernel_spmd(nc, [{"in_" + k: v for k, v in sent.items()}], core_ids=[0])
    got = {k: np.asarray(run.results[0]["out_" + k]) for k in shapes}
    y = got["y_t"].transpose(2, 1, 0).reshape(N, D)
    heads = (HEADS, HD)
    return (
        y[:SEQ].reshape(1, SEQ, D),
        y[SEQ:].reshape(DEC_B, DEC_T, D),
        got["k_out"][:SEQ].reshape(1, 1, SEQ, *heads),
        got["v_out"][:SEQ].reshape(1, 1, SEQ, *heads),
        got["conv_p_out"].transpose(2, 1, 0).reshape(1, 1, PAD, CH),
        got["k_out"][SEQ:].reshape(1, DEC_B, DEC_T, *heads),
        got["v_out"][SEQ:].reshape(1, DEC_B, DEC_T, *heads),
        got["conv_s_out"].transpose(2, 3, 1, 0).reshape(1, DEC_B, PAD, CH),
    )
```
